# Optimizing a Trainium2 kernel written in Bass

```python
import jax, jax.numpy as jnp
from jax import lax
import numpy as np

D_MODEL = 1024
BATCH = 1
SEQ = 1024
DEPTH = 1

CHUNK = 64
LEFT_CHUNKS = 8
BAND = LEFT_CHUNKS + 1
N_MEM = 256

D_MIX = D_MODEL
ATT_HEADS = 8
ATT_HEAD_DIM = 64
D_ATT = ATT_HEADS * ATT_HEAD_DIM
CONV_GROUPS = 8
CONV_GROUP_DIM = 64
D_CONV = CONV_GROUPS * CONV_GROUP_DIM
CONV_W = 3
MAX_REL = 256
N_REL = 2 * MAX_REL + 1
D_IN_PROJ = 3 * D_ATT + 3 * D_CONV

X_HEADS = 4
X_HEAD_DIM = 128
D_X = X_HEADS * X_HEAD_DIM

N_EXPERTS = 32
TOP_K = 4
D_FF = D_MODEL
SWIGLU_LIMIT = 7.0
SWIGLU_ALPHA = 1.702
EXPERT_BLOCK = 128

EPS = 1e-6
NEG_INF = -1e30

kernel_name = "hybrid_chunk_attn_shortconv_memxattn_moe"

def _rmsnorm(x, g):
    xf = x.astype(jnp.float32)
    y = xf * lax.rsqrt(jnp.mean(xf * xf, axis=-1, keepdims=True) + EPS)
    return (y * g.astype(jnp.float32)).astype(x.dtype)

def _rel_bias_band(rel_bias):
    qi = np.arange(CHUNK)[:, None] + LEFT_CHUNKS * CHUNK
    kk = np.arange(BAND * CHUNK)[None, :]
    idx = np.clip(qi - kk, -MAX_REL, MAX_REL) + MAX_REL
    return rel_bias[:, idx]

def _chunk_attention(q, k, v, q_g, k_g, rel_bias):
    B, S = q.shape[0], q.shape[1]
    nc = S // CHUNK
    q = _rmsnorm(q, q_g).reshape(B, nc, CHUNK, ATT_HEADS, ATT_HEAD_DIM)
    k = _rmsnorm(k, k_g).reshape(B, nc, CHUNK, ATT_HEADS, ATT_HEAD_DIM)
    v = v.reshape(B, nc, CHUNK, ATT_HEADS, ATT_HEAD_DIM)
    pad = ((0, 0), (LEFT_CHUNKS, 0), (0, 0), (0, 0), (0, 0))
    kp, vp = jnp.pad(k, pad), jnp.pad(v, pad)
    k_band = jnp.concatenate([kp[:, i:i + nc] for i in range(BAND)], axis=2)
    v_band = jnp.concatenate([vp[:, i:i + nc] for i in range(BAND)], axis=2)
    scale = ATT_HEAD_DIM ** -0.5
    s = jnp.einsum('bcqhd,bckhd->bhcqk', q, k_band,
                   preferred_element_type=jnp.float32) * scale
    s = s + _rel_bias_band(rel_bias).astype(jnp.float32)[None, :, None]
    key_chunk = (jnp.arange(nc)[:, None] - LEFT_CHUNKS
                 + (jnp.arange(BAND * CHUNK)[None, :] // CHUNK))
    s = jnp.where((key_chunk >= 0)[None, None, :, None, :], s, NEG_INF)
    p = jax.nn.softmax(s, axis=-1).astype(v.dtype)
    o = jnp.einsum('bhcqk,bckhd->bcqhd', p, v_band)
    return o.reshape(B, S, D_ATT)

def _short_conv(bg, cg, xv, conv_w):
    S = xv.shape[1]
    u = jnp.pad(cg * xv, ((0, 0), (CONV_W - 1, 0), (0, 0)))
    conv = conv_w[0] * u[:, 0:S] + conv_w[1] * u[:, 1:S + 1] + conv_w[2] * u[:, 2:S + 2]
    return bg * conv

def _memory_xattn(h, mem, norm_mem_g, w_xq, w_xkv, xq_g, xk_g, w_xo):
    B, S, _ = h.shape
    hm = _rmsnorm(mem, norm_mem_g)
    q = (h @ w_xq).reshape(B, S, X_HEADS, X_HEAD_DIM)
    k, v = jnp.split(hm @ w_xkv, 2, axis=-1)
    k = k.reshape(B, N_MEM, X_HEADS, X_HEAD_DIM)
    v = v.reshape(B, N_MEM, X_HEADS, X_HEAD_DIM)
    q, k = _rmsnorm(q, xq_g), _rmsnorm(k, xk_g)
    s = jnp.einsum('bshd,bmhd->bhsm', q, k,
                   preferred_element_type=jnp.float32) * (X_HEAD_DIM ** -0.5)
    p = jax.nn.softmax(s, axis=-1).astype(v.dtype)
    o = jnp.einsum('bhsm,bmhd->bshd', p, v).reshape(B, S, D_X)
    return o @ w_xo

def _clamped_swiglu(gu):
    g = jnp.minimum(gu[..., ::2], SWIGLU_LIMIT)
    lin = jnp.clip(gu[..., 1::2], -SWIGLU_LIMIT, SWIGLU_LIMIT)
    return g * jax.nn.sigmoid(SWIGLU_ALPHA * g) * (lin + 1.0)

def _moe(h, w_router, b_router, w_gate_up, b_gate_up, w_down, b_down):
    B, S, D = h.shape
    n_tok = B * S
    hf = h.reshape(n_tok, D)
    logits = (hf @ w_router).astype(jnp.float32) + b_router.astype(jnp.float32)
    top_val, top_idx = lax.top_k(logits, TOP_K)
    gates = jax.nn.softmax(top_val, axis=-1)
    n_assign = n_tok * TOP_K
    expert_ids = top_idx.reshape(-1)
    token_ids = jnp.arange(n_assign, dtype=jnp.int32) // TOP_K
    order = jnp.argsort(expert_ids)
    sorted_e = expert_ids[order]
    sorted_tok = token_ids[order]
    sorted_gate = gates.reshape(-1)[order]
    counts = jnp.bincount(expert_ids, length=N_EXPERTS)
    padded = (counts + EXPERT_BLOCK - 1) // EXPERT_BLOCK * EXPERT_BLOCK
    start = jnp.cumsum(counts) - counts
    pend = jnp.cumsum(padded)
    pstart = pend - padded
    dest = pstart[sorted_e] + (jnp.arange(n_assign, dtype=jnp.int32) - start[sorted_e])
    n_pad = n_assign + N_EXPERTS * EXPERT_BLOCK
    n_blocks = n_pad // EXPERT_BLOCK
    tok_pad = jnp.zeros((n_pad,), jnp.int32).at[dest].set(sorted_tok)
    block_e = jnp.searchsorted(pend, jnp.arange(n_blocks) * EXPERT_BLOCK, side='right')
    block_e = jnp.minimum(block_e, N_EXPERTS - 1).astype(jnp.int32)

    def expert_block(args):
        tok, e = args
        xb = hf[tok]
        act = _clamped_swiglu(xb @ w_gate_up[e] + b_gate_up[e])
        return act @ w_down[e] + b_down[e]

    y_pad = lax.map(expert_block, (tok_pad.reshape(n_blocks, EXPERT_BLOCK), block_e))
    y_sorted = y_pad.reshape(n_pad, D)[dest].astype(jnp.float32)
    out = jnp.zeros((n_tok, D), jnp.float32).at[sorted_tok].add(sorted_gate[:, None] * y_sorted)
    return out.astype(h.dtype).reshape(B, S, D)

def setup_inputs(seed: int = 0) -> dict:
    key = jax.random.key(seed)
    ks = jax.random.split(key, 26)
    f32 = jnp.float32

    def nrm(k, shape, scale):
        return jax.random.normal(k, shape, f32) * scale

    def gain(k, shape):
        return 1.0 + 0.1 * jax.random.normal(k, shape, f32)

    L = DEPTH
    return {
        "x": nrm(ks[0], (BATCH, SEQ, D_MODEL), 1.0),
        "mem": nrm(ks[1], (BATCH, N_MEM, D_MODEL), 1.0),
        "norm_mix_g": gain(ks[2], (L, D_MODEL)),
        "w_in": nrm(ks[3], (L, D_MODEL, D_IN_PROJ), D_MODEL ** -0.5),
        "q_norm_g": gain(ks[4], (L, ATT_HEAD_DIM)),
        "k_norm_g": gain(ks[5], (L, ATT_HEAD_DIM)),
        "rel_bias": nrm(ks[6], (L, ATT_HEADS, N_REL), 0.5),
        "conv_w": nrm(ks[7], (L, CONV_W, D_CONV), 0.5),
        "out_norm_a_g": gain(ks[8], (L, D_ATT)),
        "out_norm_b_g": gain(ks[9], (L, D_CONV)),
        "w_out": nrm(ks[10], (L, D_MIX, D_MODEL), D_MIX ** -0.5),
        "norm_xattn_g": gain(ks[11], (L, D_MODEL)),
        "norm_mem_g": gain(ks[12], (L, D_MODEL)),
        "w_xq": nrm(ks[13], (L, D_MODEL, D_X), D_MODEL ** -0.5),
        "w_xkv": nrm(ks[14], (L, D_MODEL, 2 * D_X), D_MODEL ** -0.5),
        "xq_norm_g": gain(ks[15], (L, X_HEAD_DIM)),
        "xk_norm_g": gain(ks[16], (L, X_HEAD_DIM)),
        "w_xo": nrm(ks[17], (L, D_X, D_MODEL), D_X ** -0.5),
        "norm_ffn_g": gain(ks[18], (L, D_MODEL)),
        "w_router": nrm(ks[19], (L, D_MODEL, N_EXPERTS), D_MODEL ** -0.5),
        "b_router": nrm(ks[20], (L, N_EXPERTS), 0.01),
        "w_gate_up": nrm(ks[21], (L, N_EXPERTS, D_MODEL, 2 * D_FF), D_MODEL ** -0.5),
        "b_gate_up": nrm(ks[22], (L, N_EXPERTS, 2 * D_FF), 0.02),
        "w_down": nrm(ks[23], (L, N_EXPERTS, D_FF, D_MODEL), D_FF ** -0.5),
        "b_down": nrm(ks[24], (L, N_EXPERTS, D_MODEL), 0.02),
    }

def reference(x, mem, norm_mix_g, w_in, q_norm_g, k_norm_g, rel_bias, conv_w,
              out_norm_a_g, out_norm_b_g, w_out, norm_xattn_g, norm_mem_g,
              w_xq, w_xkv, xq_norm_g, xk_norm_g, w_xo, norm_ffn_g,
              w_router, b_router, w_gate_up, b_gate_up, w_down, b_down):
    B, S, _ = x.shape
    splits = [D_ATT, 2 * D_ATT, 3 * D_ATT, 3 * D_ATT + D_CONV, 3 * D_ATT + 2 * D_CONV]
    for l in range(DEPTH):
        h = _rmsnorm(x, norm_mix_g[l])
        proj = h @ w_in[l]
        q, k, v, bg, cg, xv = jnp.split(proj, splits, axis=-1)
        shp = (B, S, ATT_HEADS, ATT_HEAD_DIM)
        y_a = _chunk_attention(q.reshape(shp), k.reshape(shp), v.reshape(shp),
                               q_norm_g[l], k_norm_g[l], rel_bias[l])
        y_b = _short_conv(bg, cg, xv, conv_w[l])
        y = jnp.concatenate([_rmsnorm(y_a, out_norm_a_g[l]),
                             _rmsnorm(y_b, out_norm_b_g[l])], axis=-1)
        x = x + y @ w_out[l]
        x = x + _memory_xattn(_rmsnorm(x, norm_xattn_g[l]), mem, norm_mem_g[l],
                              w_xq[l], w_xkv[l], xq_norm_g[l], xk_norm_g[l], w_xo[l])
        x = x + _moe(_rmsnorm(x, norm_ffn_g[l]), w_router[l], b_router[l],
                     w_gate_up[l], b_gate_up[l], w_down[l], b_down[l])
    return x


_drawn_inputs = setup_inputs


def setup_inputs(seed=0):
    import zlib

    import numpy as np

    out = dict(_drawn_inputs(seed))
    spreads = {}
    factors = {'b_gate_up': 6.836, 'b_down': 7.877}
    for name, (base, spread) in spreads.items():
        noise = np.random.default_rng([zlib.crc32(name.encode()), seed]).standard_normal(out[name].shape)
        drawn = base * np.exp(spread * noise) if base else spread * noise
        out[name] = __import__('jax').numpy.asarray(drawn.astype(out[name].dtype))
    for name, factor in factors.items():
        out[name] = (out[name] * factor).astype(out[name].dtype)
    return out
```

```python
from contextlib import ExitStack

import numpy as np

import concourse.bass as bass
import concourse.mybir as mybir
from concourse.alu_op_type import AluOpType as ALU

ACT = mybir.ActivationFunctionType
F32 = mybir.dt.float32
I32 = mybir.dt.int32
U32 = mybir.dt.uint32
AX_X = mybir.AxisListType.X

P = 128
D = 1024
KD = D // P
SEQ = 1024
TILES = SEQ // P
CHUNK = 64
HEADS, HEAD = 8, 64
PAIRS = HEADS // 2
D_ATT = HEADS * HEAD
CONV = 512
CS = CONV // P
CONV_W = 3
N_IN = 3 * D_ATT + 3 * CONV
BAND_TILES = 5
WINDOW = BAND_TILES * P
MAX_REL = 256
N_REL = 2 * MAX_REL + 1
MEM = 256
MT = MEM // P
XH, XD = 4, 128
D_X = XH * XD
E = 32
TOPK = 4
FF = 1024
FS = FF // P
LIMIT, ALPHA = 7.0, 1.702
EPS = 1e-6
NEG = -1e30
UNIT = 256
UB = UNIT // P
MAX_UNITS = E + SEQ * TOPK // UNIT
PAD = UNIT


class Map:

    def __init__(self, nc, base):
        self.nc, self.at = nc, base

    def put(self, name, shape, dt=F32, at=None):
        size = 4
        for n in shape[1:]:
            size *= n
        size = (size + 31) // 32 * 32
        if at is None:
            at, self.at = self.at, self.at + size
        return self.nc.alloc_sbuf_tensor_at(name, shape, dt, offset=at)


class Buffers:
    pass


def lay_out(nc):
    m = Buffers()
    s = Map(nc, (nc.sbuf_base + 31) // 32 * 32)
    m.ident = s.put("ident", [P, P])
    m.ones = s.put("ones", [P, P])
    m.before = s.put("before", [P, P])
    m.g_mix = s.put("g_mix", [P, KD])
    m.g_x = s.put("g_x", [P, KD])
    m.g_ffn = s.put("g_ffn", [P, KD])
    m.g_mem = s.put("g_mem", [P, KD])
    m.g_q = s.put("g_q", [P, 1])
    m.g_k = s.put("g_k", [P, 1])
    m.g_xq = s.put("g_xq", [P, 1])
    m.g_xk = s.put("g_xk", [P, 1])
    m.g_a = s.put("g_a", [P, CS])
    m.g_b = s.put("g_b", [P, CS])
    m.conv_w = s.put("conv_w_sb", [P, CONV_W, CS])
    m.seen = s.put("seen", [P, E])
    m.small_end = s.at
    m.kxT = s.put("kxT", [P, XH, MEM])
    m.vx = s.put("vx", [P, MT, D_X])
    m.kT = s.put("kT", [P, PAIRS, SEQ])
    m.v = s.put("v", [P, TILES, D_ATT])
    keep = s.at
    m.qT = s.put("qT", [P, PAIRS, SEQ])
    m.ybT = s.put("ybT", [P, CS, SEQ])
    wide = s.at
    m.w_in = s.put("w_in_sb", [P, KD, N_IN])
    m.xin = [s.put(f"xin{b}", [P, D]) for b in range(2)]
    m.hT = [s.put(f"hT{b}", [P, KD, P]) for b in range(2)]
    own = s.at
    m.qn = s.put("qn", [P, D])
    m.u = s.put("u", [P, CS, P + CONV_W - 1])
    m.cg = s.put("cg", [P, 2, P])
    m.ct = s.put("ct", [P, P])
    m.ybr = s.put("ybr", [P, CS, P])
    m.sqb = s.put("sqb", [P, CS, P])
    m.rb = s.put("rb", [P, P])
    m.sqk = s.put("sqk", [P, D])
    m.ss = s.put("ss", [P, 2, 1])
    m.ssqk = s.put("ssqk", [P, 16])
    m.ext = s.put("ext", [HEADS, WINDOW + P])
    m.empty = s.put("empty", [P, E * SEQ // P, 2], I32)
    m.w_xkv = s.put("w_xkv_sb", [P, KD, 2 * D_X], at=keep)
    m.keep, m.wide, m.own, m.s = keep, wide, own, s
    assert s.at <= nc.sbuf_usable_end, (s.at, nc.sbuf_usable_end)
    return m


def phase_a(nc, m, d, sem, psum):
    trp = psum("a_tr", [P, 2, 512])
    qkp = psum("a_qk", [P, 2, 512])
    vp = psum("a_v", [P, 512])
    cvp = psum("a_cv", [P, 2, 512])
    sbp = psum("a_sb", [P, 512])

    consts = sem("a_consts")
    gains = sem("a_gains")
    wxkv_in = sem("a_wxkv_in")
    win_in = sem("a_win_in")
    mem_in = [sem(f"a_mem_in{b}") for b in range(2)]
    m_sq, m_ms, m_h, m_tr = sem("m_sq"), sem("m_ms"), sem("m_h"), sem("m_tr")
    m_hTv, m_hTa = sem("m_hTv"), sem("m_hTa")
    m_kv, m_ksq, m_kms, m_krs, m_kn, m_ktr = (sem("m_" + x) for x in ("kv", "ksq", "kms", "krs", "kn", "ktr"))
    m_kT, m_v = sem("m_kT"), sem("m_v")
    x_in = [sem(f"a_x_in{b}") for b in range(2)]
    x_sq, x_ms, x_h, x_tr = sem("x_sq"), sem("x_ms"), sem("x_h"), sem("x_tr")
    hT_v, hT_a = sem("hT_v"), sem("hT_a")
    cv_mm = [sem(f"cv_mm{c}") for c in range(CS)]
    cg_a = [sem(f"cg_a{c}") for c in range(CS)]
    cv_y = [sem(f"cv_y{c}") for c in range(CS)]
    cv_free = [sem(f"cv_free{c}") for c in range(CS)]
    sqb_a, sb_mm, bms_v, brs_a = sem("sqb_a"), sem("sb_mm"), sem("bms_v"), sem("brs_a")
    qk_mm, qksq_a, qkms_v, qkrs_a, qn_v = (sem(x) for x in ("qk_mm", "qksq_a", "qkms_v", "qkrs_a", "qn_v"))
    v_mm, v_a, qk_tr, qT_v, kT_a = (sem(x) for x in ("v_mm", "v_a", "qk_tr", "qT_v", "kT_a"))
    ext_in, ext_sb, ext_out, slots_out = sem("ext_in"), sem("ext_sb"), sem("ext_out"), sem("slots_out")
    xm = m.hT
    cvv = cvp[:, :, 0:3 * P].rearrange("p b (j t) -> p b j t", j=3)

    def rows(ap, t):
        return ap[bass.ds(t * P, P), :]

    with nc.Block() as block:

        @block.sync
        def _(sp):
            for b in range(2):
                sp.dma_start(m.xin[b][:], d.mem[b * P:(b + 1) * P, :]).then_inc(mem_in[b], 16)
            with nc.allow_non_contiguous_dma(reason="gains, one value to a partition"):
                for tile, src in ((m.g_mem, d.norm_mem_g), (m.g_mix, d.norm_mix_g), (m.g_x, d.norm_xattn_g),
                                  (m.g_ffn, d.norm_ffn_g), (m.g_a, d.out_norm_a_g), (m.g_b, d.out_norm_b_g),
                                  (m.g_xq, d.xq_norm_g), (m.g_xk, d.xk_norm_g)):
                    sp.dma_start(tile[:], src.rearrange("(k p) -> p k", p=P)).then_inc(gains, 16)
                for h in range(2):
                    at = slice(h * HEAD, (h + 1) * HEAD)
                    sp.dma_start(m.g_q[at, :], d.q_norm_g.rearrange("(p a) -> p a", a=1)).then_inc(gains, 16)
                    sp.dma_start(m.g_k[at, :], d.k_norm_g.rearrange("(p a) -> p a", a=1)).then_inc(gains, 16)
                for j in range(CONV_W):
                    sp.dma_start(m.conv_w[:, j, :], d.conv_w[j].rearrange("(c p) -> p c", p=P)).then_inc(gains, 16)
            n_gains = 8 + 4 + CONV_W
            sp.dma_start(m.w_xkv[:], d.w_xkv.rearrange("(k p) n -> p k n", p=P)).then_inc(wxkv_in, 16)
            sp.dma_start(m.w_in[:], d.w_in.rearrange("(k p) n -> p k n", p=P)).then_inc(win_in, 16)
            sp.wait_ge(m_tr, 2)
            for b in range(2):
                sp.dma_start(m.xin[b][:], rows(d.x, b)).then_inc(x_in[b], 16)
            with sp.Fori(0, TILES // 2 - 1) as i:
                for b in range(2):
                    seen = sp.snap(2 * i + (b + 1))
                    sp.wait_ge(x_tr, seen)
                    sp.dma_start(m.xin[b][:], rows(d.x, 2 * i + (b + 2))).then_inc(x_in[b], 16)
            m.n_gains = 16 * n_gains

        @block.gpsimd
        def _(pool):
            nc.gpsimd.memset(m.ident[:], 0.0).then_inc(consts, 1)
            nc.gpsimd.memset(m.ones[:], 1.0).then_inc(consts, 1)
            pool.wait_ge(consts, 2)
            nc.gpsimd.affine_select(out=m.ident[:], in_=m.ident[:], compare_op=ALU.not_equal, fill=1.0, base=0,
                                    pattern=[[-1, P]], channel_multiplier=1).then_inc(consts, 1)
            nc.gpsimd.affine_select(out=m.before[:], in_=m.ones[:], compare_op=ALU.is_gt, fill=0.0, base=0,
                                    pattern=[[1, P]], channel_multiplier=-1).then_inc(consts, 1)
            flat = WINDOW + P - 1 - (MAX_REL + P)
            with nc.allow_non_contiguous_dma(reason="eight short rows"):
                pool.dma_start(m.ext[:, flat:], d.rel_rev[:, 0:WINDOW + P - flat]).then_inc(ext_in, 16)
            nc.gpsimd.memset(m.empty[:], 0).then_inc(ext_sb, 1)
            pool.wait_ge(ext_sb, 1)
            nc.gpsimd.iota(m.empty[:, :, 0], [[0, E * SEQ // P // UNIT], [1, UNIT]], base=SEQ,
                           channel_multiplier=0).then_inc(ext_sb, 1)
            pool.wait_ge(ext_sb, 2)
            pool.dma_start(d.slots.rearrange("(p s) c -> p (s c)", p=P),
                           m.empty[:].rearrange("p s c -> p (s c)")).then_inc(slots_out, 16)
            pool.wait_ge(ext_in, 16)
            nc.gpsimd.tensor_copy(m.ext[:, 0:flat], m.ext[:, flat:flat + 1].to_broadcast([HEADS, flat])).then_inc(ext_sb, 1)
            pool.wait_ge(ext_sb, 3)
            pool.dma_start(bass.AP(tensor=d.band.tensor, offset=0,
                                   ap=[[WINDOW + P, HEADS], [HEADS * (WINDOW + P) + 1, P], [1, WINDOW + P]]),
                           m.ext[:].unsqueeze(1).to_broadcast([HEADS, P, WINDOW + P])).then_inc(ext_out, 16)
            pool.wait_ge(ext_out, 16)
            pool.wait_ge(slots_out, 16)

        @block.tensor
        def _(pe):
            pe.wait_ge(consts, 4)
            for b in range(MT):
                pe.wait_ge(m_h, b + 1)
                if b:
                    pe.wait_ge(m_hTv, b)
                    pe.wait_ge(m_hTa, b)
                for k in range(KD):
                    last = nc.tensor.transpose(trp[:, k // 4, (k % 4) * P:(k % 4 + 1) * P],
                                               m.xin[b][:, k * P:(k + 1) * P], m.ident[:])
                last.then_inc(m_tr, 1)
            pe.wait_ge(wxkv_in, 16)
            for b in range(MT):
                pe.wait_ge(m_hTv, b + 1)
                pe.wait_ge(m_hTa, b + 1)
                if b:
                    pe.wait_ge(m_kn, b)
                    pe.wait_ge(m_v, b)
                for half in range(2):
                    for k in range(KD):
                        last = nc.tensor.matmul(qkp[:, half, :], xm[b][:, k, :],
                                                m.w_xkv[:, k, half * D_X:(half + 1) * D_X],
                                                start=(k == 0), stop=(k == KD - 1))
                last.then_inc(m_kv, 1)
                pe.wait_ge(m_kn, b + 1)
                for h in range(XH):
                    last = nc.tensor.transpose(trp[:, 0, h * P:(h + 1) * P], m.qn[:, h * XD:(h + 1) * XD], m.ident[:])
                last.then_inc(m_ktr, 1)
                pe.wait_ge(m_kT, b + 1)

            def transpose_x(b, t1):
                pe.wait_ge(x_h, t1)
                for k in range(KD):
                    last = nc.tensor.transpose(trp[:, k // 4, (k % 4) * P:(k % 4 + 1) * P],
                                               m.xin[b][:, k * P:(k + 1) * P], m.ident[:])
                last.then_inc(x_tr, 1)

            def convolve(b, c, t1):
                pe.wait_ge(cv_free[(c + 2) % CS], t1)
                for j in range(3):
                    col = 3 * D_ATT + j * CONV + c * P
                    for k in range(KD):
                        last = nc.tensor.matmul(cvv[:, c % 2, j, :], m.w_in[:, k, col:col + P], m.hT[b][:, k, :],
                                                start=(k == 0), stop=(k == KD - 1))
                last.then_inc(cv_mm[c], 1)

            def tile(b, t1, t2, more):
                pe.wait_ge(hT_v, t1)
                pe.wait_ge(hT_a, t1)
                convolve(b, 0, t1)
                convolve(b, 1, t1)
                pe.wait_ge(qT_v, t1)
                pe.wait_ge(kT_a, t1)
                if more:
                    transpose_x(1 - b, t2)
                convolve(b, 2, t1)
                convolve(b, 3, t1)
                for half in range(2):
                    for k in range(KD):
                        last = nc.tensor.matmul(qkp[:, half, :], m.hT[b][:, k, :],
                                                m.w_in[:, k, half * D_ATT:(half + 1) * D_ATT],
                                                start=(k == 0), stop=(k == KD - 1))
                last.then_inc(qk_mm, 1)
                pe.wait_ge(sqb_a, t1)
                for c in range(CS):
                    last = nc.tensor.matmul(sbp[:, 0:P], m.ones[:], m.sqb[:, c, :], start=(c == 0), stop=(c == CS - 1))
                last.then_inc(sb_mm, 1)
                for k in range(KD):
                    last = nc.tensor.matmul(vp[:], m.hT[b][:, k, :], m.w_in[:, k, 2 * D_ATT:3 * D_ATT],
                                            start=(k == 0), stop=(k == KD - 1))
                last.then_inc(v_mm, 1)
                pe.wait_ge(qn_v, t1)
                if more:
                    pe.wait_ge(hT_v, t2)
                    pe.wait_ge(hT_a, t2)
                for j in range(2 * PAIRS):
                    last = nc.tensor.transpose(trp[:, j // PAIRS, (j % PAIRS) * P:(j % PAIRS + 1) * P],
                                               m.qn[:, j * P:(j + 1) * P], m.ident[:])
                last.then_inc(qk_tr, 1)

            transpose_x(0, 1)
            pe.wait_ge(win_in, 16)
            with pe.Fori(0, TILES // 2 - 1) as i:
                count = [pe.snap(2 * i + j) for j in (1, 2, 3)]
                for b in range(2):
                    tile(b, count[b], count[b + 1], True)
            for b in range(2):
                tile(b, TILES - 1 + b, TILES + b, b == 0)

        @block.scalar
        def _(act):
            act.sem_inc(kT_a, 1)
            act.wait_ge(gains, m.n_gains)

            def norm(b, landed, t1, sq, ms, h):
                act.wait_ge(*landed)
                nc.scalar.activation(m.sqk[:], m.xin[b][:], ACT.Square, accum_out=m.ss[:, b, :]).then_inc(sq, 1)
                act.wait_ge(ms, t1)
                nc.scalar.activation(m.ss[:, b, :], m.ss[:, b, :], ACT.Sqrt)
                act.drain()
                nc.scalar.activation(m.xin[b][:], m.xin[b][:], ACT.Copy, scale=m.ss[:, b, :]).then_inc(h, 1)

            def copy_out(b, gain, tr, t1, done):
                act.wait_ge(tr, t1)
                for k in range(KD // 2, KD):
                    last = nc.scalar.activation(m.hT[b][:, k, :], trp[:, 1, (k % 4) * P:(k % 4 + 1) * P], ACT.Copy,
                                                scale=gain[:, k:k + 1])
                last.then_inc(done, 1)

            for b in range(MT):
                norm(b, (mem_in[b], 16), b + 1, m_sq, m_ms, m_h)
                copy_out(b, m.g_mem, m_tr, b + 1, m_hTa)
            for b in range(MT):
                act.wait_ge(m_kv, b + 1)
                nc.scalar.activation(m.sqk[:, 0:D_X], qkp[:, 0, :], ACT.Square).then_inc(m_ksq, 1)
                nc.scalar.copy(m.vx[:, b, :], qkp[:, 1, :]).then_inc(m_v, 1)
                act.wait_ge(m_kms, b + 1)
                nc.scalar.activation(m.ssqk[:, 0:XH], m.ssqk[:, 0:XH], ACT.Sqrt).then_inc(m_krs, 1)
                act.wait_ge(m_ktr, b + 1)
                nc.scalar.activation(m.kxT[:, :, b * P:(b + 1) * P], trp[:, 0, :].rearrange("p (h t) -> p h t", h=XH),
                                     ACT.Copy, scale=m.g_xk[:]).then_inc(m_kT, 1)

            def gate_copy(c, t1):
                act.wait_ge(cv_mm[c], t1)
                nc.scalar.copy(m.cg[:, c % 2, :], cvv[:, c % 2, 1, :]).then_inc(cg_a[c], 1)

            def square(c, t1):
                act.wait_ge(cv_y[c], t1)
                ins = nc.scalar.activation(m.sqb[:, c, :], m.ybr[:, c, :], ACT.Square)
                if c == CS - 1:
                    ins.then_inc(sqb_a, 1)

            def tile(b, t, t1, t2, dma1, more):
                if more:
                    norm(1 - b, (x_in[1 - b], dma1), t2, x_sq, x_ms, x_h)
                gate_copy(0, t1)
                gate_copy(1, t1)
                square(0, t1)
                square(1, t1)
                if more:
                    copy_out(1 - b, m.g_mix, x_tr, t2, hT_a)
                gate_copy(2, t1)
                gate_copy(3, t1)
                square(2, t1)
                square(3, t1)
                act.wait_ge(qk_mm, t1)
                nc.scalar.activation(m.sqk[:], qkp[:], ACT.Square).then_inc(qksq_a, 1)
                act.wait_ge(qkms_v, t1)
                nc.scalar.activation(m.ssqk[:], m.ssqk[:], ACT.Sqrt).then_inc(qkrs_a, 1)
                act.wait_ge(bms_v, t1)
                nc.scalar.activation(m.rb[:], m.rb[:], ACT.Sqrt).then_inc(brs_a, 1)
                act.wait_ge(v_mm, t1)
                nc.scalar.copy(m.v[:, t, :], vp[:]).then_inc(v_a, 1)
                act.wait_ge(qk_tr, t1)
                nc.scalar.activation(m.kT[:, :, bass.ds(t * P, P)], trp[:, 1, :].rearrange("p (h t) -> p h t", h=PAIRS),
                                     ACT.Copy, scale=m.g_k[:]).then_inc(kT_a, 1)

            norm(0, (x_in[0], 16), 1, x_sq, x_ms, x_h)
            copy_out(0, m.g_mix, x_tr, 1, hT_a)
            with act.Fori(0, TILES // 2 - 1) as i:
                count = [act.snap(2 * i + j) for j in (1, 2, 3)]
                dma = [act.snap(16 * i + 16), act.snap(16 * i + 32)]
                for b in range(2):
                    tile(b, 2 * i + b, count[b], count[b + 1], dma[b], True)
            for b in range(2):
                tile(b, TILES - 2 + b, TILES - 1 + b, TILES + b, 16 * (TILES // 2), b == 0)

        @block.vector
        def _(dve):
            nc.vector.memset(m.u[:, :, 0:CONV_W - 1], 0.0).then_inc(qT_v, 1)
            for c in (2, 3):
                dve.sem_inc(cv_free[c], 1)
            dve.wait_ge(gains, m.n_gains)

            def rstd2(ap, n):
                nc.vector.tensor_scalar(ap, ap, 1.0 / n, EPS, ALU.mult, ALU.add)
                dve.drain()
                return nc.vector.reciprocal(ap, ap)

            def norm(b, t1, sq, ms):
                dve.wait_ge(sq, t1)
                rstd2(m.ss[:, b, :], D).then_inc(ms, 1)

            def copy_out(b, gain, tr, t1, done):
                dve.wait_ge(tr, t1)
                for k in range(KD // 2):
                    last = nc.vector.tensor_scalar(m.hT[b][:, k, :], trp[:, 0, k * P:(k + 1) * P], gain[:, k:k + 1],
                                                   None, ALU.mult)
                last.then_inc(done, 1)

            nc.vector.tensor_scalar(m.g_q[:], m.g_q[:], HEAD ** -0.5, None, ALU.mult)
            nc.vector.tensor_scalar(m.g_xq[:], m.g_xq[:], XD ** -0.5, None, ALU.mult)
            for b in range(MT):
                norm(b, b + 1, m_sq, m_ms)
                copy_out(b, m.g_mem, m_tr, b + 1, m_hTv)
            for b in range(MT):
                dve.wait_ge(m_ksq, b + 1)
                nc.vector.reduce_sum(m.ssqk[:, 0:XH], m.sqk[:, 0:D_X].rearrange("p (h e) -> p h e", h=XH), AX_X)
                dve.drain()
                rstd2(m.ssqk[:, 0:XH], XD).then_inc(m_kms, 1)
                dve.wait_ge(m_krs, b + 1)
                nc.vector.tensor_tensor(m.qn[:, 0:D_X].rearrange("p (h e) -> p h e", h=XH),
                                        qkp[:, 0, :].rearrange("p (h e) -> p h e", h=XH),
                                        m.ssqk[:, 0:XH].unsqueeze(2).to_broadcast([P, XH, XD]),
                                        ALU.mult).then_inc(m_kn, 1)

            def conv(c, t1):
                dve.wait_ge(cg_a[c], t1)
                u = m.u[:, c, :]
                nc.vector.tensor_tensor(u[:, 2:P + 2], cvv[:, c % 2, 2, :], m.cg[:, c % 2, :], ALU.mult)
                dve.drain()
                nc.vector.tensor_scalar(m.ct[:], u[:, 2:P + 2], m.conv_w[:, 2, c:c + 1], None, ALU.mult)
                dve.drain()
                nc.vector.scalar_tensor_tensor(m.ct[:], u[:, 1:P + 1], m.conv_w[:, 1, c:c + 1], m.ct[:], ALU.mult, ALU.add)
                dve.drain()
                nc.vector.scalar_tensor_tensor(m.ct[:], u[:, 0:P], m.conv_w[:, 0, c:c + 1], m.ct[:], ALU.mult, ALU.add)
                dve.drain()
                nc.vector.tensor_tensor(m.ybr[:, c, :], cvv[:, c % 2, 0, :], m.ct[:], ALU.mult).then_inc(cv_y[c], 1)
                nc.vector.tensor_copy(u[:, 0:2], u[:, P:P + 2]).then_inc(cv_free[c], 1)
                dve.drain()

            def tile(b, t, t1, t2, more):
                if more:
                    norm(1 - b, t2, x_sq, x_ms)
                conv(0, t1)
                conv(1, t1)
                if more:
                    copy_out(1 - b, m.g_mix, x_tr, t2, hT_v)
                conv(2, t1)
                conv(3, t1)
                dve.wait_ge(qksq_a, t1)
                nc.vector.reduce_sum(m.ssqk[:], m.sqk[:].rearrange("p (h e) -> p h e", h=16), AX_X)
                dve.drain()
                rstd2(m.ssqk[:], HEAD).then_inc(qkms_v, 1)
                dve.wait_ge(sb_mm, t1)
                nc.vector.tensor_scalar(m.rb[:], sbp[:, 0:P], 1.0 / CONV, EPS, ALU.mult, ALU.add)
                dve.drain()
                nc.vector.reciprocal(m.rb[:], m.rb[:]).then_inc(bms_v, 1)
                dve.wait_ge(qkrs_a, t1)
                nc.vector.tensor_tensor(m.qn[:].rearrange("p (h e) -> p h e", h=16),
                                        qkp[:].rearrange("p a (h e) -> p (a h) e", e=HEAD),
                                        m.ssqk[:].unsqueeze(2).to_broadcast([P, 16, HEAD]), ALU.mult).then_inc(qn_v, 1)
                dve.wait_ge(brs_a, t1)
                for c in range(CS):
                    nc.vector.scalar_tensor_tensor(m.ybT[:, c, bass.ds(t * P, P)], m.ybr[:, c, :], m.g_b[:, c:c + 1],
                                                   m.rb[:], ALU.mult, ALU.mult)
                dve.wait_ge(qk_tr, t1)
                nc.vector.tensor_scalar(m.qT[:, :, bass.ds(t * P, P)], trp[:, 0, :].rearrange("p (h t) -> p h t", h=PAIRS),
                                        m.g_q[:], None, ALU.mult).then_inc(qT_v, 1)

            norm(0, 1, x_sq, x_ms)
            copy_out(0, m.g_mix, x_tr, 1, hT_v)
            with dve.Fori(0, TILES // 2 - 1) as i:
                count = [dve.snap(2 * i + j) for j in (1, 2, 3)]
                for b in range(2):
                    tile(b, 2 * i + b, count[b], count[b + 1], True)
            for b in range(2):
                tile(b, TILES - 2 + b, TILES - 1 + b, TILES + b, b == 0)


ORDER = [("scores", 0), ("scores", 1), ("turn_a", -1),
         ("turn_p", 0), ("values", 0), ("scores", 2), ("project", -1),
         ("turn_p", 1), ("values", 1), ("scores", 3), ("turn_p", 2), ("values", 2), ("scores", 4),
         ("turn_h", -1), ("turn_p", 3), ("values", 3), ("query", -1),
         ("scores", 5), ("turn_p", 4), ("values", 4), ("turn_q", -1), ("scores", 6), ("scores_x", -1),
         ("turn_p", 5), ("values", 5), ("scores", 7), ("turn_x", -1), ("turn_p", 6), ("values_x", -1), ("values", 6),
         ("project_x", -1), ("turn_p", 7), ("values", 7), ("turn_r", -1), ("route", -1), ("rank", -1)]
PEELED = BAND_TILES - 1


def spans(start, n):
    out, at = [], start
    while at < start + n:
        to = min(start + n, (at // 512 + 1) * 512)
        out.append((at, to))
        at = to
    return out


def phase_b(nc, m, d, sem, psum):
    s = Map(nc, m.wide)
    w_out = s.put("w_out_sb", [P, KD, D])
    w_xq = s.put("w_xq_sb", [P, KD, D_X])
    w_xo = s.put("w_xo_sb", [P, XH, D])
    bias = s.put("bias", [P, HEADS, WINDOW])
    s.at = m.own
    qz = s.put("qz", [P, HEADS, P])
    ybs = s.put("ybs", [P, CS, P])
    p = [s.put(f"p{b}", [P, WINDOW]) for b in range(2)]
    pt = [s.put(f"pt{b}", [P, WINDOW]) for b in range(2)]
    o = s.put("o", [P, D_ATT])
    x2 = m.xin[0]
    xres = m.xin[1]
    hn = m.hT[0][:].rearrange("p a b -> p (a b)")
    hT = m.hT[1]
    s2 = Map(nc, m.wide + 4 * (KD * D + KD * D_X + XH * D + HEADS * WINDOW))
    yaT = s2.put("yaT", [P, CS, P])
    qxT = s2.put("qxT", [P, XH, P])
    oxT = s2.put("oxT", [P, XH, P])
    qxn = s2.put("qxn", [P, D_X])
    sqx = s2.put("sqx", [P, D])
    assert s2.at <= m.wide + 4 * KD * N_IN
    px = sqx[:].rearrange("p (h k) -> p h k", h=XH)
    pxT = m.hT[0]
    w_r = s.put("w_r", [P, KD, E])
    b_r = s.put("b_r", [P, E])
    half = s.put("half", [P, XH])
    small = s.put("small", [P, 64])
    nm, rs = small[:, 0:8], small[:, 8:16]
    ssa, ssx, ssq, nmx, rsx = (small[:, 16:17], small[:, 17:18], small[:, 20:24], small[:, 24:28], small[:, 28:32])
    ssr = small[:, 18:19]
    pw = s.put("pw", [P, 8])
    lg = s.put("lg", [P, E])
    top = s.put("top", [P, 8])
    topi = s.put("topi", [P, 8], U32)
    topf = s.put("topf", [P, TOPK])
    eids = s.put("eids", [P, E])
    oneh = s.put("oneh", [P, TOPK, E])
    ohp = s.put("ohp", [P, TOPK, E])
    mask = s.put("mask", [P, E])
    gsum = s.put("gsum", [P, 8])
    slotf = s.put("slotf", [P, TOPK])
    tok = s.put("tok", [P, TOPK])
    sloti = s.put("sloti", [P, TOPK], I32)
    pay = s.put("pay", [P, TOPK, 2], I32)
    assert s.at <= nc.sbuf_usable_end, s.at

    att = psum("b_att", [P, 2048])
    ps, ptp, po = att[:, 0:WINDOW], att[:, 1024:1024 + WINDOW], att[:, 1024 + WINDOW:1024 + WINDOW + P]
    px0 = psum("b_x", [P, 1024])
    py0 = psum("b_y", [P, 1024])

    w_in = [sem(f"b_w{i}") for i in range(3)]
    bias_in, consts, b_small = sem("b_bias"), sem("b_consts"), sem("b_small")
    zeroed, pads = sem("b_zeroed"), sem("b_pads")
    sc_mm, sc_v, ex_a, at_mm, pt_a, av_mm, o_v = (
        [sem(f"{n}{h}") for h in range(HEADS)] for n in ("sc_mm", "sc_v", "ex_a", "at_mm", "pt_a", "av_mm", "o_v"))
    met_v, met_p = sem("b_met_v"), sem("b_met_p")
    qz_v, yb_p, xres_in = sem("qz_v"), sem("yb_p"), sem("xres_in")
    sqa_a, msa_v, pwa_p, ya_v, ta_mm, yaT_v = (sem(x) for x in ("sqa_a", "msa_v", "pwa_p", "ya_v", "ta_mm", "yaT_v"))
    pr_mm, x2_v, sq2_a, ms2_v, pw2_p, hn_a, th_mm, hT_v, hT_a = (
        sem(x) for x in ("pr_mm", "x2_v", "sq2_a", "ms2_v", "pw2_p", "hn_a", "th_mm", "bhT_v", "bhT_a"))
    xq_mm, sqq_a, msq_v, pwq_p, qxn_v, tq_mm, qxT_a = (
        sem(x) for x in ("xq_mm", "sqq_a", "msq_v", "pwq_p", "qxn_v", "tq_mm", "qxT_a"))
    sx_mm, mxx_v, exx_a, px_v, tx_mm, pxT_v, pxT_a, vx_mm, oxT_a = (
        sem(x) for x in ("sx_mm", "mxx_v", "exx_a", "px_v", "tx_mm", "pxT_v", "pxT_a", "vx_mm", "oxT_a"))
    xo_mm, x3_v, sq3_a, ms3_v, pw3_p, h3_a, tr_mm, rT_v, rT_a = (
        sem(x) for x in ("xo_mm", "x3_v", "sq3_a", "ms3_v", "pw3_p", "h3_a", "tr_mm", "rT_v", "rT_a"))
    rt_mm, top_v, eg_a, mask_v, rk_mm, slot_v, scat = (
        sem(x) for x in ("rt_mm", "top_v", "eg_a", "mask_v", "rk_mm", "slot_v", "scat"))
    x3_out, h3_out = sem("x3_out"), sem("h3_out")

    def after(eng, what, t):
        if not (isinstance(t, int) and t == 0):
            eng.wait_ge(what, t)

    def run(eng, steps):
        def body(t, t1, nw):
            if "start" in steps:
                steps["start"](t, t1)
            for name, h in ORDER:
                if name not in steps:
                    continue
                if h >= 0:
                    steps[name](h, t, t1, nw)
                elif not (isinstance(t, int) and t == 0):
                    steps[name](t)
        for t in range(PEELED):
            body(t, t + 1, t + 1)
        with eng.Fori(PEELED, TILES) as t:
            body(eng.snap(t), eng.snap(t + 1), BAND_TILES)
        for name, h in ORDER:
            if h < 0 and name in steps:
                steps[name](TILES)

    with nc.Block() as block:

        @block.sync
        def _(sp):
            sp.dma_start(w_out[:], d.w_out.rearrange("(k p) n -> p k n", p=P)).then_inc(w_in[0], 16)
            sp.dma_start(w_xq[:], d.w_xq.rearrange("(k p) n -> p k n", p=P)).then_inc(w_in[1], 16)
            sp.dma_start(w_xo[:], d.w_xo.rearrange("(k p) n -> p k n", p=P)).then_inc(w_in[2], 16)

            def project(n):
                after(sp, x2_v, n - 1)
                sp.dma_start(xres[:], d.x[bass.ds((n - 1) * P, P), :]).then_inc(xres_in, 16)

            def project_x(n):
                sp.wait_ge(x3_v, n)
                sp.dma_start(d.out[bass.ds((n - 1) * P, P), :], x2[:]).then_inc(x3_out, 16)

            def turn_r(n):
                sp.wait_ge(h3_a, n)
                sp.dma_start(d.h[bass.ds((n - 1) * P, P), :], hn).then_inc(h3_out, 16)

            run(sp, {"project": project, "project_x": project_x, "turn_r": turn_r})
            sp.wait_ge(x3_out, 16 * TILES)
            sp.wait_ge(h3_out, 16 * TILES)

        @block.gpsimd
        def _(pool):
            pool.dma_start(bias[:], bass.AP(tensor=d.band.tensor, offset=P - 1,
                                            ap=[[HEADS * (WINDOW + P), P], [WINDOW + P, HEADS],
                                                [1, WINDOW]])).then_inc(bias_in, 16)
            pool.dma_start(w_r[:], d.w_router.rearrange("(k p) n -> p k n", p=P)).then_inc(b_small, 16)
            pool.dma_start(b_r[:], d.b_router.rearrange("(a n) -> a n", a=1).to_broadcast([P, E])).then_inc(b_small, 16)
            nc.gpsimd.memset(qz[:], 0.0).then_inc(zeroed, 1)
            nc.gpsimd.memset(half[:], -0.5).then_inc(consts, 1)
            nc.gpsimd.memset(m.seen[:], 0.0).then_inc(consts, 1)
            nc.gpsimd.memset(x2[:], 0.0).then_inc(zeroed, 1)
            nc.gpsimd.iota(eids[:], [[1, E]], base=0, channel_multiplier=0, allow_small_or_imprecise_dtypes=True).then_inc(consts, 1)
            nc.gpsimd.iota(tok[:], [[0, TOPK]], base=0, channel_multiplier=1, allow_small_or_imprecise_dtypes=True).then_inc(consts, 1)
            pool.wait_ge(zeroed, 2)
            for b in range(PAD // P):
                at = slice(SEQ + b * P, SEQ + (b + 1) * P)
                pool.dma_start(d.out[at, :], x2[:]).then_inc(pads, 16)
                pool.dma_start(d.h[at, :], x2[:]).then_inc(pads, 16)
            def turn_a(n):
                after(pool, pr_mm, n - 1)
                pool.sem_inc(met_p, 1)
                nc.gpsimd.tensor_copy(ybs[:], m.ybT[:, :, bass.ds((n - 1) * P, P)]).then_inc(yb_p, 1)
                pool.wait_ge(msa_v, n)
                nc.gpsimd.tensor_tensor(pw[:, 0:1], ssa, half[:, 0:1], ALU.pow).then_inc(pwa_p, 1)

            def turn_h(n):
                pool.wait_ge(ms2_v, n)
                nc.gpsimd.tensor_tensor(pw[:, 1:2], ssx, half[:, 0:1], ALU.pow).then_inc(pw2_p, 1)

            def turn_q(n):
                pool.wait_ge(msq_v, n)
                nc.gpsimd.tensor_tensor(pw[:, 4:8], ssq, half[:], ALU.pow).then_inc(pwq_p, 1)

            def turn_r(n):
                pool.wait_ge(ms3_v, n)
                nc.gpsimd.tensor_tensor(pw[:, 2:3], ssr, half[:, 0:1], ALU.pow).then_inc(pw3_p, 1)

            def rank(n):
                pool.wait_ge(slot_v, n)
                pool.sem_inc(met_p, 1)
                for k in range(TOPK):
                    pool.indirect_dma_start(d.slots[:], bass.IndirectOffsetOnAxis(ap=sloti[:, k:k + 1], axis=0),
                                            pay[:, k, :], None).then_inc(scat, 16)

            run(pool, {"turn_a": turn_a, "turn_h": turn_h, "turn_q": turn_q, "turn_r": turn_r,
                       "rank": rank})
            pool.wait_ge(scat, 16 * TOPK * TILES)
            pool.wait_ge(pads, 16 * 2 * (PAD // P))

        @block.tensor
        def _(pe):
            def scores(h, t, t1, nw):
                pe.wait_ge(qz_v, t1)
                if h:
                    pe.wait_ge(sc_v[h - 1], t1)
                else:
                    after(pe, sc_v[HEADS - 1], t)
                for a, b in spans(0, nw * P):
                    key = (t - (nw - 1)) * P + a
                    last = nc.tensor.matmul(ps[:, a:b], qz[:, h, :], m.kT[:, h // 2, bass.ds(key, b - a)],
                                            start=True, stop=True)
                last.then_inc(sc_mm[h], 1)

            def turn_p(h, t, t1, nw):
                pe.wait_ge(ex_a[h], t1)
                if h:
                    pe.wait_ge(o_v[h - 1], t1)
                else:
                    after(pe, o_v[HEADS - 1], t)
                for j in range(nw):
                    last = nc.tensor.transpose(ptp[:, j * P:(j + 1) * P], p[h % 2][:, j * P:(j + 1) * P], m.ident[:])
                last.then_inc(at_mm[h], 1)

            def values(h, t, t1, nw):
                pe.wait_ge(pt_a[h], t1)
                for j in range(nw):
                    last = nc.tensor.matmul(po, pt[h % 2][:, j * P:(j + 1) * P],
                                            m.v[:, t - (nw - 1) + j, (h // 2) * P:(h // 2 + 1) * P],
                                            start=(j == 0), stop=(j == nw - 1))
                last.then_inc(av_mm[h], 1)

            def turn_a(n):
                pe.wait_ge(ya_v, n)
                for k in range(CS):
                    last = nc.tensor.transpose(py0[:, k * P:(k + 1) * P], o[:, k * P:(k + 1) * P], m.ident[:])
                last.then_inc(ta_mm, 1)

            def project(n):
                pe.wait_ge(yaT_v, n)
                pe.wait_ge(yb_p, n)
                pe.wait_ge(w_in[0], 16)
                after(pe, slot_v, n - 1)
                for c in range(2):
                    for k in range(KD):
                        lhs = yaT[:, k, :] if k < CS else ybs[:, k - CS, :]
                        last = nc.tensor.matmul(px0[:, c * 512:(c + 1) * 512], lhs, w_out[:, k, c * 512:(c + 1) * 512],
                                                start=(k == 0), stop=(k == KD - 1))
                last.then_inc(pr_mm, 1)

            def turn_h(n):
                pe.wait_ge(hn_a, n)
                for k in range(KD):
                    last = nc.tensor.transpose(py0[:, k * P:(k + 1) * P], hn[:, k * P:(k + 1) * P], m.ident[:])
                last.then_inc(th_mm, 1)

            def query(n):
                pe.wait_ge(hT_v, n)
                pe.wait_ge(hT_a, n)
                pe.wait_ge(w_in[1], 16)
                for k in range(KD):
                    last = nc.tensor.matmul(px0[:, 0:D_X], hT[:, k, :], w_xq[:, k, :], start=(k == 0), stop=(k == KD - 1))
                last.then_inc(xq_mm, 1)

            def turn_q(n):
                pe.wait_ge(qxn_v, n)
                for h in range(XH):
                    last = nc.tensor.transpose(py0[:, h * P:(h + 1) * P], qxn[:, h * XD:(h + 1) * XD], m.ident[:])
                last.then_inc(tq_mm, 1)

            def scores_x(n):
                pe.wait_ge(qxT_a, n)
                for h in range(XH):
                    last = nc.tensor.matmul(px0[:, h * MEM:(h + 1) * MEM], qxT[:, h, :], m.kxT[:, h, :],
                                            start=True, stop=True)
                last.then_inc(sx_mm, 1)

            def turn_x(n):
                pe.wait_ge(px_v, n)
                for j in range(XH * MT):
                    last = nc.tensor.transpose(py0[:, j * P:(j + 1) * P],
                                               px[:, j // MT, (j % MT) * P:(j % MT + 1) * P], m.ident[:])
                last.then_inc(tx_mm, 1)

            def values_x(n):
                pe.wait_ge(pxT_v, n)
                pe.wait_ge(pxT_a, n)
                for h in range(XH):
                    for b in range(MT):
                        last = nc.tensor.matmul(px0[:, h * P:(h + 1) * P], m.vx[:, b, h * XD:(h + 1) * XD],
                                                pxT[:, h * MT + b, :], start=(b == 0), stop=(b == MT - 1))
                last.then_inc(vx_mm, 1)

            def project_x(n):
                pe.wait_ge(oxT_a, n)
                pe.wait_ge(w_in[2], 16)
                for c in range(2):
                    for k in range(XH):
                        last = nc.tensor.matmul(py0[:, c * 512:(c + 1) * 512], oxT[:, k, :],
                                                w_xo[:, k, c * 512:(c + 1) * 512], start=(k == 0), stop=(k == XH - 1))
                last.then_inc(xo_mm, 1)

            def turn_r(n):
                pe.wait_ge(h3_a, n)
                for k in range(KD):
                    last = nc.tensor.transpose(px0[:, k * P:(k + 1) * P], hn[:, k * P:(k + 1) * P], m.ident[:])
                last.then_inc(tr_mm, 1)

            def route(n):
                pe.wait_ge(rT_v, n)
                pe.wait_ge(rT_a, n)
                pe.wait_ge(b_small, 32)
                for k in range(KD):
                    last = nc.tensor.matmul(py0[:, 0:E], hT[:, k, :], w_r[:, k, :], start=(k == 0), stop=(k == KD - 1))
                last.then_inc(rt_mm, 1)

            def rank(n):
                pe.wait_ge(mask_v, n)
                nc.tensor.matmul(px0[:, 0:E], m.before[:], mask[:], start=True, stop=False)
                nc.tensor.matmul(px0[:, 0:E], m.ones[:], m.seen[:], start=False, stop=True).then_inc(rk_mm, 1)

            pe.wait_ge(consts, 4)
            run(pe, {"scores": scores, "turn_p": turn_p, "values": values, "turn_a": turn_a, "project": project,
                     "turn_h": turn_h, "query": query, "turn_q": turn_q, "scores_x": scores_x, "turn_x": turn_x,
                     "values_x": values_x, "project_x": project_x, "turn_r": turn_r, "route": route, "rank": rank})

        @block.scalar
        def _(act):
            def scores(h, t, t1, nw):
                act.wait_ge(sc_v[h], t1)
                pb = p[h % 2][:, 0:nw * P]
                nc.scalar.activation(pb, pb, ACT.Exp, bias=nm[:, h:h + 1], accum_out=rs[:, h:h + 1]).then_inc(ex_a[h], 1)

            def turn_p(h, t, t1, nw):
                act.wait_ge(at_mm[h], t1)
                if h >= 2:
                    act.wait_ge(av_mm[h - 2], t1)
                else:
                    after(act, av_mm[HEADS - 2 + h], t)
                nc.scalar.copy(pt[h % 2][:, 0:nw * P], ptp[:, 0:nw * P]).then_inc(pt_a[h], 1)

            def turn_a(n):
                act.wait_ge(o_v[HEADS - 1], n)
                nc.scalar.activation(sqx[:, 0:D_ATT], o[:], ACT.Square, accum_out=ssa).then_inc(sqa_a, 1)

            def turn_h(n):
                act.wait_ge(x2_v, n)
                nc.scalar.activation(sqx[:], x2[:], ACT.Square, accum_out=ssx).then_inc(sq2_a, 1)
                act.wait_ge(pw2_p, n)
                if not (isinstance(n, int) and n == 1):
                    act.wait_ge(h3_out, 16 * (n - 1))
                nc.scalar.activation(hn, x2[:], ACT.Copy, scale=pw[:, 1:2]).then_inc(hn_a, 1)
                act.wait_ge(th_mm, n)
                for k in range(KD // 2, KD):
                    last = nc.scalar.activation(hT[:, k, :], py0[:, k * P:(k + 1) * P], ACT.Copy, scale=m.g_x[:, k:k + 1])
                last.then_inc(hT_a, 1)

            def query(n):
                act.wait_ge(xq_mm, n)
                nc.scalar.activation(sqx[:, 0:D_X], px0[:, 0:D_X], ACT.Square).then_inc(sqq_a, 1)

            def turn_q(n):
                act.wait_ge(tq_mm, n)
                nc.scalar.activation(qxT[:], py0[:, 0:D_X].rearrange("p (h t) -> p h t", h=XH), ACT.Copy,
                                     scale=m.g_xq[:]).then_inc(qxT_a, 1)

            def scores_x(n):
                act.wait_ge(mxx_v, n)
                for h in range(XH):
                    last = nc.scalar.activation(px[:, h, :], px0[:, h * MEM:(h + 1) * MEM], ACT.Exp,
                                                bias=nmx[:, h:h + 1], accum_out=rsx[:, h:h + 1])
                last.then_inc(exx_a, 1)

            def turn_x(n):
                act.wait_ge(tx_mm, n)
                nc.scalar.copy(pxT[:, 4:8, :], py0[:, 512:1024].rearrange("p (j t) -> p j t", j=4)).then_inc(pxT_a, 1)

            def values_x(n):
                act.wait_ge(vx_mm, n)
                nc.scalar.copy(oxT[:], px0[:, 0:D_X].rearrange("p (h t) -> p h t", h=XH)).then_inc(oxT_a, 1)

            def turn_r(n):
                act.wait_ge(x3_v, n)
                nc.scalar.activation(sqx[:], x2[:], ACT.Square, accum_out=ssr).then_inc(sq3_a, 1)
                act.wait_ge(pw3_p, n)
                nc.scalar.activation(hn, x2[:], ACT.Copy, scale=pw[:, 2:3]).then_inc(h3_a, 1)
                act.wait_ge(tr_mm, n)
                for k in range(KD // 2, KD):
                    last = nc.scalar.activation(hT[:, k, :], px0[:, k * P:(k + 1) * P], ACT.Copy, scale=m.g_ffn[:, k:k + 1])
                last.then_inc(rT_a, 1)

            def route(n):
                act.wait_ge(top_v, n)
                nc.scalar.activation(gsum[:, 4:8], top[:, 0:TOPK], ACT.Exp, bias=gsum[:, 0:1],
                                     accum_out=gsum[:, 1:2]).then_inc(eg_a, 1)

            run(act, {"scores": scores, "turn_p": turn_p, "turn_a": turn_a, "turn_h": turn_h, "query": query,
                      "turn_q": turn_q, "scores_x": scores_x, "turn_x": turn_x, "values_x": values_x,
                      "turn_r": turn_r, "route": route})

        @block.vector
        def _(dve):
            def mean(ap, n):
                return nc.vector.tensor_scalar(ap, ap, 1.0 / n, EPS, ALU.mult, ALU.add)

            def start(t, t1):
                after(dve, sc_mm[HEADS - 1], t)
                for odd in range(2):
                    at = slice(odd * HEAD, (odd + 1) * HEAD)
                    last = nc.vector.tensor_copy(qz[at].rearrange("p (j two) t -> p j two t", two=2)[:, :, odd, :],
                                                 m.qT[at, :, bass.ds(t * P, P)])
                last.then_inc(qz_v, 1)

            def scores(h, t, t1, nw):
                dve.wait_ge(sc_mm[h], t1)
                if h >= 2:
                    dve.wait_ge(at_mm[h - 2], t1)
                else:
                    after(dve, at_mm[HEADS - 2 + h], t)
                dve.sem_inc(met_v, 1)
                nc.vector.tensor_tensor_reduce(p[h % 2][:, 0:nw * P], ps[:, 0:nw * P],
                                               bias[:, h, WINDOW - nw * P:], 1.0, -3e38, ALU.add, ALU.max, nm[:, h:h + 1])
                dve.drain()
                nc.vector.tensor_scalar(nm[:, h:h + 1], nm[:, h:h + 1], -1.0, None, ALU.mult).then_inc(sc_v[h], 1)

            def values(h, t, t1, nw):
                dve.wait_ge(ex_a[h], t1)
                nc.vector.reciprocal(rs[:, h:h + 1], rs[:, h:h + 1])
                dve.drain()
                dve.wait_ge(av_mm[h], t1)
                if h == 0:
                    after(dve, ta_mm, t)
                nc.vector.tensor_scalar(o[:, h * HEAD:(h + 1) * HEAD], po[:, (h % 2) * HEAD:(h % 2 + 1) * HEAD],
                                        rs[:, h:h + 1], None, ALU.mult).then_inc(o_v[h], 1)

            def turn_a(n):
                dve.wait_ge(sqa_a, n)
                mean(ssa, D_ATT).then_inc(msa_v, 1)
                dve.wait_ge(pwa_p, n)
                nc.vector.tensor_scalar(o[:], o[:], pw[:, 0:1], None, ALU.mult).then_inc(ya_v, 1)
                dve.wait_ge(ta_mm, n)
                for k in range(CS):
                    last = nc.vector.tensor_scalar(yaT[:, k, :], py0[:, k * P:(k + 1) * P], m.g_a[:, k:k + 1], None, ALU.mult)
                last.then_inc(yaT_v, 1)

            def project(n):
                dve.wait_ge(pr_mm, n)
                dve.wait_ge(xres_in, 16 * n)
                if isinstance(n, int) and n == 1:
                    dve.wait_ge(pads, 16 * 2 * (PAD // P))
                else:
                    dve.wait_ge(x3_out, 16 * (n - 1))
                nc.vector.tensor_tensor(x2[:], px0[:], xres[:], ALU.add).then_inc(x2_v, 1)

            def turn_h(n):
                dve.wait_ge(sq2_a, n)
                mean(ssx, D).then_inc(ms2_v, 1)
                dve.wait_ge(th_mm, n)
                for k in range(KD // 2):
                    last = nc.vector.tensor_scalar(hT[:, k, :], py0[:, k * P:(k + 1) * P], m.g_x[:, k:k + 1], None, ALU.mult)
                last.then_inc(hT_v, 1)

            def query(n):
                dve.wait_ge(sqq_a, n)
                nc.vector.reduce_sum(ssq, sqx[:, 0:D_X].rearrange("p (h e) -> p h e", h=XH), AX_X)
                dve.drain()
                mean(ssq, XD).then_inc(msq_v, 1)

            def turn_q(n):
                dve.wait_ge(pwq_p, n)
                nc.vector.tensor_tensor(qxn[:].rearrange("p (h e) -> p h e", h=XH),
                                        px0[:, 0:D_X].rearrange("p (h e) -> p h e", h=XH),
                                        pw[:, 4:8].unsqueeze(2).to_broadcast([P, XH, XD]), ALU.mult).then_inc(qxn_v, 1)

            def scores_x(n):
                dve.wait_ge(sx_mm, n)
                nc.vector.reduce_max(nmx, px0[:].rearrange("p (h k) -> p h k", h=XH), AX_X)
                dve.drain()
                nc.vector.tensor_scalar(nmx, nmx, -1.0, None, ALU.mult).then_inc(mxx_v, 1)
                dve.wait_ge(exx_a, n)
                nc.vector.reciprocal(rsx, rsx)
                dve.drain()
                for h in range(XH):
                    last = nc.vector.tensor_scalar(px[:, h, :], px[:, h, :], rsx[:, h:h + 1], None, ALU.mult)
                last.then_inc(px_v, 1)

            def turn_x(n):
                dve.wait_ge(tx_mm, n)
                nc.vector.tensor_copy(pxT[:, 0:4, :], py0[:, 0:512].rearrange("p (j t) -> p j t", j=4)).then_inc(pxT_v, 1)

            def project_x(n):
                dve.wait_ge(xo_mm, n)
                nc.vector.tensor_tensor(x2[:], py0[:], x2[:], ALU.add).then_inc(x3_v, 1)

            def turn_r(n):
                dve.wait_ge(sq3_a, n)
                mean(ssr, D).then_inc(ms3_v, 1)
                dve.wait_ge(tr_mm, n)
                for k in range(KD // 2):
                    last = nc.vector.tensor_scalar(hT[:, k, :], px0[:, k * P:(k + 1) * P], m.g_ffn[:, k:k + 1], None, ALU.mult)
                last.then_inc(rT_v, 1)

            def route(n):
                dve.wait_ge(rt_mm, n)
                nc.vector.tensor_tensor(lg[:], py0[:, 0:E], b_r[:], ALU.add)
                dve.drain()
                nc.vector.max(top[:], lg[:])
                dve.drain()
                nc.vector.tensor_scalar(gsum[:, 0:1], top[:, 0:1], -1.0, None, ALU.mult).then_inc(top_v, 1)
                nc.vector.max_index(topi[:], top[:], lg[:])
                dve.drain()
                nc.vector.tensor_copy(topf[:], topi[:, 0:TOPK])
                dve.drain()
                nc.vector.tensor_tensor(oneh[:], eids[:].unsqueeze(1).to_broadcast([P, TOPK, E]),
                                        topf[:].unsqueeze(2).to_broadcast([P, TOPK, E]), ALU.is_equal)
                dve.drain()
                nc.vector.reduce_sum(mask[:], oneh[:].rearrange("p k e -> p e k"), AX_X).then_inc(mask_v, 1)

            def rank(n):
                if not (isinstance(n, int) and n == 1):
                    dve.wait_ge(scat, 16 * TOPK * (n - 1))
                nc.vector.tensor_copy(pay[:, :, 0], tok[:])
                dve.wait_ge(eg_a, n)
                nc.vector.reciprocal(gsum[:, 2:3], gsum[:, 1:2])
                dve.drain()
                nc.vector.tensor_scalar(pay[:, :, 1].bitcast(F32), gsum[:, 4:8], gsum[:, 2:3], None, ALU.mult)
                dve.wait_ge(rk_mm, n)
                nc.vector.tensor_tensor(ohp[:], oneh[:], px0[:, 0:E].unsqueeze(1).to_broadcast([P, TOPK, E]), ALU.mult)
                nc.vector.tensor_tensor(m.seen[:], m.seen[:], mask[:], ALU.add)
                dve.drain()
                nc.vector.reduce_sum(slotf[:], ohp[:], AX_X)
                nc.vector.tensor_scalar(tok[:], tok[:], float(P), None, ALU.add)
                dve.drain()
                nc.vector.scalar_tensor_tensor(slotf[:], topf[:], float(SEQ), slotf[:], ALU.mult, ALU.add)
                dve.drain()
                nc.vector.tensor_copy(sloti[:], slotf[:]).then_inc(slot_v, 1)

            dve.wait_ge(bias_in, 16)
            nc.vector.memset(bias[0:CHUNK, :, WINDOW - CHUNK:], NEG)
            nc.vector.memset(bias[CHUNK:P, :, 0:CHUNK], NEG)
            dve.drain()
            dve.wait_ge(zeroed, 2)
            dve.wait_ge(consts, 4)
            dve.wait_ge(b_small, 32)
            run(dve, {"start": start, "scores": scores, "values": values, "turn_a": turn_a, "project": project, "turn_h": turn_h,
                      "query": query, "turn_q": turn_q, "scores_x": scores_x, "turn_x": turn_x,
                      "project_x": project_x, "turn_r": turn_r, "route": route, "rank": rank})


SLOT_COLS = 512
GU_SLOTS = 2 * FF // SLOT_COLS
SLOTS = GU_SLOTS + D // SLOT_COLS
WIDTHS = (128, 160, 192, 224, 256)
FIELDS = 4


def phase_c(nc, m, d, sem, psum):
    s = Map(nc, m.small_end)
    w = [s.put(f"w{i}", [P, KD, SLOT_COLS]) for i in range(SLOTS)]
    xg = s.put("xg", [P, UB, D])
    xT = s.put("xT", [P, KD, UNIT])
    aT = s.put("aT", [P, FS, UNIT])
    yT = s.put("yT", [P, KD, UNIT])
    y = s.put("y", [P, UB, D])
    g = [s.put(f"g{i}", [P, UNIT]) for i in range(2)]
    sg = [s.put(f"sg{i}", [P, UNIT]) for i in range(2)]
    li = [s.put(f"li{i}", [P, UNIT]) for i in range(2)]
    bg = s.put("bg", [P, E * FS])
    bl = s.put("bl", [P, E * FS])
    bd = s.put("bd", [P, E * KD])
    rawg = s.put("rawg", [P, 2, 2 * P])
    rawd = s.put("rawd", [P, 2, P])
    idx = s.put("idx", [P, UB, 2], I32)
    cur = s.put("cur", [P, UB, 2], I32)
    cnt = s.put("cnt", [P, E])
    nun = s.put("nun", [P, E])
    cum = s.put("cum", [P, E])
    one = s.put("one", [P, E])
    le = s.put("le", [P, E])
    tmp = s.put("tmp", [P, E])
    ef = s.put("ef", [P, E])
    row = s.put("row", [P, 1])
    tcol = s.put("tcol", [P, 8])
    tint = s.put("tint", [P, FIELDS], I32)
    nint = s.put("nint", [1, 2], I32)
    tab = s.put("tab", [1, P * FIELDS], I32)
    assert s.at <= nc.sbuf_usable_end, s.at

    gup = psum("c_gu", [P, 4, 512])
    trp = psum("c_tr", [P, 2, 512])
    yp = psum("c_y", [P, 2, 512])

    raw_in, consts, cnt_mm, tab_v, tab_out, tab_in, nint_v = (
        sem(x) for x in ("raw_in", "c_consts", "cnt_mm", "tab_v", "tab_out", "tab_in", "nint_v"))
    braw_mm, bias_v, clear_v = sem("braw_mm"), sem("bias_v"), sem("clear_v")
    w_in = [sem(f"c_w{i}") for i in range(SLOTS)]
    idx_in, cur_p, xg_in = sem("idx_in"), sem("cur_p"), sem("xg_in")
    x_tr, xT_c = [sem(f"x_tr{i}") for i in range(4)], [sem(f"xT_c{i}") for i in range(4)]
    gu_mm, g_v, sg_a, l_v, a_v = ([sem(f"{n}{j}") for j in range(FS)] for n in ("gu_mm", "g_v", "sg_a", "l_v", "a_v"))
    dn_mm, yT_a = ([sem(f"{n}{i}") for i in range(KD)] for n in ("dn_mm", "yT_a"))
    y_tr, y_v = ([sem(f"{n}{i}") for i in range(2 * UB)] for n in ("y_tr", "y_v"))
    scat, met_p = sem("c_scat"), sem("c_met_p")

    def load(eng, col, most):
        return eng.value_load(tab[0:1, bass.ds(col, 1)], min_val=0, max_val=most)

    def n_units(eng):
        eng.wait_ge(tab_in, 16)
        eng.wait_ge(nint_v, 1)
        return eng.value_load(nint[0:1, 0:1], min_val=E, max_val=MAX_UNITS)

    with nc.Block() as block:

        @block.sync
        def _(sp):
            rows = d.b_gate_up.rearrange("e (j c) -> (e j) c", j=FS)
            sp.dma_start(rawg[:], rows.rearrange("(r p) c -> p r c", p=P)).then_inc(raw_in, 16)
            rows = d.b_down.rearrange("e (j c) -> (e j) c", j=KD)
            sp.dma_start(rawd[:], rows.rearrange("(r p) c -> p r c", p=P)).then_inc(raw_in, 16)

            def weights(i, e):
                if i < GU_SLOTS:
                    src = d.w_gate_up[e, :, i * SLOT_COLS:(i + 1) * SLOT_COLS]
                else:
                    src = d.w_down[e, :, (i - GU_SLOTS) * SLOT_COLS:(i - GU_SLOTS + 1) * SLOT_COLS]
                sp.dma_start(w[i][:], src.rearrange("(k p) n -> p k n", p=P)).then_inc(w_in[i], 16)

            for i in range(SLOTS):
                weights(i, 0)
            sp.wait_ge(tab_v, 1)
            sp.dma_start(d.units[:], tint[:]).then_inc(tab_out, 16)
            sp.wait_ge(tab_out, 16)
            sp.dma_start(tab[:], d.units.rearrange("(a u) f -> a (u f)", a=1)).then_inc(tab_in, 16)
            count = n_units(sp)
            with sp.Fori(1, count) as u:
                e = load(sp, u * FIELDS, E - 1)
                before = sp.snap(u)
                for i in range(SLOTS):
                    sp.wait_ge(gu_mm[2 * i + 1] if i < GU_SLOTS else dn_mm[4 * (i - GU_SLOTS) + 3], before)
                    weights(i, e)

        @block.gpsimd
        def _(pool):
            nc.gpsimd.iota(row[:], [[0, 1]], base=0, channel_multiplier=1, allow_small_or_imprecise_dtypes=True).then_inc(consts, 1)
            nc.gpsimd.iota(ef[:], [[1, E]], base=0, channel_multiplier=0, allow_small_or_imprecise_dtypes=True).then_inc(consts, 1)
            nc.gpsimd.memset(one[:], 1.0).then_inc(consts, 1)
            nc.gpsimd.memset(xg[:], 0.0).then_inc(consts, 1)
            pool.wait_ge(consts, 4)
            count = n_units(pool)

            def gather(u, u1):
                first = load(pool, u * FIELDS + 1, E * SEQ - UNIT)
                many = load(pool, u * FIELDS + 2, SEQ)
                pool.dma_start(idx[:], d.slots[bass.ds(first, UNIT), :].rearrange("(b p) c -> p b c", p=P)).then_inc(idx_in, 16)
                pool.wait_ge(idx_in, 16 * u1)
                pool.sem_inc(met_p, 1)
                pool.indirect_dma_start(xg[:, 0, :], None, d.h[:], bass.IndirectOffsetOnAxis(ap=idx[:, 0, 0:1], axis=0)).then_inc(xg_in, 16)
                pool.indirect_dma_start(xg[:, 1, :], None, d.h[:], bass.IndirectOffsetOnAxis(ap=idx[:, 1, 0:1], axis=0)).then_inc(xg_in, 16)

            gather(0, 1)
            with pool.Fori(0, count) as u:
                u1 = pool.snap(u + 1)
                pool.wait_ge(x_tr[3], u1)
                pool.sem_inc(met_p, 1)
                nc.gpsimd.tensor_copy(cur[:], idx[:]).then_inc(cur_p, 1)
                pool.wait_ge(cur_p, u1)
                gather(u1, u + 2)
                pool.wait_ge(y_v[3], u1)
                pool.sem_inc(met_p, 1)
                for b in range(UB):
                    pool.indirect_dma_start(d.out[:], bass.IndirectOffsetOnAxis(ap=cur[:, b, 0:1], axis=0), y[:, b, :],
                                            None, compute_op=ALU.add).then_inc(scat, 16)
                pool.wait_ge(scat, 16 * UB * u1)
            pool.wait_ge(xg_in, 32 * count + 32)

        @block.tensor
        def _(pe):
            pe.wait_ge(raw_in, 32)
            pe.wait_ge(clear_v, 1)
            nc.tensor.matmul(yp[:, 0, 0:E], m.ones[:], m.seen[:], start=True, stop=True).then_inc(cnt_mm, 1)
            for r in range(2):
                nc.tensor.transpose(gup[:, 0, r * P:(r + 1) * P], rawg[:, r, 0:2 * P:2], m.ident[:])
                nc.tensor.transpose(gup[:, 1, r * P:(r + 1) * P], rawg[:, r, 1:2 * P:2], m.ident[:])
                last = nc.tensor.transpose(gup[:, 2, r * P:(r + 1) * P], rawd[:, r, :], m.ident[:])
            last.then_inc(braw_mm, 1)
            pe.wait_ge(bias_v, 1)
            count = n_units(pe)

            def turn_x(u1, first=False):
                pe.wait_ge(xg_in, 32 * u1)
                for q in range(4):
                    b, k0 = q // 2, (q % 2) * 4
                    if q >= 2:
                        pe.wait_ge(xT_c[q - 2], u1)
                    elif not first:
                        pe.wait_ge(xT_c[q + 2], u1 - 1)
                    for k in range(4):
                        last = nc.tensor.transpose(trp[:, q % 2, k * P:(k + 1) * P],
                                                   xg[:, b, (k0 + k) * P:(k0 + k + 1) * P], m.ident[:])
                    last.then_inc(x_tr[q], 1)

            def gate_up(n, u1, w1):
                for j in range(FS):
                    i, c = j * 2 * P // SLOT_COLS, j * 2 * P % SLOT_COLS
                    if c == 0:
                        pe.wait_ge(w_in[i], w1)
                    if j >= 4:
                        pe.wait_ge(l_v[j - 4], u1)
                    for half in range(2):
                        for k in range(KD):
                            last = nc.tensor.matmul(gup[:, j % 4, half * UNIT:half * UNIT + n],
                                                    w[i][:, k, c + half:c + 2 * P:2], xT[:, k, 0:n],
                                                    start=(k == 0), stop=(k == KD - 1))
                    last.then_inc(gu_mm[j], 1)

            def down(n, u1, w1):
                for i in range(KD):
                    s_, c = GU_SLOTS + i * P // SLOT_COLS, i * P % SLOT_COLS
                    if c == 0:
                        pe.wait_ge(w_in[s_], w1)
                    if i == 0:
                        pe.wait_ge(a_v[FS - 1], u1)
                    if i < 4:
                        pe.wait_ge(l_v[4 + i], u1)
                    else:
                        pe.wait_ge(yT_a[i - 4], u1)
                    for k in range(FS):
                        last = nc.tensor.matmul(gup[:, i % 4, 0:n], w[s_][:, k, c:c + P], aT[:, k, 0:n],
                                                start=(k == 0), stop=(k == FS - 1))
                    last.then_inc(dn_mm[i], 1)

            turn_x(1, True)
            with pe.Fori(0, count) as u:
                u1 = pe.snap(u + 1)
                w1 = pe.snap(16 * u + 16)
                width = load(pe, u * FIELDS + 3, len(WIDTHS) - 1)
                for q in range(4):
                    pe.wait_ge(xT_c[q], u1)
                for v, n in enumerate(WIDTHS):
                    with pe.If(width == v):
                        gate_up(n, u1, w1)
                turn_x(u + 2)
                for v, n in enumerate(WIDTHS):
                    with pe.If(width == v):
                        down(n, u1, w1)
                for q in range(2 * UB):
                    b, i0 = q // 2, (q % 2) * 4
                    pe.wait_ge(yT_a[i0 + 3], u1)
                    if q >= 2:
                        pe.wait_ge(y_v[q - 2], u1)
                    for i in range(4):
                        last = nc.tensor.transpose(yp[:, q % 2, i * P:(i + 1) * P],
                                                   yT[:, i0 + i, b * P:(b + 1) * P], m.ident[:])
                    last.then_inc(y_tr[q], 1)

        @block.scalar
        def _(act):
            count = n_units(act)

            def copy_x(u1):
                for q in (1, 3):
                    act.wait_ge(x_tr[q], u1)
                    for k in range(4):
                        last = nc.scalar.activation(xT[:, 4 + k, (q // 2) * P:(q // 2 + 1) * P], trp[:, 1, k * P:(k + 1) * P],
                                                    ACT.Copy, scale=m.g_ffn[:, 4 + k:5 + k])
                    last.then_inc(xT_c[q], 1)

            copy_x(1)
            with act.Fori(0, count) as u:
                u1 = act.snap(u + 1)
                e = load(act, u * FIELDS, E - 1)
                for j in range(FS):
                    act.wait_ge(g_v[j], u1)
                    nc.scalar.activation(sg[j % 2][:], g[j % 2][:], ACT.Sigmoid, scale=ALPHA).then_inc(sg_a[j], 1)
                copy_x(u + 2)
                for i in range(KD):
                    act.wait_ge(dn_mm[i], u1)
                    nc.scalar.activation(yT[:, i, :], gup[:, i % 4, 0:UNIT], ACT.Identity,
                                         bias=bd[:, bass.ds(e * KD + i, 1)]).then_inc(yT_a[i], 1)

        @block.vector
        def _(dve):
            nc.vector.memset(gup[:], 0.0).then_inc(clear_v, 1)
            dve.wait_ge(cnt_mm, 1)
            dve.wait_ge(consts, 4)
            nc.vector.tensor_copy(cnt[:], yp[:, 0, 0:E])
            dve.drain()
            nc.vector.tensor_scalar(nun[:], cnt[:], float(UNIT), 1.0, ALU.is_gt, ALU.add)
            dve.drain()
            for r in range(2, SEQ // UNIT):
                nc.vector.scalar_tensor_tensor(nun[:], cnt[:], float(r * UNIT), nun[:], ALU.is_gt, ALU.add)
                dve.drain()
            nc.vector.tensor_tensor_scan(cum[:], one[:], nun[:], 0.0, ALU.mult, ALU.add)
            dve.drain()
            expert, before, many, first, width = (tcol[:, i:i + 1] for i in range(5))
            nc.vector.tensor_scalar(le[:], cum[:], row[:], None, ALU.is_le)
            dve.drain()
            nc.vector.reduce_sum(expert, le[:], AX_X)
            nc.vector.tensor_tensor(tmp[:], le[:], nun[:], ALU.mult)
            dve.drain()
            nc.vector.reduce_sum(before, tmp[:], AX_X)
            dve.drain()
            nc.vector.tensor_tensor(before, row[:], before, ALU.subtract)
            nc.vector.tensor_scalar(le[:], ef[:], expert, None, ALU.is_equal)
            dve.drain()
            nc.vector.tensor_tensor(tmp[:], le[:], cnt[:], ALU.mult)
            nc.vector.tensor_scalar(expert, expert, float(E - 1), None, ALU.min)
            nc.vector.tensor_scalar(before, before, float(UNIT), 0.0, ALU.mult, ALU.max)
            dve.drain()
            nc.vector.reduce_sum(many, tmp[:], AX_X)
            nc.vector.scalar_tensor_tensor(first, expert, float(SEQ), before, ALU.mult, ALU.add)
            dve.drain()
            nc.vector.tensor_tensor(many, many, before, ALU.subtract)
            nc.vector.tensor_scalar(first, first, float(E * SEQ - UNIT), None, ALU.min)
            dve.drain()
            nc.vector.tensor_scalar(many, many, 0.0, float(SEQ), ALU.max, ALU.min)
            dve.drain()
            nc.vector.tensor_scalar(width, many, float(WIDTHS[0]), None, ALU.is_gt)
            dve.drain()
            for n in WIDTHS[1:-1]:
                nc.vector.scalar_tensor_tensor(width, many, float(n), width, ALU.is_gt, ALU.add)
                dve.drain()
            for i, col in enumerate((expert, first, many, width)):
                nc.vector.tensor_copy(tint[:, i:i + 1], col)
            dve.drain()
            nc.vector.tensor_copy(nint[0:1, 0:1], cum[0:1, E - 1:E]).then_inc(nint_v, 1)
            dve.sem_inc(tab_v, 1)
            dve.wait_ge(braw_mm, 1)
            nc.vector.tensor_copy(bg[:], gup[:, 0, 0:2 * P])
            nc.vector.tensor_scalar(bl[:], gup[:, 1, 0:2 * P], 1.0, None, ALU.add)
            nc.vector.tensor_copy(bd[:], gup[:, 2, 0:2 * P]).then_inc(bias_v, 1)
            dve.drain()
            count = n_units(dve)

            def copy_x(u1):
                for q in (0, 2):
                    dve.wait_ge(x_tr[q], u1)
                    for k in range(4):
                        last = nc.vector.tensor_scalar(xT[:, k, (q // 2) * P:(q // 2 + 1) * P], trp[:, 0, k * P:(k + 1) * P],
                                                       m.g_ffn[:, k:k + 1], None, ALU.mult)
                    last.then_inc(xT_c[q], 1)

            copy_x(1)
            with dve.Fori(0, count) as u:
                u1 = dve.snap(u + 1)
                e = load(dve, u * FIELDS, E - 1)
                for j in range(FS):
                    dve.wait_ge(gu_mm[j], u1)
                    nc.vector.tensor_scalar(g[j % 2][:], gup[:, j % 4, 0:UNIT], bg[:, bass.ds(e * FS + j, 1)], LIMIT,
                                            ALU.add, ALU.min).then_inc(g_v[j], 1)
                    nc.vector.tensor_scalar(li[j % 2][:], gup[:, j % 4, UNIT:2 * UNIT], bl[:, bass.ds(e * FS + j, 1)],
                                            LIMIT + 1.0, ALU.add, ALU.min).then_inc(l_v[j], 1)
                    dve.drain()
                    nc.vector.scalar_tensor_tensor(li[j % 2][:], li[j % 2][:], 1.0 - LIMIT, g[j % 2][:], ALU.max, ALU.mult)
                    dve.drain()
                    dve.wait_ge(sg_a[j], u1)
                    nc.vector.tensor_tensor(aT[:, j, :], li[j % 2][:], sg[j % 2][:], ALU.mult).then_inc(a_v[j], 1)
                copy_x(u + 2)
                dve.wait_ge(cur_p, u1)
                if True:
                    dve.wait_ge(scat, 16 * UB * u)
                for q in range(2 * UB):
                    b, at = q // 2, (q % 2) * 512
                    dve.wait_ge(y_tr[q], u1)
                    nc.vector.tensor_scalar(y[:, b, at:at + 512], yp[:, q % 2, :], cur[:, b, 1:2].bitcast(F32), None,
                                            ALU.mult).then_inc(y_v[q], 1)


def build(nc, d):
    m = lay_out(nc)
    for phase in (phase_a, phase_b, phase_c):
        sems, banks = [], []

        def sem(name):
            sems.append(nc.alloc_semaphore(name))
            return sems[-1]

        with ExitStack() as stack:
            phase(nc, m, d, sem, lambda name, shape: stack.enter_context(nc.psum_tensor(name, shape, F32)))
        nc.all_engine_barrier()
        nc.clear_and_free_semaphores(sems)
        nc.all_engine_barrier()


def kernel(**inputs):
    import concourse.bacc as bacc
    from concourse.bass_utils import run_bass_kernel_spmd

    nc = bacc.Bacc("TRN2", target_bir_lowering=False, num_devices=1)
    d, arrays = Buffers(), {}
    inputs["rel_rev"] = np.asarray(inputs.pop("rel_bias"))[:, :, ::-1]
    for name, value in inputs.items():
        a = np.ascontiguousarray(value)
        arrays["in_" + name] = a
        ap = nc.dram_tensor("in_" + name, a.shape, mybir.dt.from_np(a.dtype), kind="ExternalInput").ap()
        d.__dict__[name] = ap[0]
    d.out = nc.dram_tensor("out_0", (SEQ + PAD, D), F32, kind="ExternalOutput").ap()
    d.h = nc.dram_tensor("h_rows", (SEQ + PAD, D), F32).ap()
    d.slots = nc.dram_tensor("slots", (E * SEQ, 2), I32).ap()
    d.band = nc.dram_tensor("band", (P, HEADS * (WINDOW + P) + 1), F32).ap()
    d.units = nc.dram_tensor("units", (P, FIELDS), I32).ap()
    build(nc, d)
    r = run_bass_kernel_spmd(nc, [arrays], core_ids=[0])
    return r.results[0]["out_0"][:SEQ].reshape(1, SEQ, D)
```

```python
from contextlib import ExitStack

import numpy as np

import concourse.bass as bass
import concourse.mybir as mybir
from concourse.alu_op_type import AluOpType as ALU

ACT = mybir.ActivationFunctionType
F32 = mybir.dt.float32
I32 = mybir.dt.int32
U32 = mybir.dt.uint32
AX_X = mybir.AxisListType.X

P = 128
D = 1024
KD = D // P
SEQ = 1024
TILES = SEQ // P
CHUNK = 64
HEADS, HEAD = 8, 64
PAIRS = HEADS // 2
D_ATT = HEADS * HEAD
CONV = 512
CS = CONV // P
CONV_W = 3
N_IN = 3 * D_ATT + 3 * CONV
BAND_TILES = 5
WINDOW = BAND_TILES * P
MAX_REL = 256
N_REL = 2 * MAX_REL + 1
MEM = 256
MT = MEM // P
XH, XD = 4, 128
D_X = XH * XD
E = 32
TOPK = 4
FF = 1024
FS = FF // P
LIMIT, ALPHA = 7.0, 1.702
EPS = 1e-6
NEG = -1e30
UNIT = 256
UB = UNIT // P
MAX_UNITS = E + SEQ * TOPK // UNIT
PAD = UNIT


class Map:

    def __init__(self, nc, base):
        self.nc, self.at = nc, base

    def put(self, name, shape, dt=F32, at=None):
        size = 4
        for n in shape[1:]:
            size *= n
        size = (size + 31) // 32 * 32
        if at is None:
            at, self.at = self.at, self.at + size
        return self.nc.alloc_sbuf_tensor_at(name, shape, dt, offset=at)


class Buffers:
    pass


def lay_out(nc):
    m = Buffers()
    s = Map(nc, (nc.sbuf_base + 31) // 32 * 32)
    m.ident = s.put("ident", [P, P])
    m.ones = s.put("ones", [P, P])
    m.before = s.put("before", [P, P])
    m.g_mix = s.put("g_mix", [P, KD])
    m.g_x = s.put("g_x", [P, KD])
    m.g_ffn = s.put("g_ffn", [P, KD])
    m.g_mem = s.put("g_mem", [P, KD])
    m.g_q = s.put("g_q", [P, 1])
    m.g_k = s.put("g_k", [P, 1])
    m.g_xq = s.put("g_xq", [P, 1])
    m.g_xk = s.put("g_xk", [P, 1])
    m.g_a = s.put("g_a", [P, CS])
    m.g_b = s.put("g_b", [P, CS])
    m.conv_w = s.put("conv_w_sb", [P, CONV_W, CS])
    m.seen = s.put("seen", [P, E])
    m.small_end = s.at
    m.kxT = s.put("kxT", [P, XH, MEM])
    m.vx = s.put("vx", [P, MT, D_X])
    m.kT = s.put("kT", [P, PAIRS, SEQ])
    m.v = s.put("v", [P, TILES, D_ATT])
    keep = s.at
    m.qT = s.put("qT", [P, PAIRS, SEQ])
    m.ybT = s.put("ybT", [P, CS, SEQ])
    wide = s.at
    m.w_in = s.put("w_in_sb", [P, KD, N_IN])
    m.xin = [s.put(f"xin{b}", [P, D]) for b in range(2)]
    m.hT = [s.put(f"hT{b}", [P, KD, P]) for b in range(2)]
    own = s.at
    m.qn = s.put("qn", [P, D])
    m.u = s.put("u", [P, CS, P + CONV_W - 1])
    m.cg = s.put("cg", [P, 2, P])
    m.ct = s.put("ct", [P, P])
    m.ybr = s.put("ybr", [P, CS, P])
    m.sqb = s.put("sqb", [P, CS, P])
    m.rb = s.put("rb", [P, P])
    m.sqk = s.put("sqk", [P, D])
    m.ss = s.put("ss", [P, 2, 1])
    m.ssqk = s.put("ssqk", [P, 16])
    m.ext = s.put("ext", [HEADS, WINDOW + P])
    m.empty = s.put("empty", [P, E * SEQ // P, 2], I32)
    m.w_xkv = s.put("w_xkv_sb", [P, KD, 2 * D_X], at=keep)
    m.keep, m.wide, m.own, m.s = keep, wide, own, s
    assert s.at <= nc.sbuf_usable_end, (s.at, nc.sbuf_usable_end)
    return m


def phase_a(nc, m, d, sem, psum):
    trp = psum("a_tr", [P, 2, 512])
    qkp = psum("a_qk", [P, 2, 512])
    vp = psum("a_v", [P, 512])
    cvp = psum("a_cv", [P, 2, 512])
    sbp = psum("a_sb", [P, 512])

    consts = sem("a_consts")
    gains = sem("a_gains")
    wxkv_in = sem("a_wxkv_in")
    win_in = sem("a_win_in")
    mem_in = [sem(f"a_mem_in{b}") for b in range(2)]
    m_sq, m_ms, m_h, m_tr = sem("m_sq"), sem("m_ms"), sem("m_h"), sem("m_tr")
    m_hTv, m_hTa = sem("m_hTv"), sem("m_hTa")
    m_kv, m_ksq, m_kms, m_krs, m_kn, m_ktr = (sem("m_" + x) for x in ("kv", "ksq", "kms", "krs", "kn", "ktr"))
    m_kT, m_v = sem("m_kT"), sem("m_v")
    x_in = [sem(f"a_x_in{b}") for b in range(2)]
    x_sq, x_ms, x_h, x_tr = sem("x_sq"), sem("x_ms"), sem("x_h"), sem("x_tr")
    hT_v, hT_a = sem("hT_v"), sem("hT_a")
    cv_mm = [sem(f"cv_mm{c}") for c in range(CS)]
    cg_a = [sem(f"cg_a{c}") for c in range(CS)]
    cv_y = [sem(f"cv_y{c}") for c in range(CS)]
    cv_free = [sem(f"cv_free{c}") for c in range(CS)]
    sqb_a, sb_mm, bms_v, brs_a = sem("sqb_a"), sem("sb_mm"), sem("bms_v"), sem("brs_a")
    qk_mm, qksq_a, qkms_v, qkrs_a, qn_v = (sem(x) for x in ("qk_mm", "qksq_a", "qkms_v", "qkrs_a", "qn_v"))
    v_mm, v_a, qk_tr, qT_v, kT_a = (sem(x) for x in ("v_mm", "v_a", "qk_tr", "qT_v", "kT_a"))
    ext_in, ext_sb, ext_out, slots_out = sem("ext_in"), sem("ext_sb"), sem("ext_out"), sem("slots_out")
    xm = m.hT
    cvv = cvp[:, :, 0:3 * P].rearrange("p b (j t) -> p b j t", j=3)

    def rows(ap, t):
        return ap[bass.ds(t * P, P), :]

    with nc.Block() as block:

        @block.sync
        def _(sp):
            for b in range(2):
                sp.dma_start(m.xin[b][:], d.mem[b * P:(b + 1) * P, :]).then_inc(mem_in[b], 16)
            with nc.allow_non_contiguous_dma(reason="gains, one value to a partition"):
                for tile, src in ((m.g_mem, d.norm_mem_g), (m.g_mix, d.norm_mix_g), (m.g_x, d.norm_xattn_g),
                                  (m.g_ffn, d.norm_ffn_g), (m.g_a, d.out_norm_a_g), (m.g_b, d.out_norm_b_g),
                                  (m.g_xq, d.xq_norm_g), (m.g_xk, d.xk_norm_g)):
                    sp.dma_start(tile[:], src.rearrange("(k p) -> p k", p=P)).then_inc(gains, 16)
                for h in range(2):
                    at = slice(h * HEAD, (h + 1) * HEAD)
                    sp.dma_start(m.g_q[at, :], d.q_norm_g.rearrange("(p a) -> p a", a=1)).then_inc(gains, 16)
                    sp.dma_start(m.g_k[at, :], d.k_norm_g.rearrange("(p a) -> p a", a=1)).then_inc(gains, 16)
                for j in range(CONV_W):
                    sp.dma_start(m.conv_w[:, j, :], d.conv_w[j].rearrange("(c p) -> p c", p=P)).then_inc(gains, 16)
            n_gains = 8 + 4 + CONV_W
            sp.dma_start(m.w_xkv[:], d.w_xkv.rearrange("(k p) n -> p k n", p=P)).then_inc(wxkv_in, 16)
            sp.dma_start(m.w_in[:], d.w_in.rearrange("(k p) n -> p k n", p=P)).then_inc(win_in, 16)
            sp.wait_ge(m_tr, 2)
            for b in range(2):
                sp.dma_start(m.xin[b][:], rows(d.x, b)).then_inc(x_in[b], 16)
            with sp.Fori(0, TILES // 2 - 1) as i:
                for b in range(2):
                    seen = sp.snap(2 * i + (b + 1))
                    sp.wait_ge(x_tr, seen)
                    sp.dma_start(m.xin[b][:], rows(d.x, 2 * i + (b + 2))).then_inc(x_in[b], 16)
            m.n_gains = 16 * n_gains

        @block.gpsimd
        def _(pool):
            nc.gpsimd.memset(m.ident[:], 0.0).then_inc(consts, 1)
            nc.gpsimd.memset(m.ones[:], 1.0).then_inc(consts, 1)
            pool.wait_ge(consts, 2)
            nc.gpsimd.affine_select(out=m.ident[:], in_=m.ident[:], compare_op=ALU.not_equal, fill=1.0, base=0,
                                    pattern=[[-1, P]], channel_multiplier=1).then_inc(consts, 1)
            nc.gpsimd.affine_select(out=m.before[:], in_=m.ones[:], compare_op=ALU.is_gt, fill=0.0, base=0,
                                    pattern=[[1, P]], channel_multiplier=-1).then_inc(consts, 1)
            flat = WINDOW + P - 1 - (MAX_REL + P)
            with nc.allow_non_contiguous_dma(reason="eight short rows"):
                pool.dma_start(m.ext[:, flat:], d.rel_rev[:, 0:WINDOW + P - flat]).then_inc(ext_in, 16)
            nc.gpsimd.memset(m.empty[:], 0).then_inc(ext_sb, 1)
            pool.wait_ge(ext_sb, 1)
            nc.gpsimd.iota(m.empty[:, :, 0], [[0, E * SEQ // P // UNIT], [1, UNIT]], base=SEQ,
                           channel_multiplier=0).then_inc(ext_sb, 1)
            pool.wait_ge(ext_sb, 2)
            pool.dma_start(d.slots.rearrange("(p s) c -> p (s c)", p=P),
                           m.empty[:].rearrange("p s c -> p (s c)")).then_inc(slots_out, 16)
            pool.wait_ge(ext_in, 16)
            nc.gpsimd.tensor_copy(m.ext[:, 0:flat], m.ext[:, flat:flat + 1].to_broadcast([HEADS, flat])).then_inc(ext_sb, 1)
            pool.wait_ge(ext_sb, 3)
            pool.dma_start(bass.AP(tensor=d.band.tensor, offset=0,
                                   ap=[[WINDOW + P, HEADS], [HEADS * (WINDOW + P) + 1, P], [1, WINDOW + P]]),
                           m.ext[:].unsqueeze(1).to_broadcast([HEADS, P, WINDOW + P])).then_inc(ext_out, 16)
            pool.wait_ge(ext_out, 16)
            pool.wait_ge(slots_out, 16)

        @block.tensor
        def _(pe):
            pe.wait_ge(consts, 4)
            for b in range(MT):
                pe.wait_ge(m_h, b + 1)
                if b:
                    pe.wait_ge(m_hTv, b)
                    pe.wait_ge(m_hTa, b)
                for k in range(KD):
                    last = nc.tensor.transpose(trp[:, k // 4, (k % 4) * P:(k % 4 + 1) * P],
                                               m.xin[b][:, k * P:(k + 1) * P], m.ident[:])
                last.then_inc(m_tr, 1)
            pe.wait_ge(wxkv_in, 16)
            for b in range(MT):
                pe.wait_ge(m_hTv, b + 1)
                pe.wait_ge(m_hTa, b + 1)
                if b:
                    pe.wait_ge(m_kn, b)
                    pe.wait_ge(m_v, b)
                for half in range(2):
                    for k in range(KD):
                        last = nc.tensor.matmul(qkp[:, half, :], xm[b][:, k, :],
                                                m.w_xkv[:, k, half * D_X:(half + 1) * D_X],
                                                start=(k == 0), stop=(k == KD - 1))
                last.then_inc(m_kv, 1)
                pe.wait_ge(m_kn, b + 1)
                for h in range(XH):
                    last = nc.tensor.transpose(trp[:, 0, h * P:(h + 1) * P], m.qn[:, h * XD:(h + 1) * XD], m.ident[:])
                last.then_inc(m_ktr, 1)
                pe.wait_ge(m_kT, b + 1)

            def transpose_x(b, t1):
                pe.wait_ge(x_h, t1)
                for k in range(KD):
                    last = nc.tensor.transpose(trp[:, k // 4, (k % 4) * P:(k % 4 + 1) * P],
                                               m.xin[b][:, k * P:(k + 1) * P], m.ident[:])
                last.then_inc(x_tr, 1)

            def convolve(b, c, t1):
                pe.wait_ge(cv_free[(c + 2) % CS], t1)
                for j in range(3):
                    col = 3 * D_ATT + j * CONV + c * P
                    for k in range(KD):
                        last = nc.tensor.matmul(cvv[:, c % 2, j, :], m.w_in[:, k, col:col + P], m.hT[b][:, k, :],
                                                start=(k == 0), stop=(k == KD - 1))
                last.then_inc(cv_mm[c], 1)

            def tile(b, t1, t2, more):
                pe.wait_ge(hT_v, t1)
                pe.wait_ge(hT_a, t1)
                convolve(b, 0, t1)
                convolve(b, 1, t1)
                pe.wait_ge(qT_v, t1)
                pe.wait_ge(kT_a, t1)
                if more:
                    transpose_x(1 - b, t2)
                convolve(b, 2, t1)
                convolve(b, 3, t1)
                for half in range(2):
                    for k in range(KD):
                        last = nc.tensor.matmul(qkp[:, half, :], m.hT[b][:, k, :],
                                                m.w_in[:, k, half * D_ATT:(half + 1) * D_ATT],
                                                start=(k == 0), stop=(k == KD - 1))
                last.then_inc(qk_mm, 1)
                pe.wait_ge(sqb_a, t1)
                for c in range(CS):
                    last = nc.tensor.matmul(sbp[:, 0:P], m.ones[:], m.sqb[:, c, :], start=(c == 0), stop=(c == CS - 1))
                last.then_inc(sb_mm, 1)
                for k in range(KD):
                    last = nc.tensor.matmul(vp[:], m.hT[b][:, k, :], m.w_in[:, k, 2 * D_ATT:3 * D_ATT],
                                            start=(k == 0), stop=(k == KD - 1))
                last.then_inc(v_mm, 1)
                pe.wait_ge(qn_v, t1)
                if more:
                    pe.wait_ge(hT_v, t2)
                    pe.wait_ge(hT_a, t2)
                for j in range(2 * PAIRS):
                    last = nc.tensor.transpose(trp[:, j // PAIRS, (j % PAIRS) * P:(j % PAIRS + 1) * P],
                                               m.qn[:, j * P:(j + 1) * P], m.ident[:])
                last.then_inc(qk_tr, 1)

            transpose_x(0, 1)
            pe.wait_ge(win_in, 16)
            with pe.Fori(0, TILES // 2 - 1) as i:
                count = [pe.snap(2 * i + j) for j in (1, 2, 3)]
                for b in range(2):
                    tile(b, count[b], count[b + 1], True)
            for b in range(2):
                tile(b, TILES - 1 + b, TILES + b, b == 0)

        @block.scalar
        def _(act):
            act.sem_inc(kT_a, 1)
            act.wait_ge(gains, m.n_gains)

            def norm(b, landed, t1, sq, ms, h):
                act.wait_ge(*landed)
                nc.scalar.activation(m.sqk[:], m.xin[b][:], ACT.Square, accum_out=m.ss[:, b, :]).then_inc(sq, 1)
                act.wait_ge(ms, t1)
                nc.scalar.activation(m.ss[:, b, :], m.ss[:, b, :], ACT.Sqrt)
                act.drain()
                nc.scalar.activation(m.xin[b][:], m.xin[b][:], ACT.Copy, scale=m.ss[:, b, :]).then_inc(h, 1)

            def copy_out(b, gain, tr, t1, done):
                act.wait_ge(tr, t1)
                for k in range(KD // 2, KD):
                    last = nc.scalar.activation(m.hT[b][:, k, :], trp[:, 1, (k % 4) * P:(k % 4 + 1) * P], ACT.Copy,
                                                scale=gain[:, k:k + 1])
                last.then_inc(done, 1)

            for b in range(MT):
                norm(b, (mem_in[b], 16), b + 1, m_sq, m_ms, m_h)
                copy_out(b, m.g_mem, m_tr, b + 1, m_hTa)
            for b in range(MT):
                act.wait_ge(m_kv, b + 1)
                nc.scalar.activation(m.sqk[:, 0:D_X], qkp[:, 0, :], ACT.Square).then_inc(m_ksq, 1)
                nc.scalar.copy(m.vx[:, b, :], qkp[:, 1, :]).then_inc(m_v, 1)
                act.wait_ge(m_kms, b + 1)
                nc.scalar.activation(m.ssqk[:, 0:XH], m.ssqk[:, 0:XH], ACT.Sqrt).then_inc(m_krs, 1)
                act.wait_ge(m_ktr, b + 1)
                nc.scalar.activation(m.kxT[:, :, b * P:(b + 1) * P], trp[:, 0, :].rearrange("p (h t) -> p h t", h=XH),
                                     ACT.Copy, scale=m.g_xk[:]).then_inc(m_kT, 1)

            def gate_copy(c, t1):
                act.wait_ge(cv_mm[c], t1)
                nc.scalar.copy(m.cg[:, c % 2, :], cvv[:, c % 2, 1, :]).then_inc(cg_a[c], 1)

            def square(c, t1):
                act.wait_ge(cv_y[c], t1)
                ins = nc.scalar.activation(m.sqb[:, c, :], m.ybr[:, c, :], ACT.Square)
                if c == CS - 1:
                    ins.then_inc(sqb_a, 1)

            def tile(b, t, t1, t2, dma1, more):
                if more:
                    norm(1 - b, (x_in[1 - b], dma1), t2, x_sq, x_ms, x_h)
                gate_copy(0, t1)
                gate_copy(1, t1)
                square(0, t1)
                square(1, t1)
                if more:
                    copy_out(1 - b, m.g_mix, x_tr, t2, hT_a)
                gate_copy(2, t1)
                gate_copy(3, t1)
                square(2, t1)
                square(3, t1)
                act.wait_ge(qk_mm, t1)
                nc.scalar.activation(m.sqk[:], qkp[:], ACT.Square).then_inc(qksq_a, 1)
                act.wait_ge(qkms_v, t1)
                nc.scalar.activation(m.ssqk[:], m.ssqk[:], ACT.Sqrt).then_inc(qkrs_a, 1)
                act.wait_ge(bms_v, t1)
                nc.scalar.activation(m.rb[:], m.rb[:], ACT.Sqrt).then_inc(brs_a, 1)
                act.wait_ge(v_mm, t1)
                nc.scalar.copy(m.v[:, t, :], vp[:]).then_inc(v_a, 1)
                act.wait_ge(qk_tr, t1)
                nc.scalar.activation(m.kT[:, :, bass.ds(t * P, P)], trp[:, 1, :].rearrange("p (h t) -> p h t", h=PAIRS),
                                     ACT.Copy, scale=m.g_k[:]).then_inc(kT_a, 1)

            norm(0, (x_in[0], 16), 1, x_sq, x_ms, x_h)
            copy_out(0, m.g_mix, x_tr, 1, hT_a)
            with act.Fori(0, TILES // 2 - 1) as i:
                count = [act.snap(2 * i + j) for j in (1, 2, 3)]
                dma = [act.snap(16 * i + 16), act.snap(16 * i + 32)]
                for b in range(2):
                    tile(b, 2 * i + b, count[b], count[b + 1], dma[b], True)
            for b in range(2):
                tile(b, TILES - 2 + b, TILES - 1 + b, TILES + b, 16 * (TILES // 2), b == 0)

        @block.vector
        def _(dve):
            nc.vector.memset(m.u[:, :, 0:CONV_W - 1], 0.0).then_inc(qT_v, 1)
            for c in (2, 3):
                dve.sem_inc(cv_free[c], 1)
            dve.wait_ge(gains, m.n_gains)

            def rstd2(ap, n):
                nc.vector.tensor_scalar(ap, ap, 1.0 / n, EPS, ALU.mult, ALU.add)
                dve.drain()
                return nc.vector.reciprocal(ap, ap)

            def norm(b, t1, sq, ms):
                dve.wait_ge(sq, t1)
                rstd2(m.ss[:, b, :], D).then_inc(ms, 1)

            def copy_out(b, gain, tr, t1, done):
                dve.wait_ge(tr, t1)
                for k in range(KD // 2):
                    last = nc.vector.tensor_scalar(m.hT[b][:, k, :], trp[:, 0, k * P:(k + 1) * P], gain[:, k:k + 1],
                                                   None, ALU.mult)
                last.then_inc(done, 1)

            nc.vector.tensor_scalar(m.g_q[:], m.g_q[:], HEAD ** -0.5, None, ALU.mult)
            nc.vector.tensor_scalar(m.g_xq[:], m.g_xq[:], XD ** -0.5, None, ALU.mult)
            for b in range(MT):
                norm(b, b + 1, m_sq, m_ms)
                copy_out(b, m.g_mem, m_tr, b + 1, m_hTv)
            for b in range(MT):
                dve.wait_ge(m_ksq, b + 1)
                nc.vector.reduce_sum(m.ssqk[:, 0:XH], m.sqk[:, 0:D_X].rearrange("p (h e) -> p h e", h=XH), AX_X)
                dve.drain()
                rstd2(m.ssqk[:, 0:XH], XD).then_inc(m_kms, 1)
                dve.wait_ge(m_krs, b + 1)
                nc.vector.tensor_tensor(m.qn[:, 0:D_X].rearrange("p (h e) -> p h e", h=XH),
                                        qkp[:, 0, :].rearrange("p (h e) -> p h e", h=XH),
                                        m.ssqk[:, 0:XH].unsqueeze(2).to_broadcast([P, XH, XD]),
                                        ALU.mult).then_inc(m_kn, 1)

            def conv(c, t1):
                dve.wait_ge(cg_a[c], t1)
                u = m.u[:, c, :]
                nc.vector.tensor_tensor(u[:, 2:P + 2], cvv[:, c % 2, 2, :], m.cg[:, c % 2, :], ALU.mult)
                dve.drain()
                nc.vector.tensor_scalar(m.ct[:], u[:, 2:P + 2], m.conv_w[:, 2, c:c + 1], None, ALU.mult)
                dve.drain()
                nc.vector.scalar_tensor_tensor(m.ct[:], u[:, 1:P + 1], m.conv_w[:, 1, c:c + 1], m.ct[:], ALU.mult, ALU.add)
                dve.drain()
                nc.vector.scalar_tensor_tensor(m.ct[:], u[:, 0:P], m.conv_w[:, 0, c:c + 1], m.ct[:], ALU.mult, ALU.add)
                dve.drain()
                nc.vector.tensor_tensor(m.ybr[:, c, :], cvv[:, c % 2, 0, :], m.ct[:], ALU.mult).then_inc(cv_y[c], 1)
                nc.vector.tensor_copy(u[:, 0:2], u[:, P:P + 2]).then_inc(cv_free[c], 1)
                dve.drain()

            def tile(b, t, t1, t2, more):
                if more:
                    norm(1 - b, t2, x_sq, x_ms)
                conv(0, t1)
                conv(1, t1)
                if more:
                    copy_out(1 - b, m.g_mix, x_tr, t2, hT_v)
                conv(2, t1)
                conv(3, t1)
                dve.wait_ge(qksq_a, t1)
                nc.vector.reduce_sum(m.ssqk[:], m.sqk[:].rearrange("p (h e) -> p h e", h=16), AX_X)
                dve.drain()
                rstd2(m.ssqk[:], HEAD).then_inc(qkms_v, 1)
                dve.wait_ge(sb_mm, t1)
                nc.vector.tensor_scalar(m.rb[:], sbp[:, 0:P], 1.0 / CONV, EPS, ALU.mult, ALU.add)
                dve.drain()
                nc.vector.reciprocal(m.rb[:], m.rb[:]).then_inc(bms_v, 1)
                dve.wait_ge(qkrs_a, t1)
                nc.vector.tensor_tensor(m.qn[:].rearrange("p (h e) -> p h e", h=16),
                                        qkp[:].rearrange("p a (h e) -> p (a h) e", e=HEAD),
                                        m.ssqk[:].unsqueeze(2).to_broadcast([P, 16, HEAD]), ALU.mult).then_inc(qn_v, 1)
                dve.wait_ge(brs_a, t1)
                for c in range(CS):
                    nc.vector.scalar_tensor_tensor(m.ybT[:, c, bass.ds(t * P, P)], m.ybr[:, c, :], m.g_b[:, c:c + 1],
                                                   m.rb[:], ALU.mult, ALU.mult)
                dve.wait_ge(qk_tr, t1)
                nc.vector.tensor_scalar(m.qT[:, :, bass.ds(t * P, P)], trp[:, 0, :].rearrange("p (h t) -> p h t", h=PAIRS),
                                        m.g_q[:], None, ALU.mult).then_inc(qT_v, 1)

            norm(0, 1, x_sq, x_ms)
            copy_out(0, m.g_mix, x_tr, 1, hT_v)
            with dve.Fori(0, TILES // 2 - 1) as i:
                count = [dve.snap(2 * i + j) for j in (1, 2, 3)]
                for b in range(2):
                    tile(b, 2 * i + b, count[b], count[b + 1], True)
            for b in range(2):
                tile(b, TILES - 2 + b, TILES - 1 + b, TILES + b, b == 0)


ORDER = [("stage", 0, 0), ("turn_p", 6, 1), ("rank", 0, 3), ("values", 6, 1),
         ("scores", 0, 0), ("stage", 1, 0), ("project_b", 0, 1), ("turn_q", 0, 2), ("turn_p", 7, 1), ("scores", 1, 0),
         ("values", 7, 1), ("scores_x", 0, 2), ("norm_a", 0, 1), ("turn_p", 0, 0), ("project_b", 1, 1),
         ("scale_a", 0, 1), ("weigh_x", 0, 2), ("values", 0, 0), ("scores", 2, 0), ("turn_a", 0, 1), ("turn_x", 0, 2),
         ("project_a", 0, 1), ("turn_p", 1, 0), ("values_x", 0, 2), ("values", 1, 0), ("scores", 3, 0),
         ("project_a", 1, 1), ("convolved", 0, 0), ("turn_p", 2, 0), ("project_x", 0, 2), ("values", 2, 0),
         ("scores", 4, 0), ("turn_h", 0, 1), ("turn_p", 3, 0), ("project_x", 1, 2), ("values", 3, 0), ("scores", 5, 0),
         ("query", 0, 1), ("turn_p", 4, 0), ("turn_r", 0, 2), ("values", 4, 0), ("scores", 6, 0),
         ("query", 1, 1), ("turn_p", 5, 0), ("route", 0, 2), ("values", 5, 0), ("norm_q", 0, 1), ("scores", 7, 0)]
LAGS = 3
STEADY = BAND_TILES


def spans(start, n):
    out, at = [], start
    while at < start + n:
        to = min(start + n, (at // 512 + 1) * 512)
        out.append((at, to))
        at = to
    return out


class Tile:

    def __init__(self, t, l, n, bands):
        self.t, self.m, self.l, self.n, self.bands = t, t, l, n, bands
        self.first = isinstance(t, int) and t == 0


def phase_b(nc, m, d, sem, psum):
    s = Map(nc, m.wide)
    w_out = s.put("w_out_sb", [P, KD, D])
    w_xq = s.put("w_xq_sb", [P, KD, D_X])
    w_xo = s.put("w_xo_sb", [P, XH, D])
    bias = s.put("bias", [P, HEADS, WINDOW])
    yaT = s.put("yaT", [P, CS, P])
    qxT = s.put("qxT", [P, XH, P])
    oxT = s.put("oxT", [P, XH, P])
    px = s.put("px", [P, XH, MEM])
    sqq = yaT[:].rearrange("p k t -> p (k t)")
    qxn = oxT[:].rearrange("p h t -> p (h t)")
    assert s.at <= m.wide + 4 * KD * N_IN
    s.at = m.own
    qz = s.put("qz", [P, HEADS, P])
    ybs = s.put("ybs", [P, CS, P])
    p = [s.put(f"p{b}", [P, WINDOW]) for b in range(2)]
    pt = s.put("pt", [P, WINDOW])
    o = s.put("o", [P, D_ATT])
    xa = m.xin[0]
    xb = m.xin[1]
    sq = m.hT[0][:].rearrange("p a b -> p (a b)")
    hT = m.hT[1]
    pxT = s.put("pxT", [P, 2 * XH, P])
    w_r = s.put("w_r", [P, KD, E])
    b_r = s.put("b_r", [P, E])
    half = s.put("half", [P, XH])
    small = s.put("small", [P, 32])
    nm, rs = small[:, 0:8], small[:, 8:16]
    ssa, ssx, ssr = small[:, 16:17], small[:, 17:18], small[:, 18:19]
    ssq, nmx, rsx = small[:, 20:24], small[:, 24:28], small[:, 28:32]
    pw = s.put("pw", [P, 8])
    lg = qxn[:, TOPK * E:(TOPK + 1) * E]
    top = s.put("top", [P, 8])
    topi = s.put("topi", [P, 8], U32)
    topf = s.put("topf", [P, TOPK])
    eids = s.put("eids", [P, E])
    oneh = s.put("oneh", [P, TOPK, E])
    ohp = sqq[:, 0:TOPK * E].rearrange("p (k e) -> p k e", k=TOPK)
    mask = s.put("mask", [P, E])
    gsum = s.put("gsum", [P, 8])
    slotf = s.put("slotf", [P, TOPK])
    tok = s.put("tok", [P, TOPK])
    sloti = s.put("sloti", [P, TOPK], I32)
    pay = s.put("pay", [P, TOPK, 2], I32)
    assert s.at <= nc.sbuf_usable_end, s.at

    att = psum("b_att", [P, 2048])
    ps, ptp, po = att[:, 0:WINDOW], att[:, 1024:1024 + WINDOW], att[:, 1024 + WINDOW:1024 + WINDOW + P]
    X = psum("b_x", [P, 1024])
    Y = psum("b_y", [P, 1024])

    w_in = [sem(f"b_w{i}") for i in range(3)]
    bias_in, consts, b_small = sem("b_bias"), sem("b_consts"), sem("b_small")
    zeroed, pads = sem("b_zeroed"), sem("b_pads")
    met_v, met_p = sem("b_met_v"), sem("b_met_p")
    sc_mm, sc_v, ex_a, at_mm, pt_a, av_mm, o_v = (
        [sem(f"{n}{h}") for h in range(HEADS)] for n in ("sc_mm", "sc_v", "ex_a", "at_mm", "pt_a", "av_mm", "o_v"))
    qz_v = [sem(f"qz_v{i}") for i in range(2)]
    yb_p, x_in, x2_in = sem("yb_p"), sem("bx_in"), sem("x2_in")
    sqa_a, msa_v, pwa_p, ya_v, ta_mm, yaT_v = (sem(x) for x in ("sqa_a", "msa_v", "pwa_p", "ya_v", "ta_mm", "yaT_v"))
    pr_mm, x2_v = ([sem(f"{n}{i}") for i in range(2)] for n in ("pr_mm", "x2_v"))
    sq2_a, th_mm, hT_v, hT_a = (sem(x) for x in ("sq2_a", "th_mm", "bhT_v", "bhT_a"))
    xq_mm, sqq_a, msq_v, pwq_p, qxn_v, tq_mm, qxT_a = (
        sem(x) for x in ("xq_mm", "sqq_a", "msq_v", "pwq_p", "qxn_v", "tq_mm", "qxT_a"))
    sx_mm, mxx_v, exx_a, px_v, tx_mm, pxT_v, pxT_a, vx_mm, oxT_a = (
        sem(x) for x in ("sx_mm", "mxx_v", "exx_a", "px_v", "tx_mm", "pxT_v", "pxT_a", "vx_mm", "oxT_a"))
    xo_mm, x3_v = ([sem(f"{n}{i}") for i in range(2)] for n in ("xo_mm", "x3_v"))
    sq3_a, ms3_v, pw3_p, h3_a, tr_mm, rT_v, rT_a = (
        sem(x) for x in ("sq3_a", "ms3_v", "pw3_p", "h3_a", "tr_mm", "rT_v", "rT_a"))
    rt_mm, lg_v, top_v, eg_a, mask_v, rk_mm, slot_v, scat = (
        sem(x) for x in ("rt_mm", "lg_v", "top_v", "eg_a", "mask_v", "rk_mm", "slot_v", "scat"))
    x3_out, h3_out = sem("x3_out"), sem("h3_out")

    def after(eng, what, tile, times=1):
        if not tile.first:
            eng.wait_ge(what, tile.m * times)

    def run(eng, steps):
        def cycle(tiles):
            for name, i, lag in ORDER:
                if name in steps and tiles[lag]:
                    steps[name](i, tiles[lag])

        def at(c):
            return [Tile(t, t - 1 if t > 1 else None, t + 1, min(t + 1, BAND_TILES)) if 0 <= t < TILES else None
                    for t in range(c, c - LAGS - 1, -1)]

        for c in range(STEADY):
            cycle(at(c))
        with eng.Fori(STEADY, TILES) as c:
            v = [eng.snap(c + 1 - k) for k in range(LAGS + 3)]
            cycle([Tile(v[k + 1], v[k + 2], v[k], BAND_TILES) for k in range(LAGS + 1)])
        for c in range(TILES, TILES + LAGS):
            cycle(at(c))

    def rows(tile):
        return bass.ds(tile.t * P, P)

    with nc.Block() as block:

        @block.sync
        def _(sp):
            near = WINDOW - 2 * P
            for at in (slice(near, WINDOW), slice(0, near)):
                src = bass.AP(tensor=d.band.tensor, offset=P - 1 + at.start,
                              ap=[[HEADS * (WINDOW + P), P], [WINDOW + P, HEADS], [1, at.stop - at.start]])
                sp.dma_start(bias[:, :, at], src).then_inc(bias_in, 16)
            sp.dma_start(w_out[:], d.w_out.rearrange("(k p) n -> p k n", p=P)).then_inc(w_in[0], 16)
            sp.dma_start(w_xq[:], d.w_xq.rearrange("(k p) n -> p k n", p=P)).then_inc(w_in[1], 16)
            sp.dma_start(w_xo[:], d.w_xo.rearrange("(k p) n -> p k n", p=P)).then_inc(w_in[2], 16)

            def load_x(i, tile):
                if not tile.first:
                    sp.wait_ge(x2_in, tile.m * 16)
                    sp.wait_ge(th_mm, tile.m)
                    sp.wait_ge(sq2_a, tile.m)
                sp.dma_start(xa[:], d.x[rows(tile), :]).then_inc(x_in, 16)

            def carry(i, tile):
                sp.wait_ge(x2_v[1], tile.n)
                if tile.first:
                    sp.wait_ge(pads, 16 * 2 * (PAD // P))
                else:
                    after(sp, x3_out, tile, 16)
                    after(sp, tr_mm, tile)
                    after(sp, h3_a, tile)
                sp.dma_start(xb[:], xa[:]).then_inc(x2_in, 16)

            def project_x(i, tile):
                if i == 1:
                    sp.wait_ge(x3_v[1], tile.n)
                    sp.dma_start(d.out[rows(tile), :], xb[:]).then_inc(x3_out, 16)

            def turn_r(i, tile):
                sp.wait_ge(h3_a, tile.n)
                sp.dma_start(d.h[rows(tile), :], sq).then_inc(h3_out, 16)

            run(sp, {"project_b": lambda i, tile: load_x(i, tile) if i == 0 else None, "project_x": project_x,
                     "turn_r": turn_r, "query": lambda i, tile: carry(i, tile) if i == 1 else None})
            sp.wait_ge(x3_out, 16 * TILES)
            sp.wait_ge(h3_out, 16 * TILES)

        @block.gpsimd
        def _(pool):
            nc.gpsimd.memset(qz[:], 0.0).then_inc(zeroed, 1)
            nc.gpsimd.memset(half[:], -0.5).then_inc(consts, 1)
            nc.gpsimd.memset(m.seen[:], 0.0).then_inc(consts, 1)
            nc.gpsimd.iota(eids[:], [[1, E]], base=0, channel_multiplier=0, allow_small_or_imprecise_dtypes=True).then_inc(consts, 1)
            nc.gpsimd.iota(tok[:], [[0, TOPK]], base=0, channel_multiplier=1, allow_small_or_imprecise_dtypes=True).then_inc(consts, 1)
            pool.dma_start(w_r[:], d.w_router.rearrange("(k p) n -> p k n", p=P)).then_inc(b_small, 16)
            pool.dma_start(b_r[:], d.b_router.rearrange("(a n) -> a n", a=1).to_broadcast([P, E])).then_inc(b_small, 16)
            nc.gpsimd.memset(xb[:], 0.0).then_inc(zeroed, 1)
            pool.wait_ge(zeroed, 2)
            for b in range(PAD // P):
                at = slice(SEQ + b * P, SEQ + (b + 1) * P)
                pool.dma_start(d.out[at, :], xb[:]).then_inc(pads, 16)
                pool.dma_start(d.h[at, :], xb[:]).then_inc(pads, 16)

            def convolved(i, tile):
                if not tile.first:
                    after(pool, pr_mm[1], tile)
                    pool.sem_inc(met_p, 1)
                nc.gpsimd.tensor_copy(ybs[:], m.ybT[:, :, rows(tile)]).then_inc(yb_p, 1)

            def norm_a(i, tile):
                pool.wait_ge(msa_v, tile.n)
                nc.gpsimd.tensor_tensor(pw[:, 0:1], ssa, half[:, 0:1], ALU.pow).then_inc(pwa_p, 1)

            def norm_q(i, tile):
                pool.wait_ge(msq_v, tile.n)
                nc.gpsimd.tensor_tensor(pw[:, 4:8], ssq, half[:], ALU.pow).then_inc(pwq_p, 1)

            def turn_r(i, tile):
                pool.wait_ge(ms3_v, tile.n)
                nc.gpsimd.tensor_tensor(pw[:, 2:3], ssr, half[:, 0:1], ALU.pow).then_inc(pw3_p, 1)

            def rank(i, tile):
                pool.wait_ge(slot_v, tile.n)
                pool.sem_inc(met_p, 1)
                for k in range(TOPK):
                    pool.indirect_dma_start(d.slots[:], bass.IndirectOffsetOnAxis(ap=sloti[:, k:k + 1], axis=0),
                                            pay[:, k, :], None).then_inc(scat, 16)

            run(pool, {"convolved": convolved, "norm_a": norm_a, "norm_q": norm_q, "turn_r": turn_r, "rank": rank})
            pool.wait_ge(scat, 16 * TOPK * TILES)
            pool.wait_ge(pads, 16 * 2 * (PAD // P))

        @block.tensor
        def _(pe):
            def scores(h, tile):
                if h % 4 == 0:
                    pe.wait_ge(qz_v[h // 4], tile.n)
                if h:
                    pe.wait_ge(sc_v[h - 1], tile.n)
                else:
                    after(pe, sc_v[HEADS - 1], tile)
                for a, b in spans(0, tile.bands * P):
                    key = (tile.t - (tile.bands - 1)) * P + a
                    last = nc.tensor.matmul(ps[:, a:b], qz[:, h, :], m.kT[:, h // 2, bass.ds(key, b - a)],
                                            start=True, stop=True)
                last.then_inc(sc_mm[h], 1)

            def turn_p(h, tile):
                pe.wait_ge(ex_a[h], tile.n)
                if h:
                    pe.wait_ge(o_v[h - 1], tile.n)
                else:
                    after(pe, o_v[HEADS - 1], tile)
                for j in range(tile.bands):
                    last = nc.tensor.transpose(ptp[:, j * P:(j + 1) * P], p[h % 2][:, j * P:(j + 1) * P], m.ident[:])
                last.then_inc(at_mm[h], 1)

            def values(h, tile):
                pe.wait_ge(pt_a[h], tile.n)
                for j in range(tile.bands):
                    last = nc.tensor.matmul(po, pt[:, j * P:(j + 1) * P],
                                            m.v[:, tile.t - (tile.bands - 1) + j, (h // 2) * P:(h // 2 + 1) * P],
                                            start=(j == 0), stop=(j == tile.bands - 1))
                last.then_inc(av_mm[h], 1)

            def turn_a(i, tile):
                pe.wait_ge(ya_v, tile.n)
                for k in range(CS):
                    last = nc.tensor.transpose(ptp[:, k * P:(k + 1) * P], o[:, k * P:(k + 1) * P], m.ident[:])
                last.then_inc(ta_mm, 1)

            def project_b(c, tile):
                pe.wait_ge(yb_p, tile.n)
                pe.wait_ge(w_in[0], 16)
                if c:
                    after(pe, qxT_a, tile)
                for k in range(CS):
                    nc.tensor.matmul(X[:, c * 512:(c + 1) * 512], ybs[:, k, :], w_out[:, CS + k, c * 512:(c + 1) * 512],
                                     start=(k == 0), stop=False)

            def project_a(c, tile):
                pe.wait_ge(yaT_v, tile.n)
                for k in range(CS):
                    last = nc.tensor.matmul(X[:, c * 512:(c + 1) * 512], yaT[:, k, :], w_out[:, k, c * 512:(c + 1) * 512],
                                            start=False, stop=(k == CS - 1))
                last.then_inc(pr_mm[c], 1)

            def turn_h(i, tile):
                pe.wait_ge(x2_v[1], tile.n)
                for k in range(KD):
                    last = nc.tensor.transpose(X[:, k * P:(k + 1) * P], xa[:, k * P:(k + 1) * P], m.ident[:])
                last.then_inc(th_mm, 1)

            def query(i, tile):
                pe.wait_ge(hT_v, tile.n)
                pe.wait_ge(hT_a, tile.n)
                pe.wait_ge(w_in[1], 16)
                for k in range(i * KD // 2, (i + 1) * KD // 2):
                    last = nc.tensor.matmul(X[:, 0:D_X], hT[:, k, :], w_xq[:, k, :], start=(k == 0), stop=(k == KD - 1))
                if i:
                    last.then_inc(xq_mm, 1)

            def turn_q(i, tile):
                pe.wait_ge(qxn_v, tile.n)
                for h in range(XH):
                    last = nc.tensor.transpose(X[:, 512 + h * P:512 + (h + 1) * P], qxn[:, h * XD:(h + 1) * XD], m.ident[:])
                last.then_inc(tq_mm, 1)

            def scores_x(i, tile):
                pe.wait_ge(qxT_a, tile.n)
                after(pe, slot_v, tile)
                for h in range(XH):
                    last = nc.tensor.matmul(Y[:, h * MEM:(h + 1) * MEM], qxT[:, h, :], m.kxT[:, h, :],
                                            start=True, stop=True)
                last.then_inc(sx_mm, 1)

            def turn_x(i, tile):
                pe.wait_ge(px_v, tile.n)
                for j in range(XH * MT):
                    last = nc.tensor.transpose(Y[:, j * P:(j + 1) * P],
                                               px[:, j // MT, (j % MT) * P:(j % MT + 1) * P], m.ident[:])
                last.then_inc(tx_mm, 1)

            def values_x(i, tile):
                pe.wait_ge(pxT_v, tile.n)
                pe.wait_ge(pxT_a, tile.n)
                for h in range(XH):
                    for b in range(MT):
                        last = nc.tensor.matmul(Y[:, h * P:(h + 1) * P], m.vx[:, b, h * XD:(h + 1) * XD],
                                                pxT[:, h * MT + b, :], start=(b == 0), stop=(b == MT - 1))
                last.then_inc(vx_mm, 1)

            def project_x(c, tile):
                pe.wait_ge(oxT_a, tile.n)
                pe.wait_ge(w_in[2], 16)
                for k in range(XH):
                    last = nc.tensor.matmul(Y[:, c * 512:(c + 1) * 512], oxT[:, k, :],
                                            w_xo[:, k, c * 512:(c + 1) * 512], start=(k == 0), stop=(k == XH - 1))
                last.then_inc(xo_mm[c], 1)

            def turn_r(i, tile):
                pe.wait_ge(x3_v[0], tile.n)
                pe.wait_ge(x3_v[1], tile.n)
                for k in range(KD):
                    last = nc.tensor.transpose(Y[:, k * P:(k + 1) * P], xb[:, k * P:(k + 1) * P], m.ident[:])
                last.then_inc(tr_mm, 1)

            def route(i, tile):
                pe.wait_ge(rT_v, tile.n)
                pe.wait_ge(rT_a, tile.n)
                pe.wait_ge(b_small, 32)
                for k in range(KD):
                    last = nc.tensor.matmul(Y[:, 0:E], pxT[:, k, :], w_r[:, k, :], start=(k == 0), stop=(k == KD - 1))
                last.then_inc(rt_mm, 1)

            def rank(i, tile):
                pe.wait_ge(mask_v, tile.n)
                nc.tensor.matmul(Y[:, 512:512 + E], m.before[:], mask[:], start=True, stop=False)
                nc.tensor.matmul(Y[:, 512:512 + E], m.ones[:], m.seen[:], start=False, stop=True).then_inc(rk_mm, 1)

            pe.wait_ge(consts, 4)
            run(pe, {"scores": scores, "turn_p": turn_p, "values": values, "turn_a": turn_a, "project_a": project_a,
                     "project_b": project_b, "turn_h": turn_h, "query": query, "turn_q": turn_q, "scores_x": scores_x,
                     "turn_x": turn_x, "values_x": values_x, "project_x": project_x, "turn_r": turn_r,
                     "route": route, "rank": rank})

        @block.scalar
        def _(act):
            def scores(h, tile):
                act.wait_ge(sc_v[h], tile.n)
                pb = p[h % 2][:, 0:tile.bands * P]
                nc.scalar.activation(pb, pb, ACT.Exp, bias=nm[:, h:h + 1], accum_out=rs[:, h:h + 1]).then_inc(ex_a[h], 1)

            def turn_p(h, tile):
                act.wait_ge(at_mm[h], tile.n)
                if h:
                    act.wait_ge(av_mm[h - 1], tile.n)
                else:
                    after(act, av_mm[HEADS - 1], tile)
                nc.scalar.copy(pt[:, 0:tile.bands * P], ptp[:, 0:tile.bands * P]).then_inc(pt_a[h], 1)

            def norm_a(i, tile):
                act.wait_ge(o_v[HEADS - 1], tile.n)
                if tile.l is not None:
                    act.wait_ge(h3_out, tile.l * 16)
                nc.scalar.activation(sq[:, 0:D_ATT], o[:], ACT.Square, accum_out=ssa).then_inc(sqa_a, 1)

            def turn_h(i, tile):
                act.wait_ge(th_mm, tile.n)
                for k in range(KD // 2, KD):
                    last = nc.scalar.activation(hT[:, k, :], X[:, k * P:(k + 1) * P], ACT.Copy, scale=m.g_x[:, k:k + 1])
                last.then_inc(hT_a, 1)
                nc.scalar.activation(sq, xa[:], ACT.Square, accum_out=ssx).then_inc(sq2_a, 1)

            def query(i, tile):
                if i:
                    act.wait_ge(xq_mm, tile.n)
                    nc.scalar.activation(sqq, X[:, 0:D_X], ACT.Square).then_inc(sqq_a, 1)

            def turn_q(i, tile):
                act.wait_ge(tq_mm, tile.n)
                nc.scalar.activation(qxT[:], X[:, 512:1024].rearrange("p (h t) -> p h t", h=XH), ACT.Copy,
                                     scale=m.g_xq[:]).then_inc(qxT_a, 1)

            def scores_x(i, tile):
                act.wait_ge(mxx_v, tile.n)
                for h in range(XH):
                    last = nc.scalar.activation(px[:, h, :], Y[:, h * MEM:(h + 1) * MEM], ACT.Exp,
                                                bias=nmx[:, h:h + 1], accum_out=rsx[:, h:h + 1])
                last.then_inc(exx_a, 1)

            def turn_x(i, tile):
                act.wait_ge(tx_mm, tile.n)
                nc.scalar.copy(pxT[:, 4:8, :], Y[:, 512:1024].rearrange("p (j t) -> p j t", j=4)).then_inc(pxT_a, 1)

            def values_x(i, tile):
                act.wait_ge(vx_mm, tile.n)
                nc.scalar.copy(oxT[:], Y[:, 0:D_X].rearrange("p (h t) -> p h t", h=XH)).then_inc(oxT_a, 1)

            def turn_r(i, tile):
                act.wait_ge(tr_mm, tile.n)
                for k in range(KD // 2, KD):
                    last = nc.scalar.activation(pxT[:, k, :], Y[:, k * P:(k + 1) * P], ACT.Copy, scale=m.g_ffn[:, k:k + 1])
                last.then_inc(rT_a, 1)
                act.drain()
                nc.scalar.activation(sq, xb[:], ACT.Square, accum_out=ssr).then_inc(sq3_a, 1)
                act.wait_ge(pw3_p, tile.n)
                nc.scalar.activation(sq, xb[:], ACT.Copy, scale=pw[:, 2:3]).then_inc(h3_a, 1)

            def route(i, tile):
                act.wait_ge(top_v, tile.n)
                nc.scalar.activation(gsum[:, 4:8], top[:, 0:TOPK], ACT.Exp, bias=gsum[:, 0:1],
                                     accum_out=gsum[:, 1:2]).then_inc(eg_a, 1)

            run(act, {"scores": scores, "turn_p": turn_p, "norm_a": norm_a, "turn_h": turn_h, "query": query,
                      "turn_q": turn_q, "scores_x": scores_x, "turn_x": turn_x, "values_x": values_x,
                      "turn_r": turn_r, "route": route})

        @block.vector
        def _(dve):
            def mean(ap, n):
                return nc.vector.tensor_scalar(ap, ap, 1.0 / n, EPS, ALU.mult, ALU.add)

            def stage(i, tile):
                after(dve, sc_mm[4 * i + 3], tile)
                for odd in range(2):
                    at = slice(odd * HEAD, (odd + 1) * HEAD)
                    last = nc.vector.tensor_copy(
                        qz[at, 4 * i:4 * i + 4].rearrange("p (j two) t -> p j two t", two=2)[:, :, odd, :],
                        m.qT[at, 2 * i:2 * i + 2, rows(tile)])
                last.then_inc(qz_v[i], 1)

            def scores(h, tile):
                dve.wait_ge(sc_mm[h], tile.n)
                if h >= 2:
                    dve.wait_ge(at_mm[h - 2], tile.n)
                else:
                    after(dve, at_mm[HEADS - 2 + h], tile)
                dve.sem_inc(met_v, 1)
                nc.vector.tensor_tensor_reduce(p[h % 2][:, 0:tile.bands * P], ps[:, 0:tile.bands * P],
                                               bias[:, h, WINDOW - tile.bands * P:], 1.0, -3e38, ALU.add, ALU.max,
                                               nm[:, h:h + 1])
                dve.drain()
                nc.vector.tensor_scalar(nm[:, h:h + 1], nm[:, h:h + 1], -1.0, None, ALU.mult).then_inc(sc_v[h], 1)

            def values(h, tile):
                dve.wait_ge(ex_a[h], tile.n)
                nc.vector.reciprocal(rs[:, h:h + 1], rs[:, h:h + 1])
                dve.drain()
                dve.wait_ge(av_mm[h], tile.n)
                if h == 0:
                    after(dve, ta_mm, tile)
                nc.vector.tensor_scalar(o[:, h * HEAD:(h + 1) * HEAD], po[:, (h % 2) * HEAD:(h % 2 + 1) * HEAD],
                                        rs[:, h:h + 1], None, ALU.mult).then_inc(o_v[h], 1)

            def norm_a(i, tile):
                dve.wait_ge(sqa_a, tile.n)
                mean(ssa, D_ATT).then_inc(msa_v, 1)

            def scale_a(i, tile):
                dve.wait_ge(pwa_p, tile.n)
                nc.vector.tensor_scalar(o[:], o[:], pw[:, 0:1], None, ALU.mult).then_inc(ya_v, 1)

            def turn_a(i, tile):
                dve.wait_ge(ta_mm, tile.n)
                for k in range(CS):
                    last = nc.vector.tensor_scalar(yaT[:, k, :], ptp[:, k * P:(k + 1) * P], m.g_a[:, k:k + 1], None, ALU.mult)
                last.then_inc(yaT_v, 1)

            def project_a(c, tile):
                dve.wait_ge(pr_mm[c], tile.n)
                dve.wait_ge(x_in, tile.n * 16)
                at = slice(c * 512, (c + 1) * 512)
                nc.vector.tensor_tensor(xa[:, at], X[:, at], xa[:, at], ALU.add).then_inc(x2_v[c], 1)

            def turn_h(i, tile):
                dve.wait_ge(th_mm, tile.n)
                for k in range(KD // 2):
                    last = nc.vector.tensor_scalar(hT[:, k, :], X[:, k * P:(k + 1) * P], m.g_x[:, k:k + 1], None, ALU.mult)
                last.then_inc(hT_v, 1)

            def norm_q(i, tile):
                dve.wait_ge(sq2_a, tile.n)
                mean(ssx, D)
                dve.drain()
                nc.vector.tensor_scalar(ssx, ssx, EPS, None, ALU.mult)
                dve.wait_ge(sqq_a, tile.n)
                nc.vector.reduce_sum(ssq, sqq.rearrange("p (h e) -> p h e", h=XH), AX_X)
                dve.drain()
                nc.vector.tensor_scalar(ssq, ssq, 1.0 / XD, ssx, ALU.mult, ALU.add).then_inc(msq_v, 1)
                dve.wait_ge(pwq_p, tile.n)
                nc.vector.tensor_tensor(qxn.rearrange("p (h e) -> p h e", h=XH),
                                        X[:, 0:D_X].rearrange("p (h e) -> p h e", h=XH),
                                        pw[:, 4:8].unsqueeze(2).to_broadcast([P, XH, XD]), ALU.mult).then_inc(qxn_v, 1)

            def scores_x(i, tile):
                dve.wait_ge(sx_mm, tile.n)
                nc.vector.reduce_max(nmx, Y[:].rearrange("p (h k) -> p h k", h=XH), AX_X)
                dve.drain()
                nc.vector.tensor_scalar(nmx, nmx, -1.0, None, ALU.mult).then_inc(mxx_v, 1)

            def weigh_x(i, tile):
                dve.wait_ge(exx_a, tile.n)
                nc.vector.reciprocal(rsx, rsx)
                dve.drain()
                for h in range(XH):
                    last = nc.vector.tensor_scalar(px[:, h, :], px[:, h, :], rsx[:, h:h + 1], None, ALU.mult)
                last.then_inc(px_v, 1)

            def turn_x(i, tile):
                dve.wait_ge(tx_mm, tile.n)
                nc.vector.tensor_copy(pxT[:, 0:4, :], Y[:, 0:512].rearrange("p (j t) -> p j t", j=4)).then_inc(pxT_v, 1)

            def project_x(c, tile):
                dve.wait_ge(xo_mm[c], tile.n)
                dve.wait_ge(x2_in, tile.n * 16)
                at = slice(c * 512, (c + 1) * 512)
                nc.vector.tensor_tensor(xb[:, at], Y[:, at], xb[:, at], ALU.add).then_inc(x3_v[c], 1)

            def turn_r(i, tile):
                dve.wait_ge(tr_mm, tile.n)
                for k in range(KD // 2):
                    last = nc.vector.tensor_scalar(pxT[:, k, :], Y[:, k * P:(k + 1) * P], m.g_ffn[:, k:k + 1], None, ALU.mult)
                last.then_inc(rT_v, 1)
                dve.wait_ge(sq3_a, tile.n)
                mean(ssr, D).then_inc(ms3_v, 1)

            def route(i, tile):
                dve.wait_ge(rt_mm, tile.n)
                dve.wait_ge(pw3_p, tile.n)
                nc.vector.scalar_tensor_tensor(lg, Y[:, 0:E], pw[:, 2:3], b_r[:], ALU.mult, ALU.add)
                dve.drain()
                nc.vector.max(top[:], lg)
                dve.drain()
                nc.vector.tensor_scalar(gsum[:, 0:1], top[:, 0:1], -1.0, None, ALU.mult).then_inc(top_v, 1)
                nc.vector.max_index(topi[:], top[:], lg)
                dve.drain()
                nc.vector.tensor_copy(topf[:], topi[:, 0:TOPK])
                dve.drain()
                nc.vector.tensor_tensor(oneh[:], eids[:].unsqueeze(1).to_broadcast([P, TOPK, E]),
                                        topf[:].unsqueeze(2).to_broadcast([P, TOPK, E]), ALU.is_equal)
                dve.drain()
                nc.vector.reduce_sum(mask[:], oneh[:].rearrange("p k e -> p e k"), AX_X).then_inc(mask_v, 1)

            def rank(i, tile):
                after(dve, scat, tile, 16 * TOPK)
                nc.vector.tensor_copy(pay[:, :, 0], tok[:])
                dve.wait_ge(eg_a, tile.n)
                nc.vector.reciprocal(gsum[:, 2:3], gsum[:, 1:2])
                dve.drain()
                nc.vector.tensor_scalar(pay[:, :, 1].bitcast(F32), gsum[:, 4:8], gsum[:, 2:3], None, ALU.mult)
                dve.wait_ge(rk_mm, tile.n)
                nc.vector.tensor_tensor(ohp, oneh[:], Y[:, 512:512 + E].unsqueeze(1).to_broadcast([P, TOPK, E]), ALU.mult)
                nc.vector.tensor_tensor(m.seen[:], m.seen[:], mask[:], ALU.add)
                dve.drain()
                nc.vector.reduce_sum(slotf[:], ohp, AX_X)
                nc.vector.tensor_scalar(tok[:], tok[:], float(P), None, ALU.add)
                dve.drain()
                nc.vector.scalar_tensor_tensor(slotf[:], topf[:], float(SEQ), slotf[:], ALU.mult, ALU.add)
                dve.drain()
                nc.vector.tensor_copy(sloti[:], slotf[:]).then_inc(slot_v, 1)

            dve.wait_ge(bias_in, 32)
            nc.vector.memset(bias[0:CHUNK, :, WINDOW - CHUNK:], NEG)
            nc.vector.memset(bias[CHUNK:P, :, 0:CHUNK], NEG)
            dve.drain()
            dve.wait_ge(zeroed, 2)
            dve.wait_ge(consts, 4)
            dve.wait_ge(b_small, 32)
            run(dve, {"stage": stage, "scores": scores, "values": values, "norm_a": norm_a, "scale_a": scale_a,
                      "turn_a": turn_a, "project_a": project_a, "turn_h": turn_h, "norm_q": norm_q,
                      "scores_x": scores_x, "weigh_x": weigh_x, "turn_x": turn_x, "project_x": project_x,
                      "turn_r": turn_r, "route": route, "rank": rank})


SLOT_COLS = 512
GU_SLOTS = 2 * FF // SLOT_COLS
SLOTS = GU_SLOTS + D // SLOT_COLS
WIDTHS = (128, 144, 160, 176, 192, 208, 224, 240, 256)
FIELDS = 4


def phase_c(nc, m, d, sem, psum):
    s = Map(nc, m.small_end)
    w = [s.put(f"w{i}", [P, KD, SLOT_COLS]) for i in range(SLOTS)]
    xg = s.put("xg", [P, UB, D])
    xT = s.put("xT", [P, KD, UNIT])
    aT = s.put("aT", [P, FS, UNIT])
    yT = s.put("yT", [P, KD, UNIT])
    y = s.put("y", [P, UB, D])
    g = [s.put(f"g{i}", [P, UNIT]) for i in range(2)]
    sg = [s.put(f"sg{i}", [P, UNIT]) for i in range(2)]
    li = [s.put(f"li{i}", [P, UNIT]) for i in range(2)]
    bg = s.put("bg", [P, E * FS])
    bl = s.put("bl", [P, E * FS])
    bd = s.put("bd", [P, E * KD])
    rawg = s.put("rawg", [P, 2, 2 * P])
    rawd = s.put("rawd", [P, 2, P])
    idx = s.put("idx", [P, UB, 2], I32)
    cur = s.put("cur", [P, UB, 2], I32)
    cnt = s.put("cnt", [P, E])
    nun = s.put("nun", [P, E])
    cum = s.put("cum", [P, E])
    one = s.put("one", [P, E])
    le = s.put("le", [P, E])
    tmp = s.put("tmp", [P, E])
    ef = s.put("ef", [P, E])
    row = s.put("row", [P, 1])
    tcol = s.put("tcol", [P, 8])
    tint = s.put("tint", [P, FIELDS], I32)
    nint = s.put("nint", [1, 2], I32)
    tab = s.put("tab", [1, P * FIELDS], I32)
    assert s.at <= nc.sbuf_usable_end, s.at

    gup = psum("c_gu", [P, 4, 512])
    trp = psum("c_tr", [P, 2, 512])
    yp = psum("c_y", [P, 2, 512])

    raw_in, consts, cnt_mm, tab_v, tab_out, tab_in, nint_v = (
        sem(x) for x in ("raw_in", "c_consts", "cnt_mm", "tab_v", "tab_out", "tab_in", "nint_v"))
    braw_mm, bias_v, clear_v = sem("braw_mm"), sem("bias_v"), sem("clear_v")
    w_in = [sem(f"c_w{i}") for i in range(SLOTS)]
    idx_in, cur_p, xg_in = sem("idx_in"), sem("cur_p"), [sem(f"xg_in{b}") for b in range(UB)]
    x_tr, xT_c = [sem(f"x_tr{i}") for i in range(4)], [sem(f"xT_c{i}") for i in range(4)]
    gu_mm, g_v, sg_a, l_v, a_v = ([sem(f"{n}{j}") for j in range(FS)] for n in ("gu_mm", "g_v", "sg_a", "l_v", "a_v"))
    dn_mm, yT_a = ([sem(f"{n}{i}") for i in range(KD)] for n in ("dn_mm", "yT_a"))
    y_tr, y_v = ([sem(f"{n}{i}") for i in range(2 * UB)] for n in ("y_tr", "y_v"))
    scat, met_p = sem("c_scat"), sem("c_met_p")

    def load(eng, col, most):
        return eng.value_load(tab[0:1, bass.ds(col, 1)], min_val=0, max_val=most)

    def n_units(eng):
        eng.wait_ge(tab_in, 16)
        eng.wait_ge(nint_v, 1)
        return eng.value_load(nint[0:1, 0:1], min_val=E, max_val=MAX_UNITS)

    def width_of(eng, unit):
        return load(eng, unit * FIELDS + 3, len(WIDTHS) - 1)

    with nc.Block() as block:

        @block.sync
        def _(sp):
            rows = d.b_gate_up.rearrange("e (j c) -> (e j) c", j=FS)
            sp.dma_start(rawg[:], rows.rearrange("(r p) c -> p r c", p=P)).then_inc(raw_in, 16)
            rows = d.b_down.rearrange("e (j c) -> (e j) c", j=KD)
            sp.dma_start(rawd[:], rows.rearrange("(r p) c -> p r c", p=P)).then_inc(raw_in, 16)

            def weights(i, e):
                if i < GU_SLOTS:
                    src = d.w_gate_up[e, :, i * SLOT_COLS:(i + 1) * SLOT_COLS]
                else:
                    src = d.w_down[e, :, (i - GU_SLOTS) * SLOT_COLS:(i - GU_SLOTS + 1) * SLOT_COLS]
                sp.dma_start(w[i][:], src.rearrange("(k p) n -> p k n", p=P)).then_inc(w_in[i], 16)

            for i in range(SLOTS):
                weights(i, 0)
            sp.wait_ge(tab_v, 1)
            sp.dma_start(d.units[:], tint[:]).then_inc(tab_out, 16)
            sp.wait_ge(tab_out, 16)
            sp.dma_start(tab[:], d.units.rearrange("(a u) f -> a (u f)", a=1)).then_inc(tab_in, 16)
            count = n_units(sp)
            with sp.Fori(1, count) as u:
                e = load(sp, u * FIELDS, E - 1)
                before = sp.snap(u)
                for i in range(SLOTS):
                    sp.wait_ge(gu_mm[2 * i + 1] if i < GU_SLOTS else dn_mm[4 * (i - GU_SLOTS) + 3], before)
                    weights(i, e)

        @block.gpsimd
        def _(pool):
            nc.gpsimd.iota(row[:], [[0, 1]], base=0, channel_multiplier=1, allow_small_or_imprecise_dtypes=True).then_inc(consts, 1)
            nc.gpsimd.iota(ef[:], [[1, E]], base=0, channel_multiplier=0, allow_small_or_imprecise_dtypes=True).then_inc(consts, 1)
            nc.gpsimd.memset(one[:], 1.0).then_inc(consts, 1)

            def slots_of(first, u1):
                pool.dma_start(idx[:], d.slots[bass.ds(first, UNIT), :].rearrange("(b p) c -> p b c", p=P)).then_inc(idx_in, 16)
                pool.wait_ge(idx_in, 16 * u1)
                pool.sem_inc(met_p, 1)

            def gather(b, n=P):
                pool.indirect_dma_start(xg[0:n, b, :], None, d.h[:],
                                        bass.IndirectOffsetOnAxis(ap=idx[0:n, b, 0:1], axis=0)).then_inc(xg_in[b], 16)

            def scatter(b, n=P):
                pool.indirect_dma_start(d.out[:], bass.IndirectOffsetOnAxis(ap=cur[0:n, b, 0:1], axis=0), y[0:n, b, :],
                                        None, compute_op=ALU.add).then_inc(scat, 16)

            slots_of(0, 1)
            for b in range(UB):
                gather(b)
            count = n_units(pool)
            with pool.Fori(0, count) as u:
                u1 = pool.snap(u + 1)
                pool.wait_ge(x_tr[3], u1)
                pool.sem_inc(met_p, 1)
                nc.gpsimd.tensor_copy(cur[:], idx[:]).then_inc(cur_p, 1)
                pool.wait_ge(cur_p, u1)
                slots_of(load(pool, u1 * FIELDS + 1, E * SEQ - UNIT), u + 2)
                gather(0)
                with pool.If(width_of(pool, u1) == 0):
                    gather(1, 16)
                with pool.Else():
                    gather(1)
                pool.wait_ge(y_v[0], u1)
                pool.wait_ge(y_v[1], u1)
                pool.sem_inc(met_p, 1)
                scatter(0)
                pool.wait_ge(y_v[2], u1)
                pool.wait_ge(y_v[3], u1)
                with pool.If(width_of(pool, u) == 0):
                    scatter(1, 16)
                with pool.Else():
                    scatter(1)
                pool.wait_ge(scat, 16 * UB * u1)
            pool.wait_ge(xg_in[0], 16 * count + 16)
            pool.wait_ge(xg_in[1], 16 * count + 16)

        @block.tensor
        def _(pe):
            pe.wait_ge(raw_in, 32)
            pe.wait_ge(clear_v, 1)
            nc.tensor.matmul(yp[:, 0, 0:E], m.ones[:], m.seen[:], start=True, stop=True).then_inc(cnt_mm, 1)
            for r in range(2):
                nc.tensor.transpose(gup[:, 0, r * P:(r + 1) * P], rawg[:, r, 0:2 * P:2], m.ident[:])
                nc.tensor.transpose(gup[:, 1, r * P:(r + 1) * P], rawg[:, r, 1:2 * P:2], m.ident[:])
                last = nc.tensor.transpose(gup[:, 2, r * P:(r + 1) * P], rawd[:, r, :], m.ident[:])
            last.then_inc(braw_mm, 1)
            pe.wait_ge(bias_v, 1)

            def turn_x(q, u1):
                for k in range(4):
                    last = nc.tensor.transpose(trp[:, q % 2, k * P:(k + 1) * P],
                                               xg[:, q // 2, ((q % 2) * 4 + k) * P:((q % 2) * 4 + k + 1) * P], m.ident[:])
                last.then_inc(x_tr[q], 1)

            def turn_y(q, u1):
                if q % 2:
                    pe.wait_ge(yT_a[7], u1)
                else:
                    pe.wait_ge(yT_a[3], u1)
                if q >= 2:
                    pe.wait_ge(y_v[q - 2], u1)
                for i in range(4):
                    last = nc.tensor.transpose(yp[:, q % 2, i * P:(i + 1) * P],
                                               yT[:, (q % 2) * 4 + i, (q // 2) * P:(q // 2 + 1) * P], m.ident[:])
                last.then_inc(y_tr[q], 1)

            def gate_up(n, u1, w1):
                for j in range(FS):
                    i, c = j * 2 * P // SLOT_COLS, j * 2 * P % SLOT_COLS
                    if c == 0:
                        pe.wait_ge(w_in[i], w1)
                    if j >= 4:
                        pe.wait_ge(l_v[j - 4], u1)
                    for half in range(2):
                        for k in range(KD):
                            last = nc.tensor.matmul(gup[:, j % 4, half * UNIT:half * UNIT + n],
                                                    w[i][:, k, c + half:c + 2 * P:2], xT[:, k, 0:n],
                                                    start=(k == 0), stop=(k == KD - 1))
                    last.then_inc(gu_mm[j], 1)

            def down(n, u1, w1, slices):
                for i in slices:
                    s_, c = GU_SLOTS + i * P // SLOT_COLS, i * P % SLOT_COLS
                    if c == 0:
                        pe.wait_ge(w_in[s_], w1)
                    if i == 0:
                        pe.wait_ge(a_v[FS - 1], u1)
                    if i < 4:
                        pe.wait_ge(l_v[4 + i], u1)
                    else:
                        pe.wait_ge(yT_a[i - 4], u1)
                    for k in range(FS):
                        last = nc.tensor.matmul(gup[:, i % 4, 0:n], w[s_][:, k, c:c + P], aT[:, k, 0:n],
                                                start=(k == 0), stop=(k == FS - 1))
                    last.then_inc(dn_mm[i], 1)

            def unit(n, u1, w1, next_one):
                gate_up(n, u1, w1)
                pe.wait_ge(xg_in[0], next_one[1])
                turn_x(0, u1)
                turn_x(1, u1)
                down(n, u1, w1, range(6))
                turn_y(0, u1)
                down(n, u1, w1, range(6, 7))
                if n > P:
                    turn_y(2, u1)
                else:
                    pe.sem_inc(y_tr[2], 1)
                down(n, u1, w1, range(7, 8))
                pe.wait_ge(xg_in[1], next_one[1])
                pe.wait_ge(xT_c[0], next_one[0])
                pe.wait_ge(xT_c[1], next_one[0])
                with pe.If(next_one[2] == 0):
                    pe.sem_inc(x_tr[2], 1)
                    pe.sem_inc(x_tr[3], 1)
                with pe.Else():
                    turn_x(2, u1)
                    turn_x(3, u1)
                turn_y(1, u1)
                if n > P:
                    turn_y(3, u1)
                else:
                    pe.sem_inc(y_tr[3], 1)

            def by_width(width, some, body):
                if len(some) == 1:
                    return body(some[0][1])
                half = len(some) // 2
                with pe.If(width < some[half][0]):
                    by_width(width, some[:half], body)
                with pe.Else():
                    by_width(width, some[half:], body)

            for q in range(2 * UB):
                pe.wait_ge(xg_in[q // 2], 16)
                if q >= 2:
                    pe.wait_ge(xT_c[q - 2], 1)
                turn_x(q, 1)
            count = n_units(pe)
            with pe.Fori(0, count) as u:
                u1, u2 = pe.snap(u + 1), pe.snap(u + 2)
                w1, w2 = pe.snap(16 * u + 16), pe.snap(16 * u + 32)
                width, next_width = width_of(pe, u), width_of(pe, u1)
                for q in range(2 * UB):
                    pe.wait_ge(xT_c[q], u1)
                by_width(width, list(enumerate(WIDTHS)), lambda n: unit(n, u1, w1, (u2, w2, next_width)))

        @block.scalar
        def _(act):
            def copy_x(q, u1):
                act.wait_ge(x_tr[q], u1)
                for k in range(4):
                    last = nc.scalar.activation(xT[:, 4 + k, (q // 2) * P:(q // 2 + 1) * P], trp[:, 1, k * P:(k + 1) * P],
                                                ACT.Copy, scale=m.g_ffn[:, 4 + k:5 + k])
                last.then_inc(xT_c[q], 1)

            copy_x(1, 1)
            copy_x(3, 1)
            count = n_units(act)
            with act.Fori(0, count) as u:
                u1 = act.snap(u + 1)
                e = load(act, u * FIELDS, E - 1)
                for j in range(FS):
                    act.wait_ge(g_v[j], u1)
                    nc.scalar.activation(sg[j % 2][:], g[j % 2][:], ACT.Sigmoid, scale=ALPHA).then_inc(sg_a[j], 1)
                u2 = act.snap(u + 2)
                copy_x(1, u2)
                for i in range(KD):
                    act.wait_ge(dn_mm[i], u1)
                    nc.scalar.activation(yT[:, i, :], gup[:, i % 4, 0:UNIT], ACT.Identity,
                                         bias=bd[:, bass.ds(e * KD + i, 1)]).then_inc(yT_a[i], 1)
                copy_x(3, u2)

        @block.vector
        def _(dve):
            nc.vector.memset(gup[:], 0.0)
            nc.vector.memset(yp[:], 0.0).then_inc(clear_v, 1)
            dve.wait_ge(cnt_mm, 1)
            dve.wait_ge(consts, 3)
            nc.vector.tensor_copy(cnt[:], yp[:, 0, 0:E])
            dve.drain()
            nc.vector.tensor_scalar(nun[:], cnt[:], float(UNIT), 1.0, ALU.is_gt, ALU.add)
            dve.drain()
            for r in range(2, SEQ // UNIT):
                nc.vector.scalar_tensor_tensor(nun[:], cnt[:], float(r * UNIT), nun[:], ALU.is_gt, ALU.add)
                dve.drain()
            nc.vector.tensor_tensor_scan(cum[:], one[:], nun[:], 0.0, ALU.mult, ALU.add)
            dve.drain()
            expert, before, many, first, width = (tcol[:, i:i + 1] for i in range(5))
            nc.vector.tensor_scalar(le[:], cum[:], row[:], None, ALU.is_le)
            dve.drain()
            nc.vector.reduce_sum(expert, le[:], AX_X)
            nc.vector.tensor_tensor(tmp[:], le[:], nun[:], ALU.mult)
            dve.drain()
            nc.vector.reduce_sum(before, tmp[:], AX_X)
            dve.drain()
            nc.vector.tensor_tensor(before, row[:], before, ALU.subtract)
            nc.vector.tensor_scalar(le[:], ef[:], expert, None, ALU.is_equal)
            dve.drain()
            nc.vector.tensor_tensor(tmp[:], le[:], cnt[:], ALU.mult)
            nc.vector.tensor_scalar(expert, expert, float(E - 1), None, ALU.min)
            nc.vector.tensor_scalar(before, before, float(UNIT), 0.0, ALU.mult, ALU.max)
            dve.drain()
            nc.vector.reduce_sum(many, tmp[:], AX_X)
            nc.vector.scalar_tensor_tensor(first, expert, float(SEQ), before, ALU.mult, ALU.add)
            dve.drain()
            nc.vector.tensor_tensor(many, many, before, ALU.subtract)
            nc.vector.tensor_scalar(first, first, float(E * SEQ - UNIT), None, ALU.min)
            dve.drain()
            nc.vector.tensor_scalar(many, many, 0.0, float(SEQ), ALU.max, ALU.min)
            dve.drain()
            nc.vector.tensor_scalar(width, many, float(WIDTHS[0]), None, ALU.is_gt)
            dve.drain()
            for n in WIDTHS[1:-1]:
                nc.vector.scalar_tensor_tensor(width, many, float(n), width, ALU.is_gt, ALU.add)
                dve.drain()
            for i, col in enumerate((expert, first, many, width)):
                nc.vector.tensor_copy(tint[:, i:i + 1], col)
            dve.drain()
            nc.vector.tensor_copy(nint[0:1, 0:1], cum[0:1, E - 1:E]).then_inc(nint_v, 1)
            dve.sem_inc(tab_v, 1)
            dve.wait_ge(braw_mm, 1)
            nc.vector.tensor_copy(bg[:], gup[:, 0, 0:2 * P])
            nc.vector.tensor_scalar(bl[:], gup[:, 1, 0:2 * P], 1.0, None, ALU.add)
            nc.vector.tensor_copy(bd[:], gup[:, 2, 0:2 * P]).then_inc(bias_v, 1)
            dve.drain()

            def copy_x(q, u1):
                dve.wait_ge(x_tr[q], u1)
                for k in range(4):
                    last = nc.vector.tensor_scalar(xT[:, k, (q // 2) * P:(q // 2 + 1) * P], trp[:, 0, k * P:(k + 1) * P],
                                                   m.g_ffn[:, k:k + 1], None, ALU.mult)
                last.then_inc(xT_c[q], 1)

            def weigh(q, u1):
                b, at = q // 2, (q % 2) * 512
                dve.wait_ge(y_tr[q], u1)
                nc.vector.tensor_scalar(y[:, b, at:at + 512], yp[:, q % 2, :], cur[:, b, 1:2].bitcast(F32), None,
                                        ALU.mult).then_inc(y_v[q], 1)

            copy_x(0, 1)
            copy_x(2, 1)
            count = n_units(dve)
            with dve.Fori(0, count) as u:
                u1 = dve.snap(u + 1)
                e = load(dve, u * FIELDS, E - 1)
                for j in range(FS):
                    dve.wait_ge(gu_mm[j], u1)
                    nc.vector.tensor_scalar(g[j % 2][:], gup[:, j % 4, 0:UNIT], bg[:, bass.ds(e * FS + j, 1)], LIMIT,
                                            ALU.add, ALU.min).then_inc(g_v[j], 1)
                    nc.vector.tensor_scalar(li[j % 2][:], gup[:, j % 4, UNIT:2 * UNIT], bl[:, bass.ds(e * FS + j, 1)],
                                            LIMIT + 1.0, ALU.add, ALU.min).then_inc(l_v[j], 1)
                    dve.drain()
                    nc.vector.scalar_tensor_tensor(li[j % 2][:], li[j % 2][:], 1.0 - LIMIT, g[j % 2][:], ALU.max, ALU.mult)
                    dve.drain()
                    dve.wait_ge(sg_a[j], u1)
                    nc.vector.tensor_tensor(aT[:, j, :], li[j % 2][:], sg[j % 2][:], ALU.mult).then_inc(a_v[j], 1)
                u2 = dve.snap(u + 2)
                copy_x(0, u2)
                dve.wait_ge(cur_p, u1)
                weigh(0, u1)
                weigh(2, u1)
                copy_x(2, u2)
                weigh(1, u1)
                weigh(3, u1)


def build(nc, d):
    m = lay_out(nc)
    for phase in (phase_a, phase_b, phase_c):
        sems, banks = [], []

        def sem(name):
            sems.append(nc.alloc_semaphore(name))
            return sems[-1]

        with ExitStack() as stack:
            phase(nc, m, d, sem, lambda name, shape: stack.enter_context(nc.psum_tensor(name, shape, F32)))
        nc.all_engine_barrier()
        nc.clear_and_free_semaphores(sems)
        nc.all_engine_barrier()


def kernel(**inputs):
    import concourse.bacc as bacc
    from concourse.bass_utils import run_bass_kernel_spmd

    nc = bacc.Bacc("TRN2", target_bir_lowering=False, num_devices=1)
    d, arrays = Buffers(), {}
    inputs["rel_rev"] = np.asarray(inputs.pop("rel_bias"))[:, :, ::-1]
    for name, value in inputs.items():
        a = np.ascontiguousarray(value)
        arrays["in_" + name] = a
        ap = nc.dram_tensor("in_" + name, a.shape, mybir.dt.from_np(a.dtype), kind="ExternalInput").ap()
        d.__dict__[name] = ap[0]
    d.out = nc.dram_tensor("out_0", (SEQ + PAD, D), F32, kind="ExternalOutput").ap()
    d.h = nc.dram_tensor("h_rows", (SEQ + PAD, D), F32).ap()
    d.slots = nc.dram_tensor("slots", (E * SEQ, 2), I32).ap()
    d.band = nc.dram_tensor("band", (P, HEADS * (WINDOW + P) + 1), F32).ap()
    d.units = nc.dram_tensor("units", (P, FIELDS), I32).ap()
    build(nc, d)
    r = run_bass_kernel_spmd(nc, [arrays], core_ids=[0])
    return r.results[0]["out_0"][:SEQ].reshape(1, SEQ, D)
```

```python
from contextlib import ExitStack

import numpy as np

import concourse.bass as bass
import concourse.mybir as mybir
from concourse.alu_op_type import AluOpType as ALU

ACT = mybir.ActivationFunctionType
F32 = mybir.dt.float32
I32 = mybir.dt.int32
U32 = mybir.dt.uint32
AX_X = mybir.AxisListType.X

P = 128
D = 1024
KD = D // P
SEQ = 1024
TILES = SEQ // P
CHUNK = 64
HEADS, HEAD = 8, 64
PAIRS = HEADS // 2
D_ATT = HEADS * HEAD
CONV = 512
CS = CONV // P
CONV_W = 3
N_IN = 3 * D_ATT + 3 * CONV
BAND_TILES = 5
WINDOW = BAND_TILES * P
MAX_REL = 256
N_REL = 2 * MAX_REL + 1
MEM = 256
MT = MEM // P
XH, XD = 4, 128
D_X = XH * XD
E = 32
TOPK = 4
FF = 1024
FS = FF // P
LIMIT, ALPHA = 7.0, 1.702
EPS = 1e-6
NEG = -1e30
UNIT = 256
UB = UNIT // P
MAX_UNITS = E + SEQ * TOPK // UNIT
SLOT_COLS = 512
GU_SLOTS = 2 * FF // SLOT_COLS
SLOTS = GU_SLOTS + D // SLOT_COLS
PAD = UNIT


SLOT_BYTES = KD * SLOT_COLS * 4


def expert_weights(eng, m, d, i, e):
    if i < GU_SLOTS:
        src = d.w_gate_up[e, :, i * SLOT_COLS:(i + 1) * SLOT_COLS]
    else:
        src = d.w_down[e, :, (i - GU_SLOTS) * SLOT_COLS:(i - GU_SLOTS + 1) * SLOT_COLS]
    return eng.dma_start(m.w[i][:], src.rearrange("(k p) n -> p k n", p=P))


class Map:

    def __init__(self, nc, base):
        self.nc, self.at = nc, base

    def put(self, name, shape, dt=F32, at=None):
        size = 4
        for n in shape[1:]:
            size *= n
        size = (size + 31) // 32 * 32
        if at is None:
            at, self.at = self.at, self.at + size
        return self.nc.alloc_sbuf_tensor_at(name, shape, dt, offset=at)


class Buffers:
    pass


def lay_out(nc):
    m = Buffers()
    s = Map(nc, (nc.sbuf_base + 31) // 32 * 32)
    m.ident = s.put("ident", [P, P])
    m.ones = s.put("ones", [P, P])
    m.before = s.put("before", [P, P])
    m.g_mix = s.put("g_mix", [P, KD])
    m.g_x = s.put("g_x", [P, KD])
    m.g_ffn = s.put("g_ffn", [P, KD])
    m.g_mem = s.put("g_mem", [P, KD])
    m.g_q = s.put("g_q", [P, 1])
    m.g_k = s.put("g_k", [P, 1])
    m.g_xq = s.put("g_xq", [P, 1])
    m.g_xk = s.put("g_xk", [P, 1])
    m.g_a = s.put("g_a", [P, CS])
    m.g_b = s.put("g_b", [P, CS])
    m.conv_w = s.put("conv_w_sb", [P, CONV_W, CS])
    m.seen = s.put("seen", [P, E])
    m.small_end = s.at
    m.kxT = s.put("kxT", [P, XH, MEM])
    m.vx = s.put("vx", [P, MT, D_X])
    kT_at = s.at
    m.kT = s.put("kT", [P, PAIRS, SEQ])
    v_at = s.at
    m.v = s.put("v", [P, TILES, D_ATT])
    keep = s.at
    m.qT = s.put("qT", [P, PAIRS, SEQ])
    m.ybT = s.put("ybT", [P, CS, SEQ])
    wide = s.at
    assert GU_SLOTS == 4 and wide == kT_at + 4 * SLOT_BYTES
    m.w = [s.put(f"w{i}", [P, KD, SLOT_COLS], at=at)
           for i, at in enumerate((kT_at, keep, v_at, keep + SLOT_BYTES, wide, wide + SLOT_BYTES))]
    m.w_in = s.put("w_in_sb", [P, KD, N_IN])
    m.xin = [s.put(f"xin{b}", [P, D]) for b in range(2)]
    m.hT = [s.put(f"hT{b}", [P, KD, P]) for b in range(2)]
    own = s.at
    m.qn = s.put("qn", [P, D])
    m.u = s.put("u", [P, CS, P + CONV_W - 1])
    m.cg = s.put("cg", [P, 2, P])
    m.ct = s.put("ct", [P, P])
    m.ybr = s.put("ybr", [P, CS, P])
    m.sqb = s.put("sqb", [P, CS, P])
    m.rb = s.put("rb", [P, P])
    m.sqk = s.put("sqk", [P, D])
    m.ss = s.put("ss", [P, 2, 1])
    m.ssqk = s.put("ssqk", [P, 16])
    m.ssm = s.put("ssm", [P, MT])
    m.epsm = s.put("epsm", [P, MT])
    m.ext = s.put("ext", [HEADS, WINDOW + P])
    m.empty = s.put("empty", [P, E * SEQ // P, 2], I32)
    m.w_xkv = s.put("w_xkv_sb", [P, KD, 2 * D_X], at=keep)
    m.keep, m.wide, m.own, m.s = keep, wide, own, s
    assert s.at <= nc.sbuf_usable_end, (s.at, nc.sbuf_usable_end)
    return m


N_GAINS = 7 + 4 + CONV_W
IN_PARTS = ((3 * D_ATT, N_IN), (0, 2 * D_ATT), (2 * D_ATT, 3 * D_ATT))


def phase_a(nc, m, d, sem, psum):
    trp = psum("a_tr", [P, 2, 512])
    qkp = psum("a_qk", [P, 2, 512])
    vp = psum("a_v", [P, 512])
    cvp = psum("a_cv", [P, 2, 512])
    sbp = psum("a_sb", [P, 512])

    consts = sem("a_consts")
    gains, g_mem_in = sem("a_gains"), sem("a_g_mem_in")
    wxkv_in = [sem(f"a_wxkv_in{i}") for i in range(2)]
    win_in = [sem(f"a_win_in{i}") for i in range(3)]
    mem_in = [sem(f"a_mem_in{b}") for b in range(2)]
    m_sq, m_ms, m_tr = sem("m_sq"), sem("m_ms"), sem("m_tr")
    m_hTv, m_hTa = sem("m_hTv"), sem("m_hTa")
    m_kv, m_ksq, m_kms, m_krs, m_kn, m_ktr = (sem("m_" + x) for x in ("kv", "ksq", "kms", "krs", "kn", "ktr"))
    m_kT, m_v, m_vv = sem("m_kT"), sem("m_v"), sem("m_vv")
    x_in = [sem(f"a_x_in{b}") for b in range(2)]
    x_sq, x_ms, x_h, x_tr = sem("x_sq"), sem("x_ms"), sem("x_h"), sem("x_tr")
    hT_v, hT_a = sem("hT_v"), sem("hT_a")
    cv_mm = [sem(f"cv_mm{c}") for c in range(CS)]
    cg_a = [sem(f"cg_a{c}") for c in range(CS)]
    cv_y = [sem(f"cv_y{c}") for c in range(CS)]
    cv_free = [sem(f"cv_free{c}") for c in range(CS)]
    sqb_a, sb_mm, bms_v, brs_a = sem("sqb_a"), sem("sb_mm"), sem("bms_v"), sem("brs_a")
    qk_mm, qksq_a, qkms_v, qkrs_a, qn_v = (sem(x) for x in ("qk_mm", "qksq_a", "qkms_v", "qkrs_a", "qn_v"))
    v_mm, v_a, qk_tr, qT_v, kT_a = (sem(x) for x in ("v_mm", "v_a", "qk_tr", "qT_v", "kT_a"))
    ext_in, ext_sb, ext_out, slots_out = sem("ext_in"), sem("ext_sb"), sem("ext_out"), sem("slots_out")
    kvp = [(qkp[:, 0, :], qkp[:, 1, :]), (vp[:], sbp[:])]
    kn = [m.qn[:, 0:D_X], m.qn[:, D_X:2 * D_X]]
    xm = m.hT
    cvv = cvp[:, :, 0:3 * P].rearrange("p b (j t) -> p b j t", j=3)

    def rows(ap, t):
        return ap[bass.ds(t * P, P), :]

    with nc.Block() as block:

        @block.sync
        def _(sp):
            for b in range(2):
                sp.dma_start(m.xin[b][:], d.mem[b * P:(b + 1) * P, :]).then_inc(mem_in[b], 16)
            with nc.allow_non_contiguous_dma(reason="a gain to a partition"):
                sp.dma_start(m.g_mem[:], d.norm_mem_g.rearrange("(k p) -> p k", p=P)).then_inc(g_mem_in, 16)
            for half in range(2):
                at = slice(half * D_X, (half + 1) * D_X)
                sp.dma_start(m.w_xkv[:, :, at], d.w_xkv[:, at].rearrange("(k p) n -> p k n", p=P)).then_inc(wxkv_in[half], 16)
            with nc.allow_non_contiguous_dma(reason="gains, one value to a partition"):
                for tile, src in ((m.g_mix, d.norm_mix_g), (m.g_x, d.norm_xattn_g),
                                  (m.g_ffn, d.norm_ffn_g), (m.g_a, d.out_norm_a_g), (m.g_b, d.out_norm_b_g),
                                  (m.g_xq, d.xq_norm_g), (m.g_xk, d.xk_norm_g)):
                    sp.dma_start(tile[:], src.rearrange("(k p) -> p k", p=P)).then_inc(gains, 16)
                for h in range(2):
                    at = slice(h * HEAD, (h + 1) * HEAD)
                    sp.dma_start(m.g_q[at, :], d.q_norm_g.rearrange("(p a) -> p a", a=1)).then_inc(gains, 16)
                    sp.dma_start(m.g_k[at, :], d.k_norm_g.rearrange("(p a) -> p a", a=1)).then_inc(gains, 16)
                for j in range(CONV_W):
                    sp.dma_start(m.conv_w[:, j, :], d.conv_w[j].rearrange("(c p) -> p c", p=P)).then_inc(gains, 16)
            for i, (a, b) in enumerate(IN_PARTS):
                sp.dma_start(m.w_in[:, :, a:b], d.w_in[:, a:b].rearrange("(k p) n -> p k n", p=P)).then_inc(win_in[i], 16)
                if i == 0:
                    sp.wait_ge(m_tr, MT)
                    sp.wait_ge(m_sq, MT)
                    for b in range(2):
                        sp.dma_start(m.xin[b][:], rows(d.x, b)).then_inc(x_in[b], 16)
            with sp.Fori(0, TILES // 2 - 1) as i:
                for b in range(2):
                    seen = sp.snap(2 * i + (b + 1))
                    sp.wait_ge(x_tr, seen)
                    sp.dma_start(m.xin[b][:], rows(d.x, 2 * i + (b + 2))).then_inc(x_in[b], 16)

        @block.gpsimd
        def _(pool):
            nc.gpsimd.memset(m.ident[:], 0.0).then_inc(consts, 1)
            nc.gpsimd.memset(m.ones[:], 1.0).then_inc(consts, 1)
            pool.wait_ge(consts, 2)
            nc.gpsimd.affine_select(out=m.ident[:], in_=m.ident[:], compare_op=ALU.not_equal, fill=1.0, base=0,
                                    pattern=[[-1, P]], channel_multiplier=1).then_inc(consts, 1)
            nc.gpsimd.affine_select(out=m.before[:], in_=m.ones[:], compare_op=ALU.is_gt, fill=0.0, base=0,
                                    pattern=[[1, P]], channel_multiplier=-1).then_inc(consts, 1)
            flat = WINDOW + P - 1 - (MAX_REL + P)
            with nc.allow_non_contiguous_dma(reason="eight short rows"):
                pool.dma_start(m.ext[:, flat:], d.rel_rev[:, 0:WINDOW + P - flat]).then_inc(ext_in, 16)
            nc.gpsimd.memset(m.empty[:], 0).then_inc(ext_sb, 1)
            pool.wait_ge(ext_sb, 1)
            nc.gpsimd.iota(m.empty[:, :, 0], [[0, E * SEQ // P // UNIT], [1, UNIT]], base=SEQ,
                           channel_multiplier=0).then_inc(ext_sb, 1)
            pool.wait_ge(ext_sb, 2)
            pool.dma_start(d.slots.rearrange("(p s) c -> p (s c)", p=P),
                           m.empty[:].rearrange("p s c -> p (s c)")).then_inc(slots_out, 16)
            pool.wait_ge(ext_in, 16)
            nc.gpsimd.tensor_copy(m.ext[:, 0:flat], m.ext[:, flat:flat + 1].to_broadcast([HEADS, flat])).then_inc(ext_sb, 1)
            pool.wait_ge(ext_sb, 3)
            pool.wait_ge(win_in[2], 16)
            pool.dma_start(bass.AP(tensor=d.band.tensor, offset=0,
                                   ap=[[WINDOW + P, HEADS], [HEADS * (WINDOW + P) + 1, P], [1, WINDOW + P]]),
                           m.ext[:].unsqueeze(1).to_broadcast([HEADS, P, WINDOW + P])).then_inc(ext_out, 16)
            pool.wait_ge(ext_out, 16)
            pool.wait_ge(slots_out, 16)

        @block.tensor
        def _(pe):
            pe.wait_ge(consts, 4)
            for b in range(MT):
                pe.wait_ge(mem_in[b], 16)
                if b:
                    pe.wait_ge(m_hTv, b)
                    pe.wait_ge(m_hTa, b)
                for k in range(KD):
                    last = nc.tensor.transpose(trp[:, k // 4, (k % 4) * P:(k % 4 + 1) * P],
                                               m.xin[b][:, k * P:(k + 1) * P], m.ident[:])
                last.then_inc(m_tr, 1)
            def mem_product(b, half):
                for k in range(KD):
                    last = nc.tensor.matmul(kvp[b][half], xm[b][:, k, :], m.w_xkv[:, k, half * D_X:(half + 1) * D_X],
                                            start=(k == 0), stop=(k == KD - 1))
                last.then_inc(m_vv if half else m_kv, 1)

            def turn_keys(b):
                pe.wait_ge(m_kn, b + 1)
                for h in range(XH):
                    last = nc.tensor.transpose(trp[:, b, h * P:(h + 1) * P], kn[b][:, h * XD:(h + 1) * XD], m.ident[:])
                last.then_inc(m_ktr, 1)

            pe.wait_ge(m_hTv, MT)
            pe.wait_ge(m_hTa, MT)
            for half in range(2):
                pe.wait_ge(wxkv_in[half], 16)
                for b in range(MT):
                    mem_product(b, half)
            for b in range(MT):
                turn_keys(b)

            def transpose_x(b, t1):
                pe.wait_ge(x_h, t1)
                if isinstance(t1, int) and t1 == 1:
                    pe.wait_ge(m_kT, MT)
                for k in range(KD):
                    last = nc.tensor.transpose(trp[:, k // 4, (k % 4) * P:(k % 4 + 1) * P],
                                               m.xin[b][:, k * P:(k + 1) * P], m.ident[:])
                last.then_inc(x_tr, 1)

            def convolve(b, c, t1):
                pe.wait_ge(cv_free[(c + 2) % CS], t1)
                for j in range(3):
                    col = 3 * D_ATT + j * CONV + c * P
                    for k in range(KD):
                        last = nc.tensor.matmul(cvv[:, c % 2, j, :], m.w_in[:, k, col:col + P], m.hT[b][:, k, :],
                                                start=(k == 0), stop=(k == KD - 1))
                last.then_inc(cv_mm[c], 1)

            def tile(b, t1, t2, more):
                pe.wait_ge(hT_v, t1)
                pe.wait_ge(hT_a, t1)
                convolve(b, 0, t1)
                convolve(b, 1, t1)
                pe.wait_ge(qT_v, t1)
                pe.wait_ge(kT_a, t1)
                if more:
                    transpose_x(1 - b, t2)
                convolve(b, 2, t1)
                convolve(b, 3, t1)
                pe.wait_ge(win_in[1], 16)
                for half in range(2):
                    for k in range(KD):
                        last = nc.tensor.matmul(qkp[:, half, :], m.hT[b][:, k, :],
                                                m.w_in[:, k, half * D_ATT:(half + 1) * D_ATT],
                                                start=(k == 0), stop=(k == KD - 1))
                last.then_inc(qk_mm, 1)
                pe.wait_ge(sqb_a, t1)
                for c in range(CS):
                    last = nc.tensor.matmul(sbp[:, 0:P], m.ones[:], m.sqb[:, c, :], start=(c == 0), stop=(c == CS - 1))
                last.then_inc(sb_mm, 1)
                pe.wait_ge(win_in[2], 16)
                for k in range(KD):
                    last = nc.tensor.matmul(vp[:], m.hT[b][:, k, :], m.w_in[:, k, 2 * D_ATT:3 * D_ATT],
                                            start=(k == 0), stop=(k == KD - 1))
                last.then_inc(v_mm, 1)
                pe.wait_ge(qn_v, t1)
                if more:
                    pe.wait_ge(hT_v, t2)
                    pe.wait_ge(hT_a, t2)
                for j in range(2 * PAIRS):
                    last = nc.tensor.transpose(trp[:, j // PAIRS, (j % PAIRS) * P:(j % PAIRS + 1) * P],
                                               m.qn[:, j * P:(j + 1) * P], m.ident[:])
                last.then_inc(qk_tr, 1)

            transpose_x(0, 1)
            pe.wait_ge(win_in[0], 16)
            with pe.Fori(0, TILES // 2 - 1) as i:
                count = [pe.snap(2 * i + j) for j in (1, 2, 3)]
                for b in range(2):
                    tile(b, count[b], count[b + 1], True)
            for b in range(2):
                tile(b, TILES - 1 + b, TILES + b, b == 0)

        @block.scalar
        def _(act):
            act.sem_inc(kT_a, 1)

            def norm(b, landed, t1, sq, ms, h):
                act.wait_ge(*landed)
                nc.scalar.activation(m.sqk[:], m.xin[b][:], ACT.Square, accum_out=m.ss[:, b, :]).then_inc(sq, 1)
                act.wait_ge(ms, t1)
                nc.scalar.activation(m.ss[:, b, :], m.ss[:, b, :], ACT.Sqrt)
                act.drain()
                nc.scalar.activation(m.xin[b][:], m.xin[b][:], ACT.Copy, scale=m.ss[:, b, :]).then_inc(h, 1)

            def copy_out(b, gain, tr, t1, done):
                act.wait_ge(tr, t1)
                act.wait_ge(g_mem_in, 16)
                for k in range(KD // 2, KD):
                    last = nc.scalar.activation(m.hT[b][:, k, :], trp[:, 1, (k % 4) * P:(k % 4 + 1) * P], ACT.Copy,
                                                scale=gain[:, k:k + 1])
                last.then_inc(done, 1)

            for b in range(MT):
                act.wait_ge(mem_in[b], 16)
                act.drain()
                nc.scalar.activation(m.sqk[:], m.xin[b][:], ACT.Square, accum_out=m.ssm[:, b:b + 1]).then_inc(m_sq, 1)
                copy_out(b, m.g_mem, m_tr, b + 1, m_hTa)
            act.wait_ge(m_ms, 1)
            nc.scalar.activation(m.ssm[:], m.ssm[:], ACT.Sqrt)
            for b in range(MT):
                act.wait_ge(m_kv, b + 1)
                nc.scalar.activation(m.sqk[:, b * D_X:(b + 1) * D_X], kvp[b][0], ACT.Square).then_inc(m_ksq, 1)
            for b in range(MT):
                act.wait_ge(m_kms, b + 1)
                ss = m.ssqk[:, b * XH:(b + 1) * XH]
                nc.scalar.activation(ss, ss, ACT.Sqrt).then_inc(m_krs, 1)
            norm(0, (x_in[0], 16), 1, x_sq, x_ms, x_h)
            for b in range(MT):
                act.wait_ge(m_vv, b + 1)
                nc.scalar.activation(m.vx[:, b, :], kvp[b][1], ACT.Copy, scale=m.ssm[:, b:b + 1]).then_inc(m_v, 1)
            act.wait_ge(gains, 16 * N_GAINS)
            for b in range(MT):
                act.wait_ge(m_ktr, b + 1)
                nc.scalar.activation(m.kxT[:, :, b * P:(b + 1) * P], trp[:, b, :].rearrange("p (h t) -> p h t", h=XH),
                                     ACT.Copy, scale=m.g_xk[:]).then_inc(m_kT, 1)

            def gate_copy(c, t1):
                act.wait_ge(cv_mm[c], t1)
                nc.scalar.copy(m.cg[:, c % 2, :], cvv[:, c % 2, 1, :]).then_inc(cg_a[c], 1)

            def square(c, t1):
                act.wait_ge(cv_y[c], t1)
                ins = nc.scalar.activation(m.sqb[:, c, :], m.ybr[:, c, :], ACT.Square)
                if c == CS - 1:
                    ins.then_inc(sqb_a, 1)

            def tile(b, t, t1, t2, dma1, more):
                if more:
                    norm(1 - b, (x_in[1 - b], dma1), t2, x_sq, x_ms, x_h)
                gate_copy(0, t1)
                gate_copy(1, t1)
                square(0, t1)
                square(1, t1)
                if more:
                    copy_out(1 - b, m.g_mix, x_tr, t2, hT_a)
                gate_copy(2, t1)
                gate_copy(3, t1)
                square(2, t1)
                square(3, t1)
                act.wait_ge(qk_mm, t1)
                nc.scalar.activation(m.sqk[:], qkp[:], ACT.Square).then_inc(qksq_a, 1)
                act.wait_ge(qkms_v, t1)
                nc.scalar.activation(m.ssqk[:], m.ssqk[:], ACT.Sqrt).then_inc(qkrs_a, 1)
                act.wait_ge(bms_v, t1)
                nc.scalar.activation(m.rb[:], m.rb[:], ACT.Sqrt).then_inc(brs_a, 1)
                act.wait_ge(v_mm, t1)
                nc.scalar.copy(m.v[:, t, :], vp[:]).then_inc(v_a, 1)
                act.wait_ge(qk_tr, t1)
                nc.scalar.activation(m.kT[:, :, bass.ds(t * P, P)], trp[:, 1, :].rearrange("p (h t) -> p h t", h=PAIRS),
                                     ACT.Copy, scale=m.g_k[:]).then_inc(kT_a, 1)

            copy_out(0, m.g_mix, x_tr, 1, hT_a)
            with act.Fori(0, TILES // 2 - 1) as i:
                count = [act.snap(2 * i + j) for j in (1, 2, 3)]
                dma = [act.snap(16 * i + 16), act.snap(16 * i + 32)]
                for b in range(2):
                    tile(b, 2 * i + b, count[b], count[b + 1], dma[b], True)
            for b in range(2):
                tile(b, TILES - 2 + b, TILES - 1 + b, TILES + b, 16 * (TILES // 2), b == 0)

        @block.vector
        def _(dve):
            nc.vector.memset(m.u[:, :, 0:CONV_W - 1], 0.0).then_inc(qT_v, 1)
            for c in (2, 3):
                dve.sem_inc(cv_free[c], 1)

            def rstd2(ap, n):
                nc.vector.tensor_scalar(ap, ap, 1.0 / n, EPS, ALU.mult, ALU.add)
                dve.drain()
                return nc.vector.reciprocal(ap, ap)

            def norm(b, t1, sq, ms):
                dve.wait_ge(sq, t1)
                rstd2(m.ss[:, b, :], D).then_inc(ms, 1)

            def copy_out(b, gain, tr, t1, done):
                dve.wait_ge(tr, t1)
                for k in range(KD // 2):
                    last = nc.vector.tensor_scalar(m.hT[b][:, k, :], trp[:, 0, k * P:(k + 1) * P], gain[:, k:k + 1],
                                                   None, ALU.mult)
                last.then_inc(done, 1)

            dve.wait_ge(g_mem_in, 16)
            for b in range(MT):
                copy_out(b, m.g_mem, m_tr, b + 1, m_hTv)
            dve.wait_ge(m_sq, MT)
            nc.vector.tensor_scalar(m.ssm[:], m.ssm[:], 1.0 / D, EPS, ALU.mult, ALU.add)
            dve.drain()
            nc.vector.tensor_scalar(m.epsm[:], m.ssm[:], EPS, None, ALU.mult)
            nc.vector.reciprocal(m.ssm[:], m.ssm[:]).then_inc(m_ms, 1)
            for b in range(MT):
                dve.wait_ge(m_ksq, b + 1)
                ss = m.ssqk[:, b * XH:(b + 1) * XH]
                nc.vector.reduce_sum(ss, m.sqk[:, b * D_X:(b + 1) * D_X].rearrange("p (h e) -> p h e", h=XH), AX_X)
                dve.drain()
                nc.vector.tensor_scalar(ss, ss, 1.0 / XD, m.epsm[:, b:b + 1], ALU.mult, ALU.add)
                dve.drain()
                nc.vector.reciprocal(ss, ss).then_inc(m_kms, 1)
            for b in range(MT):
                ss = m.ssqk[:, b * XH:(b + 1) * XH]
                dve.wait_ge(m_krs, b + 1)
                nc.vector.tensor_tensor(kn[b].rearrange("p (h e) -> p h e", h=XH),
                                        kvp[b][0].rearrange("p (h e) -> p h e", h=XH),
                                        ss.unsqueeze(2).to_broadcast([P, XH, XD]), ALU.mult).then_inc(m_kn, 1)
            norm(0, 1, x_sq, x_ms)

            dve.wait_ge(gains, 16 * N_GAINS)
            nc.vector.tensor_scalar(m.g_q[:], m.g_q[:], HEAD ** -0.5, None, ALU.mult)
            nc.vector.tensor_scalar(m.g_xq[:], m.g_xq[:], XD ** -0.5, None, ALU.mult)

            def conv(c, t1):
                dve.wait_ge(cg_a[c], t1)
                u = m.u[:, c, :]
                nc.vector.tensor_tensor(u[:, 2:P + 2], cvv[:, c % 2, 2, :], m.cg[:, c % 2, :], ALU.mult)
                dve.drain()
                nc.vector.tensor_scalar(m.ct[:], u[:, 2:P + 2], m.conv_w[:, 2, c:c + 1], None, ALU.mult)
                dve.drain()
                nc.vector.scalar_tensor_tensor(m.ct[:], u[:, 1:P + 1], m.conv_w[:, 1, c:c + 1], m.ct[:], ALU.mult, ALU.add)
                dve.drain()
                nc.vector.scalar_tensor_tensor(m.ct[:], u[:, 0:P], m.conv_w[:, 0, c:c + 1], m.ct[:], ALU.mult, ALU.add)
                dve.drain()
                nc.vector.tensor_tensor(m.ybr[:, c, :], cvv[:, c % 2, 0, :], m.ct[:], ALU.mult).then_inc(cv_y[c], 1)
                nc.vector.tensor_copy(u[:, 0:2], u[:, P:P + 2]).then_inc(cv_free[c], 1)
                dve.drain()

            def tile(b, t, t1, t2, more):
                if more:
                    norm(1 - b, t2, x_sq, x_ms)
                conv(0, t1)
                conv(1, t1)
                if more:
                    copy_out(1 - b, m.g_mix, x_tr, t2, hT_v)
                conv(2, t1)
                conv(3, t1)
                dve.wait_ge(qksq_a, t1)
                nc.vector.reduce_sum(m.ssqk[:], m.sqk[:].rearrange("p (h e) -> p h e", h=16), AX_X)
                dve.drain()
                rstd2(m.ssqk[:], HEAD).then_inc(qkms_v, 1)
                dve.wait_ge(sb_mm, t1)
                nc.vector.tensor_scalar(m.rb[:], sbp[:, 0:P], 1.0 / CONV, EPS, ALU.mult, ALU.add)
                dve.drain()
                nc.vector.reciprocal(m.rb[:], m.rb[:]).then_inc(bms_v, 1)
                dve.wait_ge(qkrs_a, t1)
                nc.vector.tensor_tensor(m.qn[:].rearrange("p (h e) -> p h e", h=16),
                                        qkp[:].rearrange("p a (h e) -> p (a h) e", e=HEAD),
                                        m.ssqk[:].unsqueeze(2).to_broadcast([P, 16, HEAD]), ALU.mult).then_inc(qn_v, 1)
                dve.wait_ge(brs_a, t1)
                for c in range(CS):
                    nc.vector.scalar_tensor_tensor(m.ybT[:, c, bass.ds(t * P, P)], m.ybr[:, c, :], m.g_b[:, c:c + 1],
                                                   m.rb[:], ALU.mult, ALU.mult)
                dve.wait_ge(qk_tr, t1)
                nc.vector.tensor_scalar(m.qT[:, :, bass.ds(t * P, P)], trp[:, 0, :].rearrange("p (h t) -> p h t", h=PAIRS),
                                        m.g_q[:], None, ALU.mult).then_inc(qT_v, 1)

            copy_out(0, m.g_mix, x_tr, 1, hT_v)
            with dve.Fori(0, TILES // 2 - 1) as i:
                count = [dve.snap(2 * i + j) for j in (1, 2, 3)]
                for b in range(2):
                    tile(b, 2 * i + b, count[b], count[b + 1], True)
            for b in range(2):
                tile(b, TILES - 2 + b, TILES - 1 + b, TILES + b, b == 0)


ORDER = [("stage", 0, 0), ("norm_q", 0, 2), ("choose", 0, 3), ("values", 6, 1),
         ("scores", 0, 0), ("project_b", 0, 1), ("turn_q", 0, 2), ("rank", 0, 3), ("turn_p", 7, 1), ("scores", 1, 0),
         ("values", 7, 1), ("scores_x", 0, 2), ("norm_a", 0, 1), ("turn_p", 0, 0), ("project_b", 1, 1),
         ("scale_a", 0, 1), ("weigh_x", 0, 2), ("values", 0, 0), ("turn_a", 0, 1), ("scores", 2, 0), ("turn_x", 0, 2),
         ("stage", 1, 0),
         ("project_a", 0, 1), ("turn_p", 1, 0), ("values_x", 0, 2), ("values", 1, 0), ("scores", 3, 0),
         ("project_a", 1, 1), ("convolved", 0, 0), ("turn_p", 2, 0), ("project_x", 0, 2), ("values", 2, 0),
         ("scores", 4, 0), ("turn_h", 0, 1), ("turn_p", 3, 0), ("project_x", 1, 2), ("square_r", 0, 2),
         ("values", 3, 0), ("scores", 5, 0),
         ("query", 0, 1), ("turn_p", 4, 0), ("turn_r", 0, 2), ("values", 4, 0), ("scores", 6, 0),
         ("query", 1, 1), ("mean_q", 0, 1), ("turn_p", 5, 0), ("route", 0, 2), ("values", 5, 0), ("turn_p", 6, 0),
         ("scores", 7, 0), ("scale_r", 0, 2)]
LAGS = 3
STEADY = BAND_TILES


def spans(start, n):
    out, at = [], start
    while at < start + n:
        to = min(start + n, (at // 512 + 1) * 512)
        out.append((at, to))
        at = to
    return out


class Tile:

    def __init__(self, t, l, n, bands):
        self.t, self.m, self.l, self.n, self.bands = t, t, l, n, bands
        self.first = isinstance(t, int) and t == 0


def phase_b(nc, m, d, sem, psum):
    s = Map(nc, m.wide)
    w_out = s.put("w_out_sb", [P, KD, D])
    w_xq = s.put("w_xq_sb", [P, KD, D_X])
    w_xo = s.put("w_xo_sb", [P, XH, D])
    bias = s.put("bias", [P, HEADS, WINDOW])
    yaT = s.put("yaT", [P, CS, P])
    qxT = s.put("qxT", [P, XH, P])
    oxT = s.put("oxT", [P, XH, P])
    px = s.put("px", [P, XH, MEM])
    sqq = yaT[:].rearrange("p k t -> p (k t)")
    qxn = oxT[:].rearrange("p h t -> p (h t)")
    assert s.at <= m.wide + 4 * KD * N_IN
    s.at = m.own
    qz = s.put("qz", [P, HEADS, P])
    ybs = s.put("ybs", [P, CS, P])
    p = [s.put(f"p{b}", [P, WINDOW]) for b in range(2)]
    pt = s.put("pt", [P, WINDOW])
    o = s.put("o", [P, D_ATT])
    xa = m.xin[0]
    xb = m.xin[1]
    sq = m.hT[0][:].rearrange("p a b -> p (a b)")
    hT = m.hT[1]
    pxT = s.put("pxT", [P, 2 * XH, P])
    w_r = s.put("w_r", [P, KD, E])
    b_r = s.put("b_r", [P, E])
    half = s.put("half", [P, XH])
    small = s.put("small", [P, 32])
    nm, rs = small[:, 0:8], small[:, 8:16]
    ssa, ssx, ssr = small[:, 16:17], small[:, 17:18], small[:, 18:19]
    ssq, nmx, rsx = small[:, 20:24], small[:, 24:28], small[:, 28:32]
    pw = s.put("pw", [P, 8])
    lg = sqq[:, TOPK * E:(TOPK + 1) * E]
    top = s.put("top", [P, 8])
    topi = s.put("topi", [P, 8], U32)
    topf = s.put("topf", [P, TOPK])
    eids = s.put("eids", [P, E])
    oneh = s.put("oneh", [P, TOPK, E])
    ohp = sqq[:, 0:TOPK * E].rearrange("p (k e) -> p k e", k=TOPK)
    mask = s.put("mask", [P, E])
    gsum = s.put("gsum", [P, 8])
    slotf = s.put("slotf", [P, TOPK])
    tok = s.put("tok", [P, TOPK])
    sloti = s.put("sloti", [P, TOPK], I32)
    pay = s.put("pay", [P, TOPK, 2], I32)
    assert s.at <= nc.sbuf_usable_end, s.at

    att = psum("b_att", [P, 2048])
    ps, ptp, po = att[:, 0:WINDOW], att[:, 1024:1024 + WINDOW], att[:, 1024 + WINDOW:1024 + WINDOW + P]
    X = psum("b_x", [P, 1024])
    Y = psum("b_y", [P, 1024])

    w_in = [sem(f"b_w{i}") for i in range(3)]
    near = WINDOW - 2 * P
    bias_in = [sem(f"b_bias{i}") for i in range(2)]
    consts, b_small = sem("b_consts"), sem("b_small")
    zeroed, pads = sem("b_zeroed"), sem("b_pads")
    met_v, met_p = sem("b_met_v"), sem("b_met_p")
    sc_mm, sc_v, ex_a, at_mm, pt_a, av_mm, o_v = (
        [sem(f"{n}{h}") for h in range(HEADS)] for n in ("sc_mm", "sc_v", "ex_a", "at_mm", "pt_a", "av_mm", "o_v"))
    qz_v = [sem(f"qz_v{i}") for i in range(2)]
    yb_p, x_in, x2_in = sem("yb_p"), sem("bx_in"), sem("x2_in")
    sqa_a, msa_v, pwa_p, ya_v, ta_mm, yaT_v = (sem(x) for x in ("sqa_a", "msa_v", "pwa_p", "ya_v", "ta_mm", "yaT_v"))
    pr_mm, x2_v = ([sem(f"{n}{i}") for i in range(2)] for n in ("pr_mm", "x2_v"))
    sq2_a, th_mm, hT_v, hT_a = (sem(x) for x in ("sq2_a", "th_mm", "bhT_v", "bhT_a"))
    xq_mm, sqq_a, msq_v, pwq_p, qxn_v, tq_mm, qxT_a = (
        sem(x) for x in ("xq_mm", "sqq_a", "msq_v", "pwq_p", "qxn_v", "tq_mm", "qxT_a"))
    sx_mm, mxx_v, exx_a, px_v, tx_mm, pxT_v, pxT_a, vx_mm, oxT_a = (
        sem(x) for x in ("sx_mm", "mxx_v", "exx_a", "px_v", "tx_mm", "pxT_v", "pxT_a", "vx_mm", "oxT_a"))
    xo_mm, x3_v = ([sem(f"{n}{i}") for i in range(2)] for n in ("xo_mm", "x3_v"))
    sq3_a, ms3_v, pw3_p, h3_a, tr_mm, rT_v, rT_a = (
        sem(x) for x in ("sq3_a", "ms3_v", "pw3_p", "h3_a", "tr_mm", "rT_v", "rT_a"))
    rt_mm, lg_v, top_v, eg_a, mask_v, rk_mm, slot_v, scat = (
        sem(x) for x in ("rt_mm", "lg_v", "top_v", "eg_a", "mask_v", "rk_mm", "slot_v", "scat"))
    x3_out, h3_out, w_gu = sem("x3_out"), sem("h3_out"), sem("b_w_gu")

    def after(eng, what, tile, times=1):
        if not tile.first:
            eng.wait_ge(what, tile.m * times)

    def run(eng, steps):
        def cycle(tiles):
            for name, i, lag in ORDER:
                if name in steps and tiles[lag]:
                    steps[name](i, tiles[lag])

        def at(c):
            return [Tile(t, t - 1 if t > 1 else None, t + 1, min(t + 1, BAND_TILES)) if 0 <= t < TILES else None
                    for t in range(c, c - LAGS - 1, -1)]

        for c in range(STEADY):
            cycle(at(c))
        with eng.Fori(STEADY, TILES) as c:
            v = [eng.snap(c + 1 - k) for k in range(LAGS + 3)]
            cycle([Tile(v[k + 1], v[k + 2], v[k], BAND_TILES) for k in range(LAGS + 1)])
        for c in range(TILES, TILES + LAGS):
            cycle(at(c))

    def rows(tile):
        return bass.ds(tile.t * P, P)

    with nc.Block() as block:

        @block.sync
        def _(sp):
            for i, at in enumerate((slice(near, WINDOW), slice(0, near))):
                src = bass.AP(tensor=d.band.tensor, offset=P - 1 + at.start,
                              ap=[[HEADS * (WINDOW + P), P], [WINDOW + P, HEADS], [1, at.stop - at.start]])
                sp.dma_start(bias[:, :, at], src).then_inc(bias_in[i], 16)
            sp.dma_start(xa[:], d.x[0:P, :]).then_inc(x_in, 16)
            sp.dma_start(w_out[:], d.w_out.rearrange("(k p) n -> p k n", p=P)).then_inc(w_in[0], 16)
            sp.dma_start(w_xq[:], d.w_xq.rearrange("(k p) n -> p k n", p=P)).then_inc(w_in[1], 16)
            sp.dma_start(w_xo[:], d.w_xo.rearrange("(k p) n -> p k n", p=P)).then_inc(w_in[2], 16)

            def prefetch():
                sp.wait_ge(sc_mm[HEADS - 1], TILES)
                expert_weights(sp, m, d, 0, 0).then_inc(w_gu, 16)
                sp.wait_ge(qz_v[1], TILES)
                expert_weights(sp, m, d, 1, 0).then_inc(w_gu, 16)
                sp.wait_ge(av_mm[HEADS - 1], TILES)
                expert_weights(sp, m, d, 2, 0).then_inc(w_gu, 16)
                sp.wait_ge(yb_p, TILES)
                expert_weights(sp, m, d, 3, 0).then_inc(w_gu, 16)

            def load_x(i, tile):
                if not tile.first:
                    sp.wait_ge(x2_in, tile.m * 16)
                    sp.wait_ge(th_mm, tile.m)
                    sp.wait_ge(sq2_a, tile.m)
                    sp.dma_start(xa[:], d.x[rows(tile), :]).then_inc(x_in, 16)

            def carry(i, tile):
                if isinstance(tile.t, int) and tile.t == TILES - 1:
                    prefetch()
                sp.wait_ge(x2_v[1], tile.n)
                if tile.first:
                    sp.wait_ge(pads, 16 * 2 * (PAD // P))
                else:
                    after(sp, x3_out, tile, 16)
                    after(sp, tr_mm, tile)
                    after(sp, h3_a, tile)
                sp.dma_start(xb[:], xa[:]).then_inc(x2_in, 16)

            def project_x(i, tile):
                if i == 1:
                    sp.wait_ge(x3_v[1], tile.n)
                    sp.dma_start(d.out[rows(tile), :], xb[:]).then_inc(x3_out, 16)

            def scale_r(i, tile):
                sp.wait_ge(h3_a, tile.n)
                sp.dma_start(d.h[rows(tile), :], sq).then_inc(h3_out, 16)

            run(sp, {"project_b": lambda i, tile: load_x(i, tile) if i == 0 else None, "project_x": project_x,
                     "scale_r": scale_r, "query": lambda i, tile: carry(i, tile) if i == 1 else None})
            sp.wait_ge(x3_out, 16 * TILES)
            sp.wait_ge(h3_out, 16 * TILES)
            sp.wait_ge(w_gu, 16 * GU_SLOTS)

        @block.gpsimd
        def _(pool):
            nc.gpsimd.memset(qz[:], 0.0).then_inc(zeroed, 1)
            nc.gpsimd.memset(half[:], -0.5).then_inc(consts, 1)
            nc.gpsimd.memset(m.seen[:], 0.0).then_inc(consts, 1)
            nc.gpsimd.iota(eids[:], [[1, E]], base=0, channel_multiplier=0, allow_small_or_imprecise_dtypes=True).then_inc(consts, 1)
            nc.gpsimd.iota(tok[:], [[0, TOPK]], base=0, channel_multiplier=1, allow_small_or_imprecise_dtypes=True).then_inc(consts, 1)
            pool.dma_start(w_r[:], d.w_router.rearrange("(k p) n -> p k n", p=P)).then_inc(b_small, 16)
            pool.dma_start(b_r[:], d.b_router.rearrange("(a n) -> a n", a=1).to_broadcast([P, E])).then_inc(b_small, 16)
            nc.gpsimd.memset(xb[:], 0.0).then_inc(zeroed, 1)
            pool.wait_ge(zeroed, 2)
            for b in range(PAD // P):
                at = slice(SEQ + b * P, SEQ + (b + 1) * P)
                pool.dma_start(d.out[at, :], xb[:]).then_inc(pads, 16)
                pool.dma_start(d.h[at, :], xb[:]).then_inc(pads, 16)

            def convolved(i, tile):
                if not tile.first:
                    after(pool, pr_mm[1], tile)
                    pool.sem_inc(met_p, 1)
                nc.gpsimd.tensor_copy(ybs[:], m.ybT[:, :, rows(tile)]).then_inc(yb_p, 1)

            def norm_a(i, tile):
                pool.wait_ge(msa_v, tile.n)
                nc.gpsimd.tensor_tensor(pw[:, 0:1], ssa, half[:, 0:1], ALU.pow).then_inc(pwa_p, 1)

            def mean_q(i, tile):
                pool.wait_ge(msq_v, tile.n)
                nc.gpsimd.tensor_tensor(pw[:, 4:8], ssq, half[:], ALU.pow).then_inc(pwq_p, 1)

            def turn_r(i, tile):
                pool.wait_ge(ms3_v, tile.n)
                nc.gpsimd.tensor_tensor(pw[:, 2:3], ssr, half[:, 0:1], ALU.pow).then_inc(pw3_p, 1)

            def rank(i, tile):
                pool.wait_ge(slot_v, tile.n)
                pool.sem_inc(met_p, 1)
                for k in range(TOPK):
                    pool.indirect_dma_start(d.slots[:], bass.IndirectOffsetOnAxis(ap=sloti[:, k:k + 1], axis=0),
                                            pay[:, k, :], None).then_inc(scat, 16)

            run(pool, {"convolved": convolved, "norm_a": norm_a, "mean_q": mean_q, "turn_r": turn_r, "rank": rank})
            pool.wait_ge(scat, 16 * TOPK * TILES)
            pool.wait_ge(pads, 16 * 2 * (PAD // P))

        @block.tensor
        def _(pe):
            def scores(h, tile):
                if h % 4 == 0:
                    pe.wait_ge(qz_v[h // 4], tile.n)
                if h:
                    pe.wait_ge(sc_v[h - 1], tile.n)
                else:
                    after(pe, sc_v[HEADS - 1], tile)
                for a, b in spans(0, tile.bands * P):
                    key = (tile.t - (tile.bands - 1)) * P + a
                    last = nc.tensor.matmul(ps[:, a:b], qz[:, h, :], m.kT[:, h // 2, bass.ds(key, b - a)],
                                            start=True, stop=True)
                last.then_inc(sc_mm[h], 1)

            def turn_p(h, tile):
                pe.wait_ge(ex_a[h], tile.n)
                if h:
                    pe.wait_ge(o_v[h - 1], tile.n)
                else:
                    after(pe, o_v[HEADS - 1], tile)
                for j in range(tile.bands):
                    last = nc.tensor.transpose(ptp[:, j * P:(j + 1) * P], p[h % 2][:, j * P:(j + 1) * P], m.ident[:])
                last.then_inc(at_mm[h], 1)

            def values(h, tile):
                pe.wait_ge(pt_a[h], tile.n)
                for j in range(tile.bands):
                    last = nc.tensor.matmul(po, pt[:, j * P:(j + 1) * P],
                                            m.v[:, tile.t - (tile.bands - 1) + j, (h // 2) * P:(h // 2 + 1) * P],
                                            start=(j == 0), stop=(j == tile.bands - 1))
                last.then_inc(av_mm[h], 1)

            def turn_a(i, tile):
                pe.wait_ge(ya_v, tile.n)
                for k in range(CS):
                    last = nc.tensor.transpose(ptp[:, k * P:(k + 1) * P], o[:, k * P:(k + 1) * P], m.ident[:])
                last.then_inc(ta_mm, 1)

            def project_b(c, tile):
                pe.wait_ge(yb_p, tile.n)
                pe.wait_ge(w_in[0], 16)
                after(pe, qxT_a if c else qxn_v, tile)
                for k in range(CS):
                    nc.tensor.matmul(X[:, c * 512:(c + 1) * 512], ybs[:, k, :], w_out[:, CS + k, c * 512:(c + 1) * 512],
                                     start=(k == 0), stop=False)

            def project_a(c, tile):
                pe.wait_ge(yaT_v, tile.n)
                for k in range(CS):
                    last = nc.tensor.matmul(X[:, c * 512:(c + 1) * 512], yaT[:, k, :], w_out[:, k, c * 512:(c + 1) * 512],
                                            start=False, stop=(k == CS - 1))
                last.then_inc(pr_mm[c], 1)

            def turn_h(i, tile):
                pe.wait_ge(x2_v[1], tile.n)
                for k in range(KD):
                    last = nc.tensor.transpose(X[:, k * P:(k + 1) * P], xa[:, k * P:(k + 1) * P], m.ident[:])
                last.then_inc(th_mm, 1)

            def query(i, tile):
                pe.wait_ge(hT_v, tile.n)
                pe.wait_ge(hT_a, tile.n)
                pe.wait_ge(w_in[1], 16)
                for k in range(i * KD // 2, (i + 1) * KD // 2):
                    last = nc.tensor.matmul(X[:, 0:D_X], hT[:, k, :], w_xq[:, k, :], start=(k == 0), stop=(k == KD - 1))
                if i:
                    last.then_inc(xq_mm, 1)

            def turn_q(i, tile):
                pe.wait_ge(qxn_v, tile.n)
                for h in range(XH):
                    last = nc.tensor.transpose(X[:, 512 + h * P:512 + (h + 1) * P], qxn[:, h * XD:(h + 1) * XD], m.ident[:])
                last.then_inc(tq_mm, 1)

            def scores_x(i, tile):
                pe.wait_ge(qxT_a, tile.n)
                after(pe, slot_v, tile)
                for h in range(XH):
                    last = nc.tensor.matmul(Y[:, h * MEM:(h + 1) * MEM], qxT[:, h, :], m.kxT[:, h, :],
                                            start=True, stop=True)
                last.then_inc(sx_mm, 1)

            def turn_x(i, tile):
                pe.wait_ge(px_v, tile.n)
                for j in range(XH * MT):
                    last = nc.tensor.transpose(Y[:, j * P:(j + 1) * P],
                                               px[:, j // MT, (j % MT) * P:(j % MT + 1) * P], m.ident[:])
                last.then_inc(tx_mm, 1)

            def values_x(i, tile):
                pe.wait_ge(pxT_v, tile.n)
                pe.wait_ge(pxT_a, tile.n)
                for h in range(XH):
                    for b in range(MT):
                        last = nc.tensor.matmul(Y[:, h * P:(h + 1) * P], m.vx[:, b, h * XD:(h + 1) * XD],
                                                pxT[:, h * MT + b, :], start=(b == 0), stop=(b == MT - 1))
                last.then_inc(vx_mm, 1)

            def project_x(c, tile):
                pe.wait_ge(oxT_a, tile.n)
                pe.wait_ge(w_in[2], 16)
                for k in range(XH):
                    last = nc.tensor.matmul(Y[:, c * 512:(c + 1) * 512], oxT[:, k, :],
                                            w_xo[:, k, c * 512:(c + 1) * 512], start=(k == 0), stop=(k == XH - 1))
                last.then_inc(xo_mm[c], 1)

            def turn_r(i, tile):
                pe.wait_ge(x3_v[0], tile.n)
                pe.wait_ge(x3_v[1], tile.n)
                for k in range(KD):
                    last = nc.tensor.transpose(Y[:, k * P:(k + 1) * P], xb[:, k * P:(k + 1) * P], m.ident[:])
                last.then_inc(tr_mm, 1)

            def route(i, tile):
                pe.wait_ge(rT_v, tile.n)
                pe.wait_ge(rT_a, tile.n)
                pe.wait_ge(b_small, 32)
                for k in range(KD):
                    last = nc.tensor.matmul(Y[:, 0:E], pxT[:, k, :], w_r[:, k, :], start=(k == 0), stop=(k == KD - 1))
                last.then_inc(rt_mm, 1)

            def rank(i, tile):
                pe.wait_ge(mask_v, tile.n)
                nc.tensor.matmul(Y[:, 512:512 + E], m.before[:], mask[:], start=True, stop=False)
                nc.tensor.matmul(Y[:, 512:512 + E], m.ones[:], m.seen[:], start=False, stop=True).then_inc(rk_mm, 1)

            pe.wait_ge(consts, 4)
            run(pe, {"scores": scores, "turn_p": turn_p, "values": values, "turn_a": turn_a, "project_a": project_a,
                     "project_b": project_b, "turn_h": turn_h, "query": query, "turn_q": turn_q, "scores_x": scores_x,
                     "turn_x": turn_x, "values_x": values_x, "project_x": project_x, "turn_r": turn_r,
                     "route": route, "rank": rank})

        @block.scalar
        def _(act):
            def scores(h, tile):
                act.wait_ge(sc_v[h], tile.n)
                pb = p[h % 2][:, 0:tile.bands * P]
                nc.scalar.activation(pb, pb, ACT.Exp, bias=nm[:, h:h + 1], accum_out=rs[:, h:h + 1]).then_inc(ex_a[h], 1)

            def turn_p(h, tile):
                act.wait_ge(at_mm[h], tile.n)
                if h:
                    act.wait_ge(av_mm[h - 1], tile.n)
                else:
                    after(act, av_mm[HEADS - 1], tile)
                nc.scalar.copy(pt[:, 0:tile.bands * P], ptp[:, 0:tile.bands * P]).then_inc(pt_a[h], 1)

            def norm_a(i, tile):
                act.wait_ge(o_v[HEADS - 1], tile.n)
                if tile.l is not None:
                    act.wait_ge(h3_out, tile.l * 16)
                nc.scalar.activation(sq[:, 0:D_ATT], o[:], ACT.Square, accum_out=ssa).then_inc(sqa_a, 1)

            def turn_h(i, tile):
                act.wait_ge(th_mm, tile.n)
                for k in range(KD // 2, KD):
                    last = nc.scalar.activation(hT[:, k, :], X[:, k * P:(k + 1) * P], ACT.Copy, scale=m.g_x[:, k:k + 1])
                last.then_inc(hT_a, 1)
                nc.scalar.activation(sq, xa[:], ACT.Square, accum_out=ssx).then_inc(sq2_a, 1)

            def query(i, tile):
                if i:
                    act.wait_ge(xq_mm, tile.n)
                    nc.scalar.activation(sqq, X[:, 0:D_X], ACT.Square).then_inc(sqq_a, 1)

            def turn_q(i, tile):
                act.wait_ge(tq_mm, tile.n)
                nc.scalar.activation(qxT[:], X[:, 512:1024].rearrange("p (h t) -> p h t", h=XH), ACT.Copy,
                                     scale=m.g_xq[:]).then_inc(qxT_a, 1)

            def scores_x(i, tile):
                act.wait_ge(mxx_v, tile.n)
                for h in range(XH):
                    last = nc.scalar.activation(px[:, h, :], Y[:, h * MEM:(h + 1) * MEM], ACT.Exp,
                                                bias=nmx[:, h:h + 1], accum_out=rsx[:, h:h + 1])
                last.then_inc(exx_a, 1)

            def turn_x(i, tile):
                act.wait_ge(tx_mm, tile.n)
                nc.scalar.copy(pxT[:, 4:8, :], Y[:, 512:1024].rearrange("p (j t) -> p j t", j=4)).then_inc(pxT_a, 1)

            def values_x(i, tile):
                act.wait_ge(vx_mm, tile.n)
                nc.scalar.copy(oxT[:], Y[:, 0:D_X].rearrange("p (h t) -> p h t", h=XH)).then_inc(oxT_a, 1)

            def turn_r(i, tile):
                act.wait_ge(tr_mm, tile.n)
                for k in range(KD // 2, KD):
                    last = nc.scalar.activation(pxT[:, k, :], Y[:, k * P:(k + 1) * P], ACT.Copy, scale=m.g_ffn[:, k:k + 1])
                last.then_inc(rT_a, 1)

            def square_r(i, tile):
                act.drain()
                act.wait_ge(x3_v[1], tile.n)
                after(act, h3_out, tile, 16)
                nc.scalar.activation(sq, xb[:], ACT.Square, accum_out=ssr).then_inc(sq3_a, 1)

            def scale_r(i, tile):
                act.wait_ge(pw3_p, tile.n)
                nc.scalar.activation(sq, xb[:], ACT.Copy, scale=pw[:, 2:3]).then_inc(h3_a, 1)

            def choose(i, tile):
                act.wait_ge(top_v, tile.n)
                nc.scalar.activation(gsum[:, 4:8], top[:, 0:TOPK], ACT.Exp, bias=gsum[:, 0:1],
                                     accum_out=gsum[:, 1:2]).then_inc(eg_a, 1)

            run(act, {"scores": scores, "turn_p": turn_p, "norm_a": norm_a, "turn_h": turn_h, "query": query,
                      "turn_q": turn_q, "scores_x": scores_x, "turn_x": turn_x, "values_x": values_x,
                      "turn_r": turn_r, "square_r": square_r, "scale_r": scale_r, "choose": choose})

        @block.vector
        def _(dve):
            def mean(ap, n):
                return nc.vector.tensor_scalar(ap, ap, 1.0 / n, EPS, ALU.mult, ALU.add)

            def stage(i, tile):
                after(dve, sc_mm[4 * i + 3], tile)
                for odd in range(2):
                    at = slice(odd * HEAD, (odd + 1) * HEAD)
                    last = nc.vector.tensor_copy(
                        qz[at, 4 * i:4 * i + 4].rearrange("p (j two) t -> p j two t", two=2)[:, :, odd, :],
                        m.qT[at, 2 * i:2 * i + 2, rows(tile)])
                last.then_inc(qz_v[i], 1)

            def scores(h, tile):
                dve.wait_ge(sc_mm[h], tile.n)
                if isinstance(tile.t, int) and tile.t == 2 and h == 0:
                    dve.wait_ge(bias_in[1], 16)
                    nc.vector.memset(bias[CHUNK:P, :, 0:CHUNK], NEG)
                    dve.drain()
                if h >= 2:
                    dve.wait_ge(at_mm[h - 2], tile.n)
                else:
                    after(dve, at_mm[HEADS - 2 + h], tile)
                dve.sem_inc(met_v, 1)
                nc.vector.tensor_tensor_reduce(p[h % 2][:, 0:tile.bands * P], ps[:, 0:tile.bands * P],
                                               bias[:, h, WINDOW - tile.bands * P:], 1.0, -3e38, ALU.add, ALU.max,
                                               nm[:, h:h + 1])
                dve.drain()
                nc.vector.tensor_scalar(nm[:, h:h + 1], nm[:, h:h + 1], -1.0, None, ALU.mult).then_inc(sc_v[h], 1)

            def values(h, tile):
                dve.wait_ge(ex_a[h], tile.n)
                nc.vector.reciprocal(rs[:, h:h + 1], rs[:, h:h + 1])
                dve.drain()
                dve.wait_ge(av_mm[h], tile.n)
                if h == 0:
                    after(dve, ta_mm, tile)
                nc.vector.tensor_scalar(o[:, h * HEAD:(h + 1) * HEAD], po[:, (h % 2) * HEAD:(h % 2 + 1) * HEAD],
                                        rs[:, h:h + 1], None, ALU.mult).then_inc(o_v[h], 1)

            def norm_a(i, tile):
                dve.wait_ge(sqa_a, tile.n)
                mean(ssa, D_ATT).then_inc(msa_v, 1)

            def scale_a(i, tile):
                dve.wait_ge(pwa_p, tile.n)
                nc.vector.tensor_scalar(o[:], o[:], pw[:, 0:1], None, ALU.mult).then_inc(ya_v, 1)

            def turn_a(i, tile):
                dve.wait_ge(ta_mm, tile.n)
                for k in range(CS):
                    last = nc.vector.tensor_scalar(yaT[:, k, :], ptp[:, k * P:(k + 1) * P], m.g_a[:, k:k + 1], None, ALU.mult)
                last.then_inc(yaT_v, 1)

            def project_a(c, tile):
                dve.wait_ge(pr_mm[c], tile.n)
                dve.wait_ge(x_in, tile.n * 16)
                at = slice(c * 512, (c + 1) * 512)
                nc.vector.tensor_tensor(xa[:, at], X[:, at], xa[:, at], ALU.add).then_inc(x2_v[c], 1)

            def turn_h(i, tile):
                dve.wait_ge(th_mm, tile.n)
                for k in range(KD // 2):
                    last = nc.vector.tensor_scalar(hT[:, k, :], X[:, k * P:(k + 1) * P], m.g_x[:, k:k + 1], None, ALU.mult)
                last.then_inc(hT_v, 1)

            def mean_q(i, tile):
                dve.wait_ge(sq2_a, tile.n)
                mean(ssx, D)
                dve.drain()
                nc.vector.tensor_scalar(ssx, ssx, EPS, None, ALU.mult)
                dve.wait_ge(sqq_a, tile.n)
                nc.vector.reduce_sum(ssq, sqq.rearrange("p (h e) -> p h e", h=XH), AX_X)
                dve.drain()
                nc.vector.tensor_scalar(ssq, ssq, 1.0 / XD, ssx, ALU.mult, ALU.add).then_inc(msq_v, 1)

            def norm_q(i, tile):
                dve.wait_ge(pwq_p, tile.n)
                nc.vector.tensor_tensor(qxn.rearrange("p (h e) -> p h e", h=XH),
                                        X[:, 0:D_X].rearrange("p (h e) -> p h e", h=XH),
                                        pw[:, 4:8].unsqueeze(2).to_broadcast([P, XH, XD]), ALU.mult).then_inc(qxn_v, 1)

            def scores_x(i, tile):
                dve.wait_ge(sx_mm, tile.n)
                nc.vector.reduce_max(nmx, Y[:].rearrange("p (h k) -> p h k", h=XH), AX_X)
                dve.drain()
                nc.vector.tensor_scalar(nmx, nmx, -1.0, None, ALU.mult).then_inc(mxx_v, 1)

            def weigh_x(i, tile):
                dve.wait_ge(exx_a, tile.n)
                nc.vector.reciprocal(rsx, rsx)
                dve.drain()
                for h in range(XH):
                    last = nc.vector.tensor_scalar(px[:, h, :], px[:, h, :], rsx[:, h:h + 1], None, ALU.mult)
                last.then_inc(px_v, 1)

            def turn_x(i, tile):
                dve.wait_ge(tx_mm, tile.n)
                nc.vector.tensor_copy(pxT[:, 0:4, :], Y[:, 0:512].rearrange("p (j t) -> p j t", j=4)).then_inc(pxT_v, 1)

            def project_x(c, tile):
                dve.wait_ge(xo_mm[c], tile.n)
                dve.wait_ge(x2_in, tile.n * 16)
                at = slice(c * 512, (c + 1) * 512)
                nc.vector.tensor_tensor(xb[:, at], Y[:, at], xb[:, at], ALU.add).then_inc(x3_v[c], 1)

            def turn_r(i, tile):
                dve.wait_ge(tr_mm, tile.n)
                for k in range(KD // 2):
                    last = nc.vector.tensor_scalar(pxT[:, k, :], Y[:, k * P:(k + 1) * P], m.g_ffn[:, k:k + 1], None, ALU.mult)
                last.then_inc(rT_v, 1)
                dve.wait_ge(sq3_a, tile.n)
                mean(ssr, D).then_inc(ms3_v, 1)

            def choose(i, tile):
                dve.wait_ge(rt_mm, tile.n)
                dve.wait_ge(b_small, 32)
                dve.wait_ge(pw3_p, tile.n)
                nc.vector.scalar_tensor_tensor(lg, Y[:, 0:E], pw[:, 2:3], b_r[:], ALU.mult, ALU.add)
                dve.drain()
                nc.vector.max(top[:], lg)
                dve.drain()
                nc.vector.tensor_scalar(gsum[:, 0:1], top[:, 0:1], -1.0, None, ALU.mult).then_inc(top_v, 1)
                nc.vector.max_index(topi[:], top[:], lg)
                dve.drain()
                nc.vector.tensor_copy(topf[:], topi[:, 0:TOPK])
                dve.drain()
                nc.vector.tensor_tensor(oneh[:], eids[:].unsqueeze(1).to_broadcast([P, TOPK, E]),
                                        topf[:].unsqueeze(2).to_broadcast([P, TOPK, E]), ALU.is_equal)
                dve.drain()
                nc.vector.reduce_sum(mask[:], oneh[:].rearrange("p k e -> p e k"), AX_X).then_inc(mask_v, 1)

            def rank(i, tile):
                after(dve, scat, tile, 16 * TOPK)
                nc.vector.tensor_copy(pay[:, :, 0], tok[:])
                dve.wait_ge(eg_a, tile.n)
                nc.vector.reciprocal(gsum[:, 2:3], gsum[:, 1:2])
                dve.drain()
                nc.vector.tensor_scalar(pay[:, :, 1].bitcast(F32), gsum[:, 4:8], gsum[:, 2:3], None, ALU.mult)
                dve.wait_ge(rk_mm, tile.n)
                nc.vector.tensor_tensor(ohp, oneh[:], Y[:, 512:512 + E].unsqueeze(1).to_broadcast([P, TOPK, E]), ALU.mult)
                nc.vector.tensor_tensor(m.seen[:], m.seen[:], mask[:], ALU.add)
                dve.drain()
                nc.vector.reduce_sum(slotf[:], ohp, AX_X)
                nc.vector.tensor_scalar(tok[:], tok[:], float(P), None, ALU.add)
                dve.drain()
                nc.vector.scalar_tensor_tensor(slotf[:], topf[:], float(SEQ), slotf[:], ALU.mult, ALU.add)
                dve.drain()
                nc.vector.tensor_copy(sloti[:], slotf[:]).then_inc(slot_v, 1)

            dve.wait_ge(bias_in[0], 16)
            nc.vector.memset(bias[0:CHUNK, :, WINDOW - CHUNK:], NEG)
            dve.drain()
            dve.wait_ge(zeroed, 2)
            dve.wait_ge(consts, 4)
            run(dve, {"stage": stage, "scores": scores, "values": values, "norm_a": norm_a, "scale_a": scale_a,
                      "turn_a": turn_a, "project_a": project_a, "turn_h": turn_h, "mean_q": mean_q, "norm_q": norm_q,
                      "scores_x": scores_x, "weigh_x": weigh_x, "turn_x": turn_x, "project_x": project_x,
                      "turn_r": turn_r, "choose": choose, "rank": rank})


WIDTHS = tuple(range(P, UNIT + 1, 8))
FEW = 8
FIELDS = 3


def phase_c(nc, m, d, sem, psum):
    w = m.w
    s = Map(nc, m.small_end)
    g = [s.put(f"g{i}", [P, UNIT]) for i in range(2)]
    sg = [s.put(f"sg{i}", [P, UNIT]) for i in range(2)]
    li = [s.put(f"li{i}", [P, UNIT]) for i in range(2)]
    idx = s.put("idx", [P, UB, 2], I32)
    cur = s.put("cur", [P, UB, 2], I32)
    cnt = s.put("cnt", [P, E])
    nun = s.put("nun", [P, E])
    cum = s.put("cum", [P, E])
    one = s.put("one", [P, E])
    le = s.put("le", [P, E])
    tmp = s.put("tmp", [P, E])
    ef = s.put("ef", [P, E])
    widths = s.put("widths", [P, len(WIDTHS) - 1])
    fit = s.put("fit", [P, len(WIDTHS) - 1])
    row = s.put("row", [P, 1])
    tcol = s.put("tcol", [P, 8])
    tint = s.put("tint", [P, FIELDS], I32)
    nint = s.put("nint", [1, 2], I32)
    assert s.at <= m.keep - 2 * SLOT_BYTES
    s = Map(nc, m.wide + (SLOTS - GU_SLOTS) * SLOT_BYTES)
    xg = s.put("xg", [P, UB, D])
    xT = s.put("xT", [P, KD, UNIT])
    aT = s.put("aT", [P, FS, UNIT])
    yT = s.put("yT", [P, KD, UNIT])
    y = s.put("y", [P, UB, D])
    bg = s.put("bg", [P, E * FS])
    bl = s.put("bl", [P, E * FS])
    bd = s.put("bd", [P, E * KD])
    rawg = s.put("rawg", [P, 2, 2 * P])
    rawd = s.put("rawd", [P, 2, P])
    tab = s.put("tab", [1, P * FIELDS], I32)
    assert s.at <= nc.sbuf_usable_end, s.at

    gup = psum("c_gu", [P, 4, 512])
    trp = psum("c_tr", [P, 2, 512])
    yp = psum("c_y", [P, 2, 512])

    raw_in, consts, cnt_mm, tab_v, tab_out, tab_in, nint_v = (
        sem(x) for x in ("raw_in", "c_consts", "cnt_mm", "tab_v", "tab_out", "tab_in", "nint_v"))
    braw_mm, bias_v, clear_v = sem("braw_mm"), sem("bias_v"), sem("clear_v")
    w_in = [sem(f"c_w{i}") for i in range(SLOTS)]
    idx_in, cur_p, xg_in = sem("idx_in"), sem("cur_p"), [sem(f"xg_in{b}") for b in range(UB)]
    x_tr, xT_c = [sem(f"x_tr{i}") for i in range(4)], [sem(f"xT_c{i}") for i in range(4)]
    gu_mm, g_v, sg_a, l_v, a_v = ([sem(f"{n}{j}") for j in range(FS)] for n in ("gu_mm", "g_v", "sg_a", "l_v", "a_v"))
    dn_mm, yT_a = ([sem(f"{n}{i}") for i in range(KD)] for n in ("dn_mm", "yT_a"))
    y_tr, y_v = ([sem(f"{n}{i}") for i in range(2 * UB)] for n in ("y_tr", "y_v"))
    scat, met_p = sem("c_scat"), sem("c_met_p")

    def load(eng, field, unit, most):
        return eng.value_load(tab[0:1, field * P:(field + 1) * P][:, bass.ds(unit, 1)], min_val=0, max_val=most)

    def n_units(eng):
        eng.wait_ge(tab_in, 16)
        eng.wait_ge(nint_v, 1)
        return eng.value_load(nint[0:1, 0:1], min_val=E, max_val=MAX_UNITS)

    def expert_of(eng, unit):
        return load(eng, 0, unit, E - 1)

    def width_of(eng, unit):
        return load(eng, 2, unit, len(WIDTHS) - 1)

    def by_width(eng, width, some, body):
        if len(some) == 1:
            return body(some[0][1])
        half = len(some) // 2
        with eng.If(width < some[half][0]):
            by_width(eng, width, some[:half], body)
        with eng.Else():
            by_width(eng, width, some[half:], body)

    with nc.Block() as block:

        @block.sync
        def _(sp):
            rows = d.b_gate_up.rearrange("e (j c) -> (e j) c", j=FS)
            sp.dma_start(rawg[:], rows.rearrange("(r p) c -> p r c", p=P)).then_inc(raw_in, 16)
            rows = d.b_down.rearrange("e (j c) -> (e j) c", j=KD)
            sp.dma_start(rawd[:], rows.rearrange("(r p) c -> p r c", p=P)).then_inc(raw_in, 16)

            for i in range(GU_SLOTS):
                sp.sem_inc(w_in[i], 16)
            for b in range(UB):
                sp.wait_ge(xg_in[b], 32)
            for i in range(GU_SLOTS, SLOTS):
                expert_weights(sp, m, d, i, 0).then_inc(w_in[i], 16)
            count = n_units(sp)
            with sp.Fori(1, count) as u:
                e = expert_of(sp, u)
                before = sp.snap(u)
                for i in range(SLOTS):
                    sp.wait_ge(gu_mm[2 * i + 1] if i < GU_SLOTS else dn_mm[4 * (i - GU_SLOTS) + 3], before)
                    expert_weights(sp, m, d, i, e).then_inc(w_in[i], 16)

        @block.gpsimd
        def _(pool):
            nc.gpsimd.iota(row[:], [[0, 1]], base=0, channel_multiplier=1, allow_small_or_imprecise_dtypes=True).then_inc(consts, 1)
            nc.gpsimd.iota(ef[:], [[1, E]], base=0, channel_multiplier=0, allow_small_or_imprecise_dtypes=True).then_inc(consts, 1)
            nc.gpsimd.iota(widths[:], [[WIDTHS[1] - WIDTHS[0], len(WIDTHS) - 1]], base=WIDTHS[0], channel_multiplier=0,
                           allow_small_or_imprecise_dtypes=True).then_inc(consts, 1)
            nc.gpsimd.memset(yT[:], 0.0).then_inc(consts, 1)
            nc.gpsimd.memset(one[:], 1.0).then_inc(consts, 1)

            def slots_of(first, u1):
                pool.dma_start(idx[:], d.slots[bass.ds(first, UNIT), :].rearrange("(b p) c -> p b c", p=P)).then_inc(idx_in, 16)
                pool.wait_ge(idx_in, 16 * u1)
                pool.sem_inc(met_p, 1)

            def gather(b, n=P):
                pool.indirect_dma_start(xg[0:n, b, :], None, d.h[:],
                                        bass.IndirectOffsetOnAxis(ap=idx[0:n, b, 0:1], axis=0)).then_inc(xg_in[b], 16)

            def scatter(b, n=P):
                pool.indirect_dma_start(d.out[:], bass.IndirectOffsetOnAxis(ap=cur[0:n, b, 0:1], axis=0), y[0:n, b, :],
                                        None, compute_op=ALU.add).then_inc(scat, 16)

            slots_of(0, 1)
            for b in range(UB):
                gather(b)
            count = n_units(pool)
            with pool.Fori(0, count) as u:
                u1, u2 = pool.snap(u + 1), pool.snap(u + 2)
                pool.wait_ge(x_tr[3], u1)
                pool.sem_inc(met_p, 1)
                nc.gpsimd.tensor_copy(cur[:], idx[:]).then_inc(cur_p, 1)
                pool.wait_ge(cur_p, u1)
                slots_of(load(pool, 1, u1, E * SEQ - UNIT), u2)
                gather(0)
                by_width(pool, width_of(pool, u1), list(enumerate(WIDTHS)), lambda n: gather(1, max(n - P, FEW)))
                pool.wait_ge(y_v[0], u2)
                pool.wait_ge(y_v[1], u1)
                pool.sem_inc(met_p, 1)
                scatter(0)
                pool.wait_ge(y_v[2], u2)
                pool.wait_ge(y_v[3], u1)
                by_width(pool, width_of(pool, u), list(enumerate(WIDTHS)), lambda n: scatter(1, max(n - P, FEW)))
                pool.wait_ge(scat, 16 * UB * u1)
            pool.wait_ge(xg_in[0], 16 * count + 16)
            pool.wait_ge(xg_in[1], 16 * count + 16)

        @block.tensor
        def _(pe):
            pe.wait_ge(raw_in, 32)
            pe.wait_ge(clear_v, 1)
            nc.tensor.matmul(yp[:, 0, 0:E], m.ones[:], m.seen[:], start=True, stop=True).then_inc(cnt_mm, 1)
            for r in range(2):
                nc.tensor.transpose(gup[:, 0, r * P:(r + 1) * P], rawg[:, r, 0:2 * P:2], m.ident[:])
                nc.tensor.transpose(gup[:, 1, r * P:(r + 1) * P], rawg[:, r, 1:2 * P:2], m.ident[:])
                last = nc.tensor.transpose(gup[:, 2, r * P:(r + 1) * P], rawd[:, r, :], m.ident[:])
            last.then_inc(braw_mm, 1)

            def turn_x(q, u1, n=4):
                for k in range(n):
                    last = nc.tensor.transpose(trp[:, q % 2, k * P:(k + 1) * P],
                                               xg[:, q // 2, ((q % 2) * 4 + k) * P:((q % 2) * 4 + k + 1) * P], m.ident[:])
                last.then_inc(x_tr[q], 1)

            def turn_y(q, n=4):
                for i in range(n):
                    last = nc.tensor.transpose(yp[:, q // 2, i * P:(i + 1) * P],
                                               yT[:, (q % 2) * 4 + i, (q // 2) * P:(q // 2 + 1) * P], m.ident[:])
                last.then_inc(y_tr[q], 1)

            def turn_last(u1):
                pe.wait_ge(yT_a[KD - 1], u1)
                for b in range(UB):
                    pe.wait_ge(y_v[2 * b], u1)
                    turn_y(2 * b + 1)

            def gate_up(n, u1, w1):
                pe.wait_ge(yT_a[4], u1)
                for j in range(FS):
                    i, c = j * 2 * P // SLOT_COLS, j * 2 * P % SLOT_COLS
                    if c == 0:
                        pe.wait_ge(w_in[i], w1)
                    if j >= 4:
                        pe.wait_ge(l_v[j - 4], u1)
                    for half in range(2):
                        for k in range(KD):
                            last = nc.tensor.matmul(gup[:, j % 4, half * UNIT:half * UNIT + n],
                                                    w[i][:, k, c + half:c + 2 * P:2], xT[:, k, 0:n],
                                                    start=(k == 0), stop=(k == KD - 1))
                    last.then_inc(gu_mm[j], 1)
                    if j == 0:
                        turn_last(u1)

            def down(n, u1, w1, slices):
                for i in slices:
                    s_, c = GU_SLOTS + i * P // SLOT_COLS, i * P % SLOT_COLS
                    if c == 0:
                        pe.wait_ge(w_in[s_], w1)
                    if i < 4:
                        pe.wait_ge(l_v[4 + i], u1)
                    else:
                        pe.wait_ge(yT_a[i - 4], u1)
                    for k in range(FS):
                        if i == 0 and k in (0, FS - 2, FS - 1):
                            pe.wait_ge(a_v[k or FS - 3], u1)
                        last = nc.tensor.matmul(gup[:, i % 4, 0:n], w[s_][:, k, c:c + P], aT[:, k, 0:n],
                                                start=(k == 0), stop=(k == FS - 1))
                    last.then_inc(dn_mm[i], 1)

            def unit(n, u1, w1, next_one):
                if n > P:
                    for q in (2, 3):
                        pe.wait_ge(xT_c[q], u1)
                gate_up(n, u1, w1)
                if n == P:
                    for q in (2, 3):
                        pe.wait_ge(xT_c[q], u1)
                pe.wait_ge(xg_in[0], next_one[1])
                turn_x(0, u1)
                turn_x(1, u1)
                down(n, u1, w1, range(6))
                pe.wait_ge(yT_a[3], u1)
                turn_y(0)
                pe.wait_ge(xg_in[1], next_one[1])
                pe.wait_ge(xT_c[0], next_one[0])
                pe.wait_ge(xT_c[1], next_one[0])
                pe.reg_mov(next_width, width_of(pe, u1))
                with pe.If(pe.snap(next_width) == 0):
                    turn_x(2, u1, 1)
                    turn_x(3, u1, 1)
                with pe.Else():
                    turn_x(2, u1)
                    turn_x(3, u1)
                down(n, u1, w1, range(6, 7))
                turn_y(2, 4 if n > P else 1)
                down(n, u1, w1, range(7, 8))

            for q in range(2 * UB):
                pe.wait_ge(xg_in[q // 2], 16)
                if q >= 2:
                    pe.wait_ge(xT_c[q - 2], 1)
                turn_x(q, 1)
            for q in (0, 1):
                pe.wait_ge(xT_c[q], 1)
            pe.wait_ge(consts, 5)
            pe.wait_ge(bias_v, 1)
            count = n_units(pe)
            next_width = pe.alloc_register("next_width")
            pe.reg_mov(next_width, width_of(pe, 0))
            with pe.Fori(0, count) as u:
                u1, u2 = pe.snap(u + 1), pe.snap(u + 2)
                w1, w2 = pe.snap(16 * u + 16), pe.snap(16 * u + 32)
                width = pe.snap(next_width)
                by_width(pe, width, list(enumerate(WIDTHS)), lambda n: unit(n, u1, w1, (u2, w2)))
            turn_last(count + 1)

        @block.scalar
        def _(act):
            def copy_x(q, u1):
                act.wait_ge(x_tr[q], u1)
                for k in range(4):
                    last = nc.scalar.activation(xT[:, 4 + k, (q // 2) * P:(q // 2 + 1) * P], trp[:, 1, k * P:(k + 1) * P],
                                                ACT.Copy, scale=m.g_ffn[:, 4 + k:5 + k])
                last.then_inc(xT_c[q], 1)

            act.wait_ge(tab_v, 1)
            with nc.allow_non_contiguous_dma(reason="a field's values side by side"):
                act.dma_start(d.units.rearrange("f u -> u f"), tint[:]).then_inc(tab_out, 16)
            act.wait_ge(tab_out, 16)
            act.dma_start(tab[:], d.units.rearrange("(a f) u -> a (f u)", a=1)).then_inc(tab_in, 16)
            copy_x(1, 1)
            copy_x(3, 1)
            for i in (4, KD - 1):
                act.sem_inc(yT_a[i], 1)
            count = n_units(act)
            with act.Fori(0, count) as u:
                u1 = act.snap(u + 1)
                e = expert_of(act, u)
                for j in range(FS):
                    act.wait_ge(g_v[j], u1)
                    nc.scalar.activation(sg[j % 2][:], g[j % 2][:], ACT.Sigmoid, scale=ALPHA).then_inc(sg_a[j], 1)
                u2 = act.snap(u + 2)
                copy_x(1, u2)
                for i in range(KD):
                    act.wait_ge(dn_mm[i], u1)
                    nc.scalar.activation(yT[:, i, :], gup[:, i % 4, 0:UNIT], ACT.Identity,
                                         bias=bd[:, bass.ds(e * KD + i, 1)]).then_inc(yT_a[i], 1)
                    if i == 5:
                        copy_x(3, u2)

        @block.vector
        def _(dve):
            nc.vector.memset(gup[:], 0.0)
            nc.vector.memset(yp[:], 0.0).then_inc(clear_v, 1)
            dve.wait_ge(cnt_mm, 1)
            dve.wait_ge(consts, 5)
            nc.vector.tensor_copy(cnt[:], yp[:, 0, 0:E])
            dve.drain()
            nc.vector.tensor_scalar(nun[:], cnt[:], float(UNIT), 1.0, ALU.is_gt, ALU.add)
            dve.drain()
            for r in range(2, SEQ // UNIT):
                nc.vector.scalar_tensor_tensor(nun[:], cnt[:], float(r * UNIT), nun[:], ALU.is_gt, ALU.add)
                dve.drain()
            nc.vector.tensor_tensor_scan(cum[:], one[:], nun[:], 0.0, ALU.mult, ALU.add)
            dve.drain()
            expert, before, many, first, width = (tcol[:, i:i + 1] for i in range(5))
            nc.vector.tensor_scalar(le[:], cum[:], row[:], None, ALU.is_le)
            dve.drain()
            nc.vector.reduce_sum(expert, le[:], AX_X)
            nc.vector.tensor_tensor(tmp[:], le[:], nun[:], ALU.mult)
            dve.drain()
            nc.vector.reduce_sum(before, tmp[:], AX_X)
            dve.drain()
            nc.vector.tensor_tensor(before, row[:], before, ALU.subtract)
            nc.vector.tensor_scalar(le[:], ef[:], expert, None, ALU.is_equal)
            dve.drain()
            nc.vector.tensor_tensor(tmp[:], le[:], cnt[:], ALU.mult)
            nc.vector.tensor_scalar(expert, expert, float(E - 1), None, ALU.min)
            nc.vector.tensor_scalar(before, before, float(UNIT), 0.0, ALU.mult, ALU.max)
            dve.drain()
            nc.vector.reduce_sum(many, tmp[:], AX_X)
            nc.vector.scalar_tensor_tensor(first, expert, float(SEQ), before, ALU.mult, ALU.add)
            dve.drain()
            nc.vector.tensor_tensor(many, many, before, ALU.subtract)
            nc.vector.tensor_scalar(first, first, float(E * SEQ - UNIT), None, ALU.min)
            dve.drain()
            nc.vector.tensor_scalar(many, many, 0.0, float(SEQ), ALU.max, ALU.min)
            dve.drain()
            nc.vector.tensor_scalar(fit[:], widths[:], many, None, ALU.is_lt)
            dve.drain()
            nc.vector.reduce_sum(width, fit[:], AX_X)
            dve.drain()
            for i, col in enumerate((expert, first, width)):
                nc.vector.tensor_copy(tint[:, i:i + 1], col)
            dve.drain()
            nc.vector.tensor_copy(nint[0:1, 0:1], cum[0:1, E - 1:E]).then_inc(nint_v, 1)
            dve.sem_inc(tab_v, 1)
            dve.wait_ge(braw_mm, 1)
            nc.vector.tensor_copy(bg[:], gup[:, 0, 0:2 * P])
            nc.vector.tensor_scalar(bl[:], gup[:, 1, 0:2 * P], 1.0, None, ALU.add)
            nc.vector.tensor_copy(bd[:], gup[:, 2, 0:2 * P]).then_inc(bias_v, 1)
            dve.drain()

            def copy_x(q, u1):
                dve.wait_ge(x_tr[q], u1)
                for k in range(4):
                    last = nc.vector.tensor_scalar(xT[:, k, (q // 2) * P:(q // 2 + 1) * P], trp[:, 0, k * P:(k + 1) * P],
                                                   m.g_ffn[:, k:k + 1], None, ALU.mult)
                last.then_inc(xT_c[q], 1)

            def weigh(q, u1):
                b, at = q // 2, (q % 2) * 512
                dve.wait_ge(y_tr[q], u1)
                nc.vector.tensor_scalar(y[:, b, at:at + 512], yp[:, b, :], cur[:, b, 1:2].bitcast(F32), None,
                                        ALU.mult).then_inc(y_v[q], 1)

            copy_x(0, 1)
            copy_x(2, 1)
            for b in range(UB):
                dve.sem_inc(y_v[2 * b], 1)
            count = n_units(dve)
            with dve.Fori(0, count) as u:
                u1 = dve.snap(u + 1)
                e = expert_of(dve, u)
                for j in range(FS):
                    dve.wait_ge(gu_mm[j], u1)
                    nc.vector.tensor_scalar(g[j % 2][:], gup[:, j % 4, 0:UNIT], bg[:, bass.ds(e * FS + j, 1)], LIMIT,
                                            ALU.add, ALU.min).then_inc(g_v[j], 1)
                    nc.vector.tensor_scalar(li[j % 2][:], gup[:, j % 4, UNIT:2 * UNIT], bl[:, bass.ds(e * FS + j, 1)],
                                            LIMIT + 1.0, ALU.add, ALU.min).then_inc(l_v[j], 1)
                    dve.drain()
                    nc.vector.scalar_tensor_tensor(li[j % 2][:], li[j % 2][:], 1.0 - LIMIT, g[j % 2][:], ALU.max, ALU.mult)
                    dve.drain()
                    dve.wait_ge(sg_a[j], u1)
                    nc.vector.tensor_tensor(aT[:, j, :], li[j % 2][:], sg[j % 2][:], ALU.mult).then_inc(a_v[j], 1)
                u2 = dve.snap(u + 2)
                copy_x(0, u2)
                dve.wait_ge(cur_p, u1)
                weigh(0, u1)
                copy_x(2, u2)
                weigh(2, u1)
                weigh(1, u2)
                weigh(3, u2)


def build(nc, d):
    m = lay_out(nc)
    for phase in (phase_a, phase_b, phase_c):
        sems, banks = [], []

        def sem(name):
            sems.append(nc.alloc_semaphore(name))
            return sems[-1]

        with ExitStack() as stack:
            phase(nc, m, d, sem, lambda name, shape: stack.enter_context(nc.psum_tensor(name, shape, F32)))
        nc.all_engine_barrier()
        nc.clear_and_free_semaphores(sems)
        nc.all_engine_barrier()


def kernel(**inputs):
    import concourse.bacc as bacc
    from concourse.bass_utils import run_bass_kernel_spmd

    nc = bacc.Bacc("TRN2", target_bir_lowering=False, num_devices=1)
    d, arrays = Buffers(), {}
    inputs["rel_rev"] = np.asarray(inputs.pop("rel_bias"))[:, :, ::-1]
    for name, value in inputs.items():
        a = np.ascontiguousarray(value)
        arrays["in_" + name] = a
        ap = nc.dram_tensor("in_" + name, a.shape, mybir.dt.from_np(a.dtype), kind="ExternalInput").ap()
        d.__dict__[name] = ap[0]
    d.out = nc.dram_tensor("out_0", (SEQ + PAD, D), F32, kind="ExternalOutput").ap()
    d.h = nc.dram_tensor("h_rows", (SEQ + PAD, D), F32).ap()
    d.slots = nc.dram_tensor("slots", (E * SEQ, 2), I32).ap()
    d.band = nc.dram_tensor("band", (P, HEADS * (WINDOW + P) + 1), F32).ap()
    d.units = nc.dram_tensor("units", (FIELDS, P), I32).ap()
    build(nc, d)
    r = run_bass_kernel_spmd(nc, [arrays], core_ids=[0])
    return r.results[0]["out_0"][:SEQ].reshape(1, SEQ, D)
```
